# Optimizing a Trainium2 kernel written in Bass

```python
import math
import jax, jax.numpy as jnp
from jax import lax
import numpy as np

D_MODEL = 1024
BATCH = 1
SEQ = 512
DEPTH = 2
DEC_BATCH = 8
DEC_SEQ = 8
PAST_LEN = 256
PAGE_SIZE = 128

N_EVEN = (DEPTH + 1) // 2
N_ODD = DEPTH // 2
D_MIX = D_MODEL
D_A = D_MIX // 2
CONV_W = 31
H_B = 4
DH_B = (D_MIX // 2) // H_B
D_B = H_B * DH_B
H_C = 4
DH_C = (D_MIX // 2) // (2 * H_C)
D_C = H_C * 2 * DH_C
H_D = 8
DH_D = (D_MIX // 2) // H_D
D_D = H_D * DH_D
D_FF = 2816
PLE_DIM = 256
N_BUCKETS = 32
MAX_DIST = 128
Q_BLOCK = 128
MLSTM_CHUNK = 128
IN_EVEN = 2 * D_A + 4 * D_B + 2 * H_B
IN_ODD = 3 * D_C + 3 * D_D
SPLIT_EVEN = (D_A, 2 * D_A, 2 * D_A + D_B, 2 * D_A + 2 * D_B, 2 * D_A + 3 * D_B, 2 * D_A + 4 * D_B)
SPLIT_ODD = (D_C, 2 * D_C, 3 * D_C, 3 * D_C + D_D, 3 * D_C + 2 * D_D)
NEG_INF = -1e30

kernel_name = 'hybrid_conv_mlstm_diffattn_stickbreak_step'

def rms_norm(x, g, eps=1e-6):
    xf = x.astype(jnp.float32)
    y = xf * lax.rsqrt(jnp.mean(xf * xf, axis=-1, keepdims=True) + eps)
    return (y * g.astype(jnp.float32)).astype(x.dtype)

def swiglu(x, wi, wo):
    g, u = jnp.split(x @ wi, 2, axis=-1)
    return (jax.nn.silu(g) * u) @ wo

def t5_bucket(dist):
    n = jnp.maximum(dist, 0)
    exact = N_BUCKETS // 2
    nf = jnp.maximum(n, 1).astype(jnp.float32)
    large = exact + (jnp.log(nf / exact) / math.log(MAX_DIST / exact) * (N_BUCKETS - exact)).astype(jnp.int32)
    return jnp.where(n < exact, n, jnp.minimum(large, N_BUCKETS - 1))

def mlstm_scan(q, k, v, li, lf, C0, n0, m0):
    B, T, H, _ = q.shape
    L = MLSTM_CHUNK if T % MLSTM_CHUNK == 0 else T
    nc = T // L

    def chunks(a):
        return a.reshape(B, nc, L, H, a.shape[-1]).transpose(1, 0, 3, 2, 4)

    def gchunks(a):
        return a.reshape(B, nc, L, H).transpose(1, 0, 3, 2)

    causal = jnp.tril(jnp.ones((L, L), dtype=bool))

    def step(carry, inp):
        C, n, m = carry
        qc, kc, vc, lic, lfc = inp
        b = jnp.cumsum(lfc, axis=-1)
        dmat = jnp.where(causal, b[..., :, None] - b[..., None, :] + lic[..., None, :], -jnp.inf)
        inter = b + m[..., None]
        mt = jnp.maximum(inter, jnp.max(dmat, axis=-1))
        w_inter = jnp.exp(inter - mt)
        s = jnp.einsum('bhtd,bhsd->bhts', qc, kc) * jnp.exp(dmat - mt[..., None])
        num = w_inter[..., None] * jnp.einsum('bhtd,bhde->bhte', qc, C) + jnp.einsum('bhts,bhse->bhte', s, vc)
        den = w_inter * jnp.einsum('bhtd,bhd->bht', qc, n) + jnp.sum(s, axis=-1)
        h = num / jnp.maximum(jnp.abs(den), jnp.exp(-mt))[..., None]
        m_new = mt[..., -1]
        decay = jnp.exp(b[..., -1] + m - m_new)
        w_s = jnp.exp(b[..., -1:] - b + lic - m_new[..., None])
        C_new = decay[..., None, None] * C + jnp.einsum('bhs,bhsd,bhse->bhde', w_s, kc, vc)
        n_new = decay[..., None] * n + jnp.einsum('bhs,bhsd->bhd', w_s, kc)
        return (C_new, n_new, m_new), h

    carry0 = (C0.astype(jnp.float32), n0.astype(jnp.float32), m0.astype(jnp.float32))
    (C1, n1, m1), hs = lax.scan(step, carry0, (chunks(q), chunks(k), chunks(v), gchunks(li), gchunks(lf)))
    h = hs.transpose(1, 0, 3, 2, 4).reshape(B, T, H, v.shape[-1])
    return h, C1, n1, m1

def diff_attention(q, k, v, q_pos, k_pos, rel_bias, lam):
    dist = q_pos[:, None] - k_pos[None, :]
    bias = jnp.moveaxis(rel_bias.astype(jnp.float32)[t5_bucket(dist)], -1, 0)
    mask = dist >= 0
    scale = DH_C ** -0.5

    def probs(qh, kh):
        s = jnp.einsum('bhtd,bhsd->bhts', qh, kh) * scale + bias
        return jax.nn.softmax(jnp.where(mask, s, NEG_INF), axis=-1)

    a = probs(q[..., :DH_C], k[..., :DH_C]) - lam * probs(q[..., DH_C:], k[..., DH_C:])
    return jnp.einsum('bhts,bhse->bhte', a, v)

def stick_breaking(q, k, v, q_pos, k_pos):
    dist = q_pos[:, None] - k_pos[None, :]
    mask = dist > 0
    z = jnp.einsum('bhtd,bhsd->bhts', q, k) * (q.shape[-1] ** -0.5)
    log_keep = jnp.where(mask, jax.nn.log_sigmoid(-z), 0.0)
    after = lax.cumsum(log_keep, axis=3, reverse=True) - log_keep
    weights = jnp.where(mask, jnp.exp(jax.nn.log_sigmoid(z) + after), 0.0)
    return jnp.einsum('bhts,bhse->bhte', weights, v)

def sweep_query_blocks(fn, q):
    B, H, T, _ = q.shape

    def body(i):
        start = i * Q_BLOCK
        qb = lax.dynamic_slice_in_dim(q, start, Q_BLOCK, axis=2)
        return fn(qb, start + jnp.arange(Q_BLOCK, dtype=jnp.int32))

    out = lax.map(body, jnp.arange(T // Q_BLOCK, dtype=jnp.int32))
    return jnp.moveaxis(out, 0, 2).reshape(B, H, T, out.shape[-1])

def gather_pages(pool, page_table):
    rows = pool[page_table]
    return rows.reshape(page_table.shape[0], -1, pool.shape[-2], pool.shape[-1])

def even_mixer(hn, state, W, j):
    f32 = jnp.float32
    conv_buf, C0, n0, m0 = state
    B, T, _ = hn.shape
    a_val, a_gate, q, k, v, o, gates = jnp.split(hn @ W['ev_w_in'][j], SPLIT_EVEN, axis=-1)
    u = a_val * jax.nn.sigmoid(a_gate)
    full = jnp.concatenate([conv_buf.astype(u.dtype), u], axis=1)
    taps = W['ev_conv_w'][j].astype(u.dtype)[:, None, :]
    c = lax.conv_general_dilated(full, taps, window_strides=(1,), padding='VALID',
                                 dimension_numbers=('NWC', 'WIO', 'NWC'), feature_group_count=D_A)
    c = c.astype(f32) + W['ev_conv_b'][j].astype(f32)
    mu = jnp.mean(c, axis=-1, keepdims=True)
    var = jnp.mean(jnp.square(c - mu), axis=-1, keepdims=True)
    cn = (c - mu) * lax.rsqrt(var + 1e-5) * W['ev_ln_g'][j].astype(f32) + W['ev_ln_b'][j].astype(f32)
    a_out = jax.nn.silu(cn)
    qh = q.reshape(B, T, H_B, DH_B).astype(f32)
    kh = k.reshape(B, T, H_B, DH_B).astype(f32) * (DH_B ** -0.5)
    vh = v.reshape(B, T, H_B, DH_B).astype(f32)
    g = gates.astype(f32) + W['ev_gate_b'][j].astype(f32)
    li = g[..., :H_B]
    lf = jax.nn.log_sigmoid(g[..., H_B:])
    h, C1, n1, m1 = mlstm_scan(qh, kh, vh, li, lf, C0, n0, m0)
    b_out = jax.nn.sigmoid(o.astype(f32)) * h.reshape(B, T, D_B)
    mix = jnp.concatenate([a_out, b_out], axis=-1).astype(hn.dtype) @ W['ev_w_out'][j]
    return mix, (full[:, -(CONV_W - 1):], C1, n1, m1)

def odd_mixer(hn, past, W, j, layer):
    f32 = jnp.float32
    B, T, _ = hn.shape
    cq, ck, cv, sq, sk, sv = jnp.split(hn @ W['od_w_in'][j], SPLIT_ODD, axis=-1)
    cq = cq.reshape(B, T, H_C, 2 * DH_C)
    ck = ck.reshape(B, T, H_C, 2 * DH_C)
    cv = cv.reshape(B, T, H_C, 2 * DH_C)
    sq = sq.reshape(B, T, H_D, DH_D)
    sk = sk.reshape(B, T, H_D, DH_D)
    sv = sv.reshape(B, T, H_D, DH_D)
    new_rows = (ck, cv, sk, sv)
    if past is None:
        keys = new_rows
        q_start = 0
    else:
        keys = tuple(jnp.concatenate([pk.astype(r.dtype), r], axis=1) for pk, r in zip(past, new_rows))
        q_start = past[0].shape[1]
    bhtd = lambda a: jnp.swapaxes(a, 1, 2).astype(f32)
    kc, vc, ks, vs = (bhtd(a) for a in keys)
    k_pos = jnp.arange(kc.shape[2], dtype=jnp.int32)
    lam_init = 0.8 - 0.6 * math.exp(-0.3 * layer)
    lp = W['od_lambda'][j].astype(f32)
    lam = jnp.exp(jnp.sum(lp[0] * lp[1])) - jnp.exp(jnp.sum(lp[2] * lp[3])) + lam_init
    rel_bias = W['rel_bias']
    diff_fn = lambda qb, q_pos: diff_attention(qb, kc, vc, q_pos, k_pos, rel_bias, lam)
    sb_fn = lambda qb, q_pos: stick_breaking(qb, ks, vs, q_pos, k_pos)
    qc_, qs_ = bhtd(cq), bhtd(sq)
    if past is None:
        oc = sweep_query_blocks(diff_fn, qc_)
        os_ = sweep_query_blocks(sb_fn, qs_)
    else:
        q_pos = q_start + jnp.arange(T, dtype=jnp.int32)
        oc = diff_fn(qc_, q_pos)
        os_ = sb_fn(qs_, q_pos)
    hg = W['od_head_g'][j].astype(f32).reshape(H_C, 1, 2 * DH_C)
    oc = oc * lax.rsqrt(jnp.mean(oc * oc, axis=-1, keepdims=True) + 1e-6) * hg * (1.0 - lam_init)
    oc = jnp.swapaxes(oc, 1, 2).reshape(B, T, D_C)
    os_ = jnp.swapaxes(os_, 1, 2).reshape(B, T, D_D)
    mix = jnp.concatenate([oc, os_], axis=-1).astype(hn.dtype) @ W['od_w_out'][j]
    return mix, new_rows

def trunk(x, p, even_states, odd_past, W):
    h = x
    new_even, new_odd = [], []
    for l in range(DEPTH):
        h = h + 0.5 * swiglu(rms_norm(h, W['ffn_norm1'][l]), W['ffn1_wi'][l], W['ffn1_wo'][l])
        hn = rms_norm(h, W['mix_norm'][l])
        if l % 2 == 0:
            mix, st = even_mixer(hn, even_states[l // 2], W, l // 2)
            new_even.append(st)
        else:
            mix, st = odd_mixer(hn, odd_past[l // 2], W, l // 2, l)
            new_odd.append(st)
        h = h + mix
        h = h + 0.5 * swiglu(rms_norm(h, W['ffn_norm2'][l]), W['ffn2_wi'][l], W['ffn2_wo'][l])
        gate = jax.nn.sigmoid(rms_norm(h, W['ple_norm'][l]) @ W['ple_wg'][l])
        h = h + gate * (p[l] @ W['ple_wp'][l])
    return rms_norm(h, W['final_norm']), new_even, new_odd

def setup_inputs(seed: int = 0) -> dict:
    key = jax.random.key(seed)
    ks = iter(jax.random.split(key, 48))
    nrm = lambda shape, scale=1.0: jax.random.normal(next(ks), shape, jnp.float32) * scale
    gain = lambda shape: 1.0 + 0.02 * jax.random.normal(next(ks), shape, jnp.float32)
    n_pages = PAST_LEN // PAGE_SIZE
    n_used = DEC_BATCH * n_pages
    n_pool = n_used + n_used // 4
    page_table = jax.random.permutation(next(ks), n_pool)[:n_used].reshape(DEC_BATCH, n_pages).astype(jnp.int32)
    return {
        'x_prompt': nrm((BATCH, SEQ, D_MODEL)),
        'x_sample': nrm((DEC_BATCH, DEC_SEQ, D_MODEL)),
        'p_prompt': nrm((DEPTH, BATCH, SEQ, PLE_DIM)),
        'p_sample': nrm((DEPTH, DEC_BATCH, DEC_SEQ, PLE_DIM)),
        'state_conv': nrm((N_EVEN, DEC_BATCH, CONV_W - 1, D_A), 0.5),
        'state_mlstm_C': nrm((N_EVEN, DEC_BATCH, H_B, DH_B, DH_B), 0.1),
        'state_mlstm_n': nrm((N_EVEN, DEC_BATCH, H_B, DH_B), 0.1),
        'state_mlstm_m': nrm((N_EVEN, DEC_BATCH, H_B), 0.5),
        'cache_diff_k': nrm((N_ODD, n_pool, PAGE_SIZE, H_C, 2 * DH_C)),
        'cache_diff_v': nrm((N_ODD, n_pool, PAGE_SIZE, H_C, 2 * DH_C)),
        'cache_sb_k': nrm((N_ODD, n_pool, PAGE_SIZE, H_D, DH_D)),
        'cache_sb_v': nrm((N_ODD, n_pool, PAGE_SIZE, H_D, DH_D)),
        'page_table': page_table,
        'ffn_norm1': gain((DEPTH, D_MODEL)),
        'ffn1_wi': nrm((DEPTH, D_MODEL, 2 * D_FF), D_MODEL ** -0.5),
        'ffn1_wo': nrm((DEPTH, D_FF, D_MODEL), D_FF ** -0.5),
        'mix_norm': gain((DEPTH, D_MODEL)),
        'ffn_norm2': gain((DEPTH, D_MODEL)),
        'ffn2_wi': nrm((DEPTH, D_MODEL, 2 * D_FF), D_MODEL ** -0.5),
        'ffn2_wo': nrm((DEPTH, D_FF, D_MODEL), D_FF ** -0.5),
        'ple_norm': gain((DEPTH, D_MODEL)),
        'ple_wg': nrm((DEPTH, D_MODEL, D_MODEL), D_MODEL ** -0.5),
        'ple_wp': nrm((DEPTH, PLE_DIM, D_MODEL), PLE_DIM ** -0.5),
        'ev_w_in': nrm((N_EVEN, D_MODEL, IN_EVEN), D_MODEL ** -0.5),
        'ev_conv_w': nrm((N_EVEN, CONV_W, D_A), CONV_W ** -0.5),
        'ev_conv_b': nrm((N_EVEN, D_A), 0.02),
        'ev_ln_g': gain((N_EVEN, D_A)),
        'ev_ln_b': nrm((N_EVEN, D_A), 0.02),
        'ev_gate_b': jnp.concatenate([nrm((N_EVEN, H_B), 0.1), 3.0 + nrm((N_EVEN, H_B), 0.1)], axis=-1),
        'ev_w_out': nrm((N_EVEN, D_A + D_B, D_MODEL), (D_A + D_B) ** -0.5),
        'od_w_in': nrm((N_ODD, D_MODEL, IN_ODD), D_MODEL ** -0.5),
        'od_lambda': nrm((N_ODD, 4, DH_C), 0.1),
        'od_head_g': gain((N_ODD, D_C)),
        'od_w_out': nrm((N_ODD, D_C + D_D, D_MODEL), (D_C + D_D) ** -0.5),
        'rel_bias': nrm((N_BUCKETS, H_C), 0.3),
        'final_norm': gain((D_MODEL,)),
    }

def reference(x_prompt, x_sample, p_prompt, p_sample, state_conv, state_mlstm_C, state_mlstm_n, state_mlstm_m,
              cache_diff_k, cache_diff_v, cache_sb_k, cache_sb_v, page_table,
              ffn_norm1, ffn1_wi, ffn1_wo, mix_norm, ffn_norm2, ffn2_wi, ffn2_wo, ple_norm, ple_wg, ple_wp,
              ev_w_in, ev_conv_w, ev_conv_b, ev_ln_g, ev_ln_b, ev_gate_b, ev_w_out,
              od_w_in, od_lambda, od_head_g, od_w_out, rel_bias, final_norm):
    W = dict(ffn_norm1=ffn_norm1, ffn1_wi=ffn1_wi, ffn1_wo=ffn1_wo, mix_norm=mix_norm,
             ffn_norm2=ffn_norm2, ffn2_wi=ffn2_wi, ffn2_wo=ffn2_wo,
             ple_norm=ple_norm, ple_wg=ple_wg, ple_wp=ple_wp,
             ev_w_in=ev_w_in, ev_conv_w=ev_conv_w, ev_conv_b=ev_conv_b, ev_ln_g=ev_ln_g, ev_ln_b=ev_ln_b,
             ev_gate_b=ev_gate_b, ev_w_out=ev_w_out,
             od_w_in=od_w_in, od_lambda=od_lambda, od_head_g=od_head_g, od_w_out=od_w_out,
             rel_bias=rel_bias, final_norm=final_norm)
    bp = x_prompt.shape[0]
    even_p = [(jnp.zeros((bp, CONV_W - 1, D_A), x_prompt.dtype),
               jnp.zeros((bp, H_B, DH_B, DH_B), jnp.float32),
               jnp.zeros((bp, H_B, DH_B), jnp.float32),
               jnp.zeros((bp, H_B), jnp.float32)) for _ in range(N_EVEN)]
    y_prompt, ev_p, od_p = trunk(x_prompt, p_prompt, even_p, [None] * N_ODD, W)
    even_s = [(state_conv[j], state_mlstm_C[j], state_mlstm_n[j], state_mlstm_m[j]) for j in range(N_EVEN)]
    odd_s = [tuple(gather_pages(c[j], page_table) for c in (cache_diff_k, cache_diff_v, cache_sb_k, cache_sb_v))
             for j in range(N_ODD)]
    y_sample, ev_s, od_s = trunk(x_sample, p_sample, even_s, odd_s, W)
    stack = lambda states, i: jnp.stack([s[i] for s in states])
    return (y_prompt, y_sample,
            stack(ev_p, 0), stack(ev_s, 0), stack(ev_p, 1), stack(ev_s, 1),
            stack(ev_p, 2), stack(ev_s, 2), stack(ev_p, 3), stack(ev_s, 3),
            stack(od_p, 0), stack(od_s, 0), stack(od_p, 1), stack(od_s, 1),
            stack(od_p, 2), stack(od_s, 2), stack(od_p, 3), stack(od_s, 3))


_drawn_inputs = setup_inputs


def setup_inputs(seed=0):
    import zlib

    import numpy as np

    out = dict(_drawn_inputs(seed))
    spreads = {}
    factors = {'ffn_norm2': 7.183,
     'ple_norm': 64.0,
     'ev_conv_b': 2.887,
     'ev_ln_g': 6.61,
     'ev_ln_b': 6.582,
     'od_head_g': 64.0,
     'final_norm': 7.163,
     'cache_sb_k': 8.0,
     'cache_sb_v': 4.562}
    for name, (base, spread) in spreads.items():
        noise = np.random.default_rng([zlib.crc32(name.encode()), seed]).standard_normal(out[name].shape)
        drawn = base * np.exp(spread * noise) if base else spread * noise
        out[name] = __import__('jax').numpy.asarray(drawn.astype(out[name].dtype))
    for name, factor in factors.items():
        out[name] = (out[name] * factor).astype(out[name].dtype)
    return out
```

```python
from contextlib import ExitStack

import numpy as np
import concourse.bass as bass
from concourse import mybir

F32 = mybir.dt.float32
F32R = mybir.dt.float32r
I32 = mybir.dt.int32
ALU = mybir.AluOpType
ACT = mybir.ActivationFunctionType
AX = mybir.AxisListType

P = 128
D = 1024
SEQ = 512
NB, TB = 8, 8
SMP = NB * TB
T = SEQ + SMP
HALF = T // 2
KD = D // P
DFF = 2816
CHUNKS = (12, 10)
assert sum(CHUNKS) * P == DFF
HIST = 30
TAPS = 31
HEADS = 4
DA = 512
TM = DA // P
PAST, PAGE = 256, 128
NPG = PAST // PAGE
PLE = 256
KP = PLE // P
KEYS = PAST + SMP
PAIRS = NB // 2
GL = 640
NEG = -1e30
LAM_INIT = 0.8 - 0.6 * float(np.exp(-0.3))
ST = T // P + 1
BLK = 2048

CONST = dict(ident=128, cm=128, neg_incl=128, sb_mul=128, sb_neg=128, blk_ml=64, blk_col=8,
             dneg=4 * 64, smul=4 * 64, sneg=4 * 64, fold=64, half0=1, half1=1,
             sel=4 * 128)
COFF = {}
_o = 0
for _n, _w in CONST.items():
    COFF[_n] = _o
    _o += _w
CW = _o
PARAM = dict(gains=9 * KD, conv_w=TM * TAPS, conv_b=TM, ln_g=TM, ln_b=TM, gate_b=2, head_g=TM,
             lam=256, m0=8)
POFF = {}
_o = 0
for _n, _w in PARAM.items():
    POFF[_n] = _o
    _o += _w
PW = _o


class Phase:
    blocks = tiles = 0

    def __init__(self, src, at, nb, ks):
        self.src, self.at, self.nb, self.ks = src, at, nb, ks
        self.width = sum(ks) * P
        self.n0, self.t0, self.T = Phase.blocks, Phase.tiles, len(ks)
        Phase.blocks += nb
        Phase.tiles += nb * len(ks)
        assert nb % 2 == 0 and (nb * len(ks)) % 2 == 0 and self.width <= BLK


def schedule():
    Phase.blocks = Phase.tiles = 0
    ph = {}
    order = []

    def add(name, *a):
        ph[name] = Phase(*a)
        order.append(name)

    def ffn(n):
        at = 0
        for c, k in enumerate(CHUNKS):
            add(("up", n, c), "up", n * sum(CHUNKS) + at, k, (KD, KD))
            at += k
            add(("down", n, c), f"down{c}", n * KD, KD, (k,))

    for l in range(2):
        ffn(2 * l)
        if l == 0:
            add("glu", "mixin", 0, 4, (KD, KD))
            add("kv", "mixin", 4, 4, (KD, KD))
            add("qo", "mixin", 8, 4, (KD, KD))
        else:
            add("qk0", "mixin", 12, 4, (KD, KD))
            add("v0", "mixin", 16, 2, (KD, KD))
            add("qk1", "mixin", 18, 4, (KD, KD))
            add("v1", "mixin", 22, 2, (KD, KD))
        add(("out", l), "mixout", l * 4, 4, (KD, KD))
        ffn(2 * l + 1)
        add(("ple", l), "ple", l * KD, KD, (KD, KP))
    return ph, order


def build(nc, A):
    ph, order = schedule()
    ctx = ExitStack()
    sems = {}

    def S(name):
        if name not in sems:
            sems[name] = ctx.enter_context(nc.semaphore(name))
        return sems[name]

    top = [(nc.sbuf_base + 31) // 32 * 32]
    END = nc.sbuf_base + nc.sbuf_bytes_remaining

    def sb(name, shape, dt=F32, at=None):
        size = (int(np.prod(shape[1:])) * 4 + 31) // 32 * 32
        if at is None:
            a = top[0]
            top[0] += size
        else:
            a = at[0]
            at[0] += size
        assert a + size <= END, (name, a + size - END)
        return nc.alloc_sbuf_tensor_at(name, shape, dt, offset=a)

    h = sb("h", [P, KD, T])
    xr = sb("xr", [P, KD, T], F32R)
    xl = sb("xl", [P, KD, T], F32R)
    raw = [sb(f"raw{s}", [P, BLK]) for s in range(2)]
    wr = [sb(f"wr{s}", [P, BLK], F32R) for s in range(2)]
    wl = [sb(f"wl{s}", [P, BLK], F32R) for s in range(2)]
    R = sb("R", [P, T])
    tg, sg, tu, hd, sq, acc = (sb(n, [P, T]) for n in ("tg", "sg", "tu", "hd", "sq", "acc"))
    cst = sb("cst", [P, CW])
    prm = sb("prm", [P, PW])
    ones = sb("ones", [P, P])
    eps6 = sb("eps6", [P, 1])
    eps5 = sb("eps5", [P, 1])
    pages = sb("pages", [1, NB * NPG], I32)
    tiny = sb("tiny", [P, 64])
    ZONE = top[0]
    vtmp = [hd, sq, tg, sg]

    z = [ZONE]
    hr = sb("hr", [P, max(CHUNKS), T], F32R, at=z)
    hl = sb("hl", [P, max(CHUNKS), T], F32R, at=z)
    brel = sb("brel", [32, HEADS * P], at=z)
    bone = sb("bone", [32, GL], at=z)
    grep = sb("grep", [P, GL], at=z)
    z = [ZONE]
    praw = sb("praw", [P, KP, T], at=z)
    pr = sb("pr", [P, KP, T], F32R, at=z)
    pl = sb("pl", [P, KP, T], F32R, at=z)
    z = [ZONE]
    up = sb("up", [P, TM, HIST + SEQ], at=z)
    us = sb("us", [P, TM, NB, HIST + TB], at=z)
    z2 = [ZONE]
    C0 = sb("C0", [P, NB, P + 1], at=z2)
    Cn = sb("Cn", [P, NB, P + 1], at=z2)
    Cp = sb("Cp", [P, P + 1], at=z2)
    kw = sb("kw", [P, TM, P], at=z2)
    assert z2[0] <= z[0]
    cv = sb("cv", [P, TM, T], at=z)
    z3 = [z[0] - TM * T * 4]
    Xs = sb("Xs", [P, 2, SEQ], at=z3)
    Ds = sb("Ds", [P, 2, SEQ], at=z3)
    assert z3[0] <= z[0]
    qT = sb("qT", [P, HEADS, T], at=z)
    kT = sb("kT", [P, HEADS, T], at=z)
    oT = sb("oT", [P, HEADS, T], at=z)
    kn = sb("kn", [P, ST, HEADS, P], at=z)
    vn = sb("vn", [P, ST, HEADS, P + 1], at=z)
    rowt, rowB, rowa, rowM, rowem, rowwi, rowws = (
        sb(n, [HEADS, T], at=z) for n in ("rowt", "rowB", "rowa", "rowM", "rowem", "rowwi", "rowws"))
    gcol = sb("gcol", [P, 2 * ST * HEADS], at=z)
    wgraw = sb("wgraw", [P, KD, 36], at=z)
    wgr = sb("wgr", [P, KD, 36], F32R, at=z)
    wgl = sb("wgl", [P, KD, 36], F32R, at=z)
    kwm = sb("kwm", [SMP, NB, P], at=z)
    smp = sb("smp", [P, 4 * SMP], at=z)
    wsm = sb("wsm", [SMP, NB], at=z)
    ENDS = [z[0]]
    Pm = [tg, sg]
    z = [ZONE]
    oq = [sb(f"oq{i}", [P, TM, T], at=z) for i in range(2)]
    ok = [sb(f"ok{i}", [P, TM, T], at=z) for i in range(2)]
    ov = [sb(f"ov{i}", [P, ST, DA], at=z) for i in range(2)]
    strip = sb("strip", [P, HEADS, SEQ], at=z)
    sstrip = sb("sstrip", [P, PAST + TB], at=z)
    sbias = sb("sbias", [P, PAIRS * SMP], at=z)
    kc = sb("kc", [P, 2, HEADS, NPG, PAGE], at=z)
    vc = sb("vc", [P, 2, NPG, DA], at=z)
    qbd = sb("qbd", [P, 2, 5 * 64], at=z)
    nlam = sb("nlam", [P, 8], at=z)
    lamt = sb("lamt", [P, 128], at=z)
    ENDS.append(z[0])
    assert max(ENDS) <= END, ("zone", [END - x for x in ENDS])

    ps = ctx.enter_context(nc.psum_tensor("ps", [P, 8, 512], F32))

    def unit(u):
        return ps[:, 2 * u:2 * u + 2, 0:HALF]

    def two(ap):
        return ap.rearrange("p (a t) -> p a t", a=2)

    psn = ps[:, 4:6, 0:HALF]

    def C(name, a=0, b=None, rows=P):
        o = COFF[name]
        return cst[0:rows, o + a:o + (CONST[name] if b is None else b)]

    def W(name, a, b=None, rows=P):
        o = POFF[name]
        return prm[0:rows, o + a:o + (a + 1 if b is None else b)]

    scratch = A["scratch"]

    CR_TILE = 1
    CR_EVAC = 2

    def done_at(p, t):
        return ph[p].t0 + t + 1 + CR_TILE

    def evac_at(p, t):
        return ph[p].t0 + t + 1 + CR_EVAC

    TOTAL_U = sum(CHUNKS)

    def st(k, q):
        o = 5 * (k % 2) + q
        return tiny[:, o:o + 1]

    DIFF_STEPS = [(hh, i) for hh in range(HEADS) for i in range(TM)]
    SB_STEPS = [(hh, c, i) for hh in range(HEADS) for i in range(TM) for c in range(2)]

    block = ctx.enter_context(nc.Block())

    @block.sync
    def _(e):
        e.dma_start(h[:], A["xT"]).then_inc(S("h_loaded"), 16)
        e.dma_start(prm[:], A["prm"]).then_inc(S("prm_loaded"), 16)
        e.dma_start(cst[:], A["cst"]).then_inc(S("cst_loaded"), 16)
        e.dma_start(pages[:], A["pages"]).then_inc(S("pages_loaded"), 16)
        for name in order:
            p = ph[name]
            with e.Fori(0, p.nb // 2) as i:
                for s in range(2):
                    e.wait_ge(S(f"w_split{s}"), i + (p.n0 // 2 + 1))
                    e.dma_start(raw[s][:, 0:p.width],
                                A[p.src][bass.ds(i * 2 + (p.at + s), 1)].rearrange("a p w -> p (a w)")
                                ).then_inc(S(f"raw_loaded{s}"), 16)

    @block.gpsimd
    def _(e):
        for s in range(2):
            e.memset(raw[s][:], 0.0).then_inc(S(f"w_split{s}"), 1)
        for name in order:
            p = ph[name]
            with e.Fori(0, p.nb // 2) as i:
                for s in range(2):
                    e.wait_ge(S("w_rounded"), i * 2 + (p.n0 + s + 1))
                    e.tensor_tensor(wl[s][:, 0:p.width], raw[s][:, 0:p.width],
                                    wr[s][:, 0:p.width].bitcast(F32), ALU.subtract
                                    ).then_inc(S(f"w_split{s}"), 1)

    @block.tensor
    def _(e):
        e.nop().then_inc(S("tile_done"), CR_TILE)

        def mm3(out, wrt, wlt, xrt, xlt, first, last):
            e.matmul(out, wrt, xrt, start=first, stop=False)
            e.matmul(out, wrt, xlt, start=False, stop=False)
            return e.matmul(out, wlt, xrt, start=False, stop=last)

        def gemm(name, rhs, ready):
            p = ph[name]
            with e.Fori(0, p.nb // 2) as i:
                for s in range(2):
                    e.wait_ge(S(f"w_split{s}"), i + (p.n0 // 2 + 2))
                    off = 0
                    for tile, kn_ in enumerate(p.ks):
                        t = s * p.T + tile
                        u = t % 2
                        e.wait_ge(S("tile_evacuated"), i * (2 * p.T) + (p.t0 + t - 2 + 1 + CR_EVAC))
                        for k in range(kn_):
                            need = ready(tile, k) if s == 0 else None
                            if need:
                                e.wait_ge(S(need[0]), need[1])
                            a, b = off + k * P, off + (k + 1) * P
                            r, q = rhs(tile, k)
                            for hf in range(2):
                                x0, x1 = hf * HALF, (hf + 1) * HALF
                                mm = mm3(ps[:, 2 * u + hf, 0:HALF], wr[s][:, a:b], wl[s][:, a:b],
                                         r[:, x0:x1], q[:, x0:x1], k == 0, k == kn_ - 1)
                        off += kn_ * P
                        mm.then_inc(S("tile_done"), 1)

        def xin(tile, k):
            return xr[:, k, :], xl[:, k, :]

        def norm_sum(m):
            e.wait_ge(S("acc_done"), KD * (m + 1))
            if m:
                e.wait_ge(S("root_ready"), m)
            for hf in range(2):
                mm = e.matmul(ps[:, 4 + hf, 0:HALF], ones[:], acc[:, hf * HALF:(hf + 1) * HALF],
                              start=True, stop=True)
            mm.then_inc(S("ss_ready"), 1)

        def x_of(m):
            return lambda tile, k: ("x_ready", KD * m + k + 1) if tile == 0 else None

        no_wait = lambda tile, k: None

        def ffn(n, m):
            hid = n * TOTAL_U
            for c, kc_ in enumerate(CHUNKS):
                gemm(("up", n, c), xin, x_of(m) if c == 0 else no_wait)
                hid += kc_
                gemm(("down", n, c), lambda tile, k: (hr[:, k, :], hl[:, k, :]),
                     lambda tile, k, hid=hid, kc_=kc_: {0: ("hidden_ready", hid - 1),
                                                        kc_ - 1: ("hidden_ready", hid)}.get(k))

        e.wait_ge(S("ones_ready"), 3)
        e.wait_ge(S("bias_loaded"), 32)
        for hh in range(HEADS):
            if hh:
                e.wait_ge(S("grep_copied"), hh)
            for hf in range(2):
                mm = e.matmul(ps[:, 6 + hf, 0:GL // 2], brel[:, hh * P:(hh + 1) * P],
                              bone[:, hf * (GL // 2):(hf + 1) * (GL // 2)], start=True, stop=True)
            mm.then_inc(S("grep_made"), 1)

        norm_sum(0)
        ffn(0, 0)
        norm_sum(1)

        gemm("glu", xin, x_of(1))
        e.wait_ge(S("wg_split"), 2)
        for hf in range(2):
            for k in range(KD):
                mm = mm3(ps[0:36, 6 + hf, 0:HALF], wgr[:, k, :], wgl[:, k, :],
                         xr[:, k, hf * HALF:(hf + 1) * HALF], xl[:, k, hf * HALF:(hf + 1) * HALF],
                         k == 0, k == KD - 1)
        mm.then_inc(S("gates_done"), 1)
        gemm("kv", xin, no_wait)

        def turn(src, phase, t, n):
            e.wait_ge(S("tile_evacuated"), evac_at(phase, t))
            if n:
                e.wait_ge(S("turned_copied"), 2 * n)
            else:
                e.wait_ge(S("root_ready"), 2)
            for i in range(ST):
                w = P if i < ST - 1 else SMP
                mm = e.transpose(ps[0:w, 4 + i // 4, (i % 4) * P:(i % 4 + 1) * P],
                                 src[:, i * P:i * P + w], C("ident"))
            mm.then_inc(S("turned"), 1)

        for n in range(8):
            turn(kT[:, n, :] if n < 4 else vtmp[n - 4][:], "kv", n, n)
        e.wait_ge(S("rows_exp"), 3)
        e.wait_ge(S("turned_copied"), 16)
        for q, row in enumerate((rowa, rowws)):
            for i in range(ST):
                w = P if i < ST - 1 else SMP
                o = (q * ST + i) * HEADS
                mm = e.transpose(ps[0:w, 4, o:o + HEADS], row[:, i * P:i * P + w],
                                 C("ident", 0, 4, rows=4))
        mm.then_inc(S("cols_turned"), 1)
        gemm("qo", xin, no_wait)

        e.wait_ge(S("conv_done"), TM)
        e.wait_ge(S("cols_copied"), 4)
        for j in range(TM):
            for hf in range(2):
                mm = e.matmul(ps[:, 4 + hf, 0:HALF], ones[:], cv[:, j, hf * HALF:(hf + 1) * HALF],
                              start=j == 0, stop=j == TM - 1)
        mm.then_inc(S("ln_sum"), 1)
        for j in range(TM):
            e.wait_ge(S("ln_sq"), j + 1)
            if j == 0:
                e.wait_ge(S("ln_centered"), TM)
            for hf in range(2):
                mm = e.matmul(ps[:, 4 + hf, 0:HALF], ones[:], (hd, sq)[j % 2][:, hf * HALF:(hf + 1) * HALF],
                              start=j == 0, stop=j == TM - 1)
            mm.then_inc(S("ln_var"), 1)

        e.wait_ge(S("tile_evacuated"), evac_at("qo", 7))
        e.wait_ge(S("ln_root"), 1)
        e.wait_ge(S("vn_ones"), 1)
        for hh in range(HEADS):
            if hh:
                e.wait_ge(S("head_done"), hh)
            sel = C("sel", hh * P, (hh + 1) * P, rows=4)
            e.matmul(ps[:, 0, 0:SEQ], sel, rowM[:, 0:SEQ], start=True, stop=True)
            e.matmul(ps[:, 1, 0:SEQ], sel, rowem[:, 0:SEQ], start=True, stop=True)
            for q, row in enumerate((rowM, rowem, rowwi)):
                mm = e.matmul(ps[:, 6, SMP * q:SMP * (q + 1)], sel, row[:, SEQ:T], start=True, stop=True)
            mm.then_inc(S("bcast_ready"), 1)
            q_, k_ = qT[:, hh, :], kT[:, hh, :]

            def scores(i):
                w = P if i < ST - 1 else SMP
                n0 = i * P
                n1 = SEQ if i < ST - 1 else T
                if i >= 2:
                    e.wait_ge(S("p_ready"), ST * hh + i - 1)
                e.matmul(ps[0:w, 4 + i % 2, 0:n1 - n0], k_[:, n0:n0 + w], q_[:, n0:n1],
                         start=True, stop=True).then_inc(S("s_ready"), 1)

            def values(i):
                n0 = i * P
                e.wait_ge(S("p_ready"), ST * hh + i + 1)
                if i < ST - 1:
                    e.matmul(ps[:, 2, n0:SEQ], vn[:, i, hh, 0:P], Pm[i % 2][:, 0:SEQ - n0],
                             start=i == 0, stop=i == ST - 2)
                    e.matmul(ps[:, 3, n0:SEQ], ones[:], Pm[i % 2][:, 0:SEQ - n0],
                             start=i == 0, stop=i == ST - 2).then_inc(S("pv_done"), 1)
                else:
                    o = 3 * SMP
                    e.matmul(ps[:, 6, o:o + SMP], vn[0:SMP, i, hh, 0:P], Pm[i % 2][0:SMP, 0:SMP],
                             start=True, stop=True)
                    e.matmul(ps[:, 6, o + SMP:o + 2 * SMP], ones[0:SMP, :], Pm[i % 2][0:SMP, 0:SMP],
                             start=True, stop=True).then_inc(S("pv_done"), 1)

            scores(0)
            scores(1)
            for i in range(ST):
                values(i)
                if i + 2 < ST:
                    scores(i + 2)
            e.wait_ge(S("qn_ready"), hh + 1)
            for b in range(NB):
                o = 5 * SMP + b * TB
                e.matmul(ps[:, 6, o:o + TB], C0[:, b, 0:P], q_[:, SEQ + b * TB:SEQ + (b + 1) * TB],
                         start=True, stop=True)
            e.matmul(ps[:, 6, 6 * SMP:7 * SMP], ones[:], smp[:, 3 * SMP:4 * SMP], start=True, stop=True
                     ).then_inc(S("inter_ready"), 1)
            e.wait_ge(S("kw_ready"), hh + 1)
            for i in range(TM):
                mm = e.matmul(ps[:, 7, 0:P + 1], kw[:, i, :], vn[:, i, hh, :], start=i == 0, stop=i == TM - 1)
            e.wait_ge(S("h_read"), hh + 1)
            for b in range(NB):
                o = (b % 3) * (P + 1)
                mm = e.matmul(ps[:, b // 3, o:o + P + 1], kwm[:, b, :], vn[0:SMP, ST - 1, hh, :],
                              start=True, stop=True)
            mm.then_inc(S("state_ready"), 1)

        e.wait_ge(S("head_done"), HEADS)
        gemm(("out", 0), xin, lambda tile, k: ("mix_ready", k + 1) if tile == 0 else None)
        norm_sum(2)
        ffn(1, 2)
        norm_sum(3)

        def ple(l):
            gemm(("ple", l), lambda tile, k: (xr[:, k, :], xl[:, k, :]) if tile == 0
                 else (pr[:, k, :], pl[:, k, :]),
                 lambda tile, k: ("x_ready", KD * (4 * l + 3) + k + 1) if tile == 0 else ("p_split", l + 1))

        ple(0)
        norm_sum(4)
        ffn(2, 4)
        norm_sum(5)

        gemm("qk0", xin, x_of(5))
        gemm("v0", xin, no_wait)
        e.wait_ge(S("root_ready"), 6)
        for n in range(4):
            turn(vtmp[n][:], "v0", n, 8 + n)
        gemm("qk1", xin, no_wait)
        gemm("v1", xin, no_wait)
        for n in range(4):
            turn(vtmp[n][:], "v1", n, 12 + n)
        e.wait_ge(S("turned_copied"), 32)
        e.wait_ge(S("tile_evacuated"), evac_at("v1", 3))

        def turn_rows(u, src, w, other=None):
            e.wait_ge(S("rows_done"), u + 1)
            if u >= 2:
                e.wait_ge(S("rowsT_copied"), u - 1)
            nblk = (w + P - 1) // P
            for b in range(nblk):
                wb = min(P, w - b * P)
                if other is None:
                    mm = e.transpose(ps[0:wb, 4 + u % 2, b * P:(b + 1) * P], src[:, b * P:b * P + wb], C("ident"))
                else:
                    mm = e.matmul(ps[0:wb, 4 + u % 2, b * 64:(b + 1) * 64], src[:, b * P:b * P + wb], other,
                                  start=True, stop=True)
            mm.then_inc(S("rows_turned"), 1)

        N = len(DIFF_STEPS)
        for tick in range(N + 3):
            if tick < N:
                hh, i = DIFF_STEPS[tick]
                for c in range(2):
                    if tick >= 2:
                        e.wait_ge(S("biased"), 2 * (tick - 2) + c + 1)
                    e.matmul(ps[:, 2 * (tick % 2) + c, 0:(i + 1) * P], oq[0][64 * c:64 * c + 64, hh, i * P:(i + 1) * P],
                             ok[0][64 * c:64 * c + 64, hh, 0:(i + 1) * P], start=True, stop=True
                             ).then_inc(S("scores"), 1)
            if 2 <= tick < N + 2:
                u = tick - 2
                hh, i = DIFF_STEPS[u]
                turn_rows(u, (tg, tu)[u % 2], (i + 1) * P)
            if tick >= 3:
                u = tick - 3
                hh, i = DIFF_STEPS[u]
                e.wait_ge(S("rowsT_copied"), u + 1)
                if i == 0 and hh >= 2:
                    e.wait_ge(S("attn_copied"), hh - 1)
                for b in range(i + 1):
                    mm = e.matmul(ps[:, 6 + hh % 2, i * P:(i + 1) * P], ov[0][:, b, hh * P:(hh + 1) * P],
                                  (sq, acc)[u % 2][:, b * P:(b + 1) * P], start=b == 0, stop=b == i)
                mm.then_inc(S("attn_out"), 1)
        M = len(SB_STEPS)
        for tick in range(M + 4):
            if tick < M:
                hh, c, i = SB_STEPS[tick]
                if tick >= 4:
                    e.wait_ge(S("summed"), tick - 3)
                elif tick == 0:
                    e.wait_ge(S("biased"), 2 * N)
                e.matmul(ps[:, tick % 4, 0:(i + 1) * P], oq[1][64 * c:64 * c + 64, hh, i * P:(i + 1) * P],
                         ok[1][64 * c:64 * c + 64, hh, 0:(i + 1) * P], start=True, stop=True
                         ).then_inc(S("scores"), 1)
            if 3 <= tick < M + 3:
                u = tick - 3
                hh, c, i = SB_STEPS[u]
                turn_rows(N + u, (tg, tu)[u % 2], (i + 1) * P)
            if tick >= 4:
                u = tick - 4
                hh, c, i = SB_STEPS[u]
                e.wait_ge(S("rowsT_copied"), N + u + 1)
                if i == 0 and c == 0:
                    e.wait_ge(S("attn_copied"), HEADS + hh - 1)
                for b in range(i + 1):
                    mm = e.matmul(ps[64 * c:64 * c + 64, 6 + hh % 2, i * P:(i + 1) * P],
                                  ov[1][:, b, (2 * hh + c) * 64:(2 * hh + c + 1) * 64],
                                  (sq, acc)[(N + u) % 2][:, b * P:(b + 1) * P], start=b == 0, stop=b == i)
                mm.then_inc(S("attn_out"), 1)
        for kind in range(2):
            for pair in range(PAIRS):
                u = N + M + kind * PAIRS + pair
                job = kind * PAIRS + pair
                e.wait_ge(S("qbd_ready"), job + 1)
                e.wait_ge(S("keys_loaded"), 16 * 2 * NPG * (job + 1))
                if job == 0:
                    e.wait_ge(S("summed"), M)
                    e.wait_ge(S("attn_copied"), 2 * HEADS)
                for b in range(2):
                    for hh in range(HEADS):
                        e.matmul(ps[64 * b:64 * b + 64, 0, 0:PAST], qbd[:, b, hh * 64:(hh + 1) * 64],
                                 kc[:, b, hh, :, :].rearrange("p g s -> p (g s)"),
                                 start=hh == 0, stop=hh == HEADS - 1)
                    for hh in range(HEADS):
                        mm = e.matmul(ps[64 * b:64 * b + 64, 0, PAST:KEYS], qbd[:, b, hh * 64:(hh + 1) * 64],
                                      ok[kind][:, hh, SEQ:T], start=hh == 0, stop=hh == HEADS - 1)
                mm.then_inc(S("scores"), 1)
                turn_rows(u, tg, KEYS, C("fold") if kind == 0 else None)
                e.wait_ge(S("rowsT_copied"), u + 1)
                e.wait_ge(S("values_loaded"), 16 * 2 * NPG * (job + 1))
                if job:
                    e.wait_ge(S("sample_copied"), job)
                rt = (sq, acc)[u % 2]
                for b in range(2):
                    for hh in range(HEADS):
                        w, pitch = (TB, 64) if kind == 0 else (2 * TB, P)
                        o = (b * HEADS + hh) * w
                        for g in range(NPG + 1):
                            r = P if g < NPG else SMP
                            lhs = vc[:, b, g, hh * P:(hh + 1) * P] if g < NPG else ov[kind][0:SMP, ST - 1, hh * P:(hh + 1) * P]
                            mm = e.matmul(ps[:, 6, o:o + w], lhs, rt[0:r, g * pitch + o:g * pitch + o + w],
                                          start=g == 0, stop=g == NPG)
                mm.then_inc(S("sample_out"), 1)

        for hh in range(HEADS):
            e.wait_ge(S("oc_sq"), hh + 1)
            if hh:
                e.wait_ge(S("oc_root"), hh)
            for hf in range(2):
                mm = e.matmul(ps[:, 4 + hf, 0:HALF], ones[:], (sg, hd)[hh % 2][:, hf * HALF:(hf + 1) * HALF],
                              start=True, stop=True)
            mm.then_inc(S("oc_ss"), 1)
        e.wait_ge(S("oc_root"), HEADS)
        gemm(("out", 1), xin, lambda tile, k: ("mix_ready", KD + k + 1) if tile == 0 else None)
        norm_sum(6)
        ffn(3, 6)
        norm_sum(7)
        ple(1)
        norm_sum(8)

    @block.scalar
    def _(e):
        def width_after(name):
            at = order.index(name) + 1
            return ph[order[at]].width if at < len(order) else 0

        def round_block(name, i, s, first=False):
            p = ph[name]
            if first:
                k, slot = p.n0 // 2 + 1, 0
                e.wait_ge(S("raw_loaded0"), 16 * k)
                w = p.width
            else:
                slot = 1 - s
                e.wait_ge(S(f"raw_loaded{slot}"), i * 16 + 16 * (p.n0 // 2 + 1 + s))
                e.wait_ge(S("tile_done"), i * (2 * p.T) + (p.t0 + p.T * s + CR_TILE))
                w = max(p.width, width_after(name)) if s == 1 else p.width
            e.activation(wr[slot][:, 0:w], raw[slot][:, 0:w], ACT.Copy).then_inc(S("w_rounded"), 1)

        def blocks(name):
            p = ph[name]
            for n in range(p.nb):
                if not (name == order[-1] and n == p.nb - 1):
                    round_block(name, n // 2, n % 2)
                yield n

        def square(m, j, wait):
            if wait:
                e.wait_ge(*wait)
            if m or not isinstance(j, int) or j:
                e.wait_ge(S("acc_done"), j + KD * m)
            if not isinstance(j, int):
                e.nop(nofuse=True)
            hj = h[:, bass.ds(j, 1), :].rearrange("p a t -> p (a t)")
            e.activation(sq[:], hj, ACT.Square).then_inc(S("sq_ready"), 1)

        def head(m, j, wait=None):
            if wait:
                e.wait_ge(*wait)
                e.nop(nofuse=True)
            hj = h[:, bass.ds(j, 1), :].rearrange("p a t -> p (a t)")
            xj = xr[:, bass.ds(j, 1), :].rearrange("p a t -> p (a t)")
            g0 = POFF["gains"] + m * KD
            e.activation(xj, hj, ACT.Copy, scale=prm[:, bass.ds(j + g0, 1)]).then_inc(S("xr_ready"), 1)

        def root(m):
            e.wait_ge(S("ss_ready"), m + 1)
            e.activation(two(R[:]), psn, ACT.Sqrt, scale=1.0 / D, bias=eps6[:, 0:1]).then_inc(S("root_ready"), 1)

        def up_phase(n, c):
            p = ph[("up", n, c)]
            u0 = n * TOTAL_U + (CHUNKS[0] if c else 0)
            with e.Fori(0, p.nb // 2) as i:
                for s in range(2):
                    round_block(("up", n, c), i, s)
                    e.wait_ge(S("tile_evacuated"), i * 4 + (p.t0 + 2 * s + 1 + CR_EVAC))
                    e.activation(sg[:], tg[:], ACT.Silu).then_inc(S("silu_ready"), 1)
                    e.wait_ge(S("hidden_made"), i * 2 + (u0 + s + 1))
                    e.nop(nofuse=True)
                    e.activation(hr[:, bass.ds(i * 2 + s, 1), :].rearrange("p a t -> p (a t)"), hd[:], ACT.Copy
                                 ).then_inc(S("hr_ready"), 1)

        def down_phase(n, c, m_next):
            p = ph[("down", n, c)]
            with e.Fori(0, p.nb // 2) as i:
                for s in range(2):
                    round_block(("down", n, c), i, s)
                    if c == 1:
                        w = (S("tile_evacuated"), i * 2 + (p.t0 + s + 1 + CR_EVAC))
                        head(m_next, i * 2 + s, w)
                        square(m_next, i * 2 + s, None)

        def ffn(n, m):
            up_phase(n, 0)
            down_phase(n, 0, None)
            up_phase(n, 1)
            down_phase(n, 1, m + 1)
            root(m + 1)

        e.dma_start(brel[:], A["brel"]).then_inc(S("bias_loaded"), 16)
        e.dma_start(bone[:], A["bone"]).then_inc(S("bias_loaded"), 16)
        e.wait_ge(S("h_loaded"), 16)
        e.wait_ge(S("prm_loaded"), 16)
        for j in range(KD):
            head(0, j)
            square(0, j, (S("h_loaded"), 16))
        round_block(order[0], 0, 0, first=True)
        for hh in range(HEADS):
            e.wait_ge(S("grep_copied"), hh + 1)
            e.dma_start(scratch[hh].rearrange("(p y) -> p y", p=P), grep[:]).then_inc(S("grep_stored"), 16)
        e.wait_ge(S("ones_ready"), 3)
        root(0)
        ffn(0, 0)

        e.dma_start(wgraw[:], A["wg"]).then_inc(S("wg_loaded"), 16)
        e.dma_start(us[:, :, :, 0:HIST], A["hist"]).then_inc(S("hist_loaded"), 16)
        e.wait_ge(S("wg_loaded"), 16)
        e.activation(wgr[:], wgraw[:], ACT.Copy).then_inc(S("wgr_ready"), 1)
        for n in blocks("glu"):
            e.wait_ge(S("tile_evacuated"), evac_at("glu", 2 * n + 1))
            e.activation(sg[:], tu[:], ACT.Sigmoid).then_inc(S("glu_sig"), 1)
        e.wait_ge(S("u_ready"), 2 * TM)
        e.dma_start(A["conv_p"], up[:, :, SEQ:SEQ + HIST]).then_inc(S("conv_stored"), 16)
        e.wait_ge(S("hist_loaded"), 16)
        for j in range(TM):
            e.dma_start(A["conv_s"][:, j], us[:, j, :, TB:TB + HIST]).then_inc(S("conv_stored"), 16)
        for n in blocks("kv"):
            if n == 0:
                e.wait_ge(S("row_z"), 1)
                e.activation(rowB[:], rowt[:], ACT.Abs).then_inc(S("row_act"), 1)
                e.wait_ge(S("row_act"), 1)
                e.activation(rowB[:], rowB[:], ACT.Exp, scale=-1.0).then_inc(S("row_act"), 1)
                e.wait_ge(S("row_act"), 2)
                e.activation(rowB[:], rowB[:], ACT.Ln, bias=1.0).then_inc(S("row_act"), 1)
            if n == 1:
                e.wait_ge(S("row_m"), 1)
                e.dma_start(A["mrow"], rowt[:]).then_inc(S("m_stored"), 16)
                e.activation(rowem[:], rowt[:], ACT.Exp, scale=-1.0).then_inc(S("rows_exp"), 1)
                e.wait_ge(S("row_m"), 2)
                e.activation(rowwi[:, SEQ:T], rowwi[:, SEQ:T], ACT.Exp).then_inc(S("rows_exp"), 1)
                e.wait_ge(S("row_m"), 4)
                e.activation(rowws[:], rowws[:], ACT.Exp).then_inc(S("rows_exp"), 1)

        def copy_turned(n, full, part):
            e.wait_ge(S("turned"), n + 1)
            e.activation(full, ps[:, 4, :].rearrange("p (i d) -> p i d", d=P), ACT.Copy
                         ).then_inc(S("turned_copied"), 1)
            e.activation(part, ps[0:SMP, 5, 0:P], ACT.Copy).then_inc(S("turned_copied"), 1)

        for n in range(8):
            dst = kn[:, :, n, :] if n < 4 else vn[:, :, n - 4, 0:P]
            copy_turned(n, dst[:, 0:TM, :], dst[0:SMP, TM, :])
        for n in blocks("qo"):
            if n >= 2:
                for o in (2 * (n - 2), 2 * (n - 2) + 1):
                    e.wait_ge(S("tile_evacuated"), evac_at("qo", 4 + o))
                    e.activation(oT[:, o, :], tu[:], ACT.Sigmoid).then_inc(S("o_ready"), 1)
        e.wait_ge(S("conv_stored"), 16 * (1 + TM))
        for j in range(TM):
            e.wait_ge(S("ln_centered"), j + 1)
            if j >= 2:
                e.wait_ge(S("ln_var"), j - 1)
            e.activation((hd, sq)[j % 2][:], cv[:, j, :], ACT.Square).then_inc(S("ln_sq"), 1)
        e.wait_ge(S("ln_var"), TM)
        e.activation(two(acc[:]), psn, ACT.Sqrt, scale=1.0 / DA, bias=eps5[:, 0:1]).then_inc(S("ln_root"), 1)
        for j in range(TM):
            e.wait_ge(S("ln_scaled"), j + 1)
            e.activation(cv[:, j, :], cv[:, j, :], ACT.Silu, scale=W("ln_g", j), bias=W("ln_b", j)
                         ).then_inc(S("conv_out"), 1)
            e.wait_ge(S("conv_out"), j + 1)
            e.activation(xr[:, j, :], cv[:, j, :], ACT.Copy).then_inc(S("mixr_ready"), 1)
        def load_state(hh):
            e.dma_start(C0[:], A["C0"][hh]).then_inc(S("C0_loaded"), 16)

        load_state(0)
        for hh in range(HEADS):
            e.wait_ge(S("bcast_ready"), hh + 1)
            if hh == 0:
                e.wait_ge(S("mix_ready"), TM)
            else:
                e.wait_ge(S("head_done"), hh)
            e.activation(hd[:, 0:SEQ], ps[:, 1, 0:SEQ], ACT.Copy).then_inc(S("em_copied"), 1)
            for i in range(ST):
                w = SEQ - i * P if i < TM else SMP
                r = P if i < TM else SMP
                e.wait_ge(S("gap_ready"), ST * hh + i + 1)
                e.activation(Ds[0:r, i % 2, 0:w], Xs[0:r, i % 2, 0:w], ACT.Exp, scale=-1.0
                             ).then_inc(S("decay_ready"), 1)
            e.wait_ge(S("b_out"), hh + 1)
            e.activation(xr[:, TM + hh, :], sq[:], ACT.Copy).then_inc(S("mixr_ready"), 1)
            e.wait_ge(S("head_done"), hh + 1)
            e.dma_start(A["Cp"][hh], Cp[:]).then_inc(S("C_stored"), 16)
            e.dma_start(A["Cs"][hh], Cn[:]).then_inc(S("C_stored"), 16)
            if hh + 1 < HEADS:
                load_state(hh + 1)

        def out_phase(name, m):
            for n in blocks(name):
                for j in (2 * n, 2 * n + 1):
                    square(m, j, (S("tile_evacuated"), evac_at(name, j)))

        def heads_after(m):
            for j in range(KD):
                head(m, j)

        out_phase(("out", 0), 2)
        heads_after(2)
        root(2)
        e.wait_ge(S("C_stored"), 32 * HEADS)
        e.wait_ge(S("m_stored"), 16)
        ffn(1, 2)

        def ple(l):
            m = 4 * l + 4
            e.dma_start(praw[:], A["pT"][l]).then_inc(S("p_loaded"), 16)
            name = ("ple", l)
            for n in blocks(name):
                if n == 0:
                    e.wait_ge(S("p_loaded"), 16 * (l + 1))
                    e.activation(pr[:], praw[:], ACT.Copy).then_inc(S("pr_ready"), 1)
                e.wait_ge(S("tile_evacuated"), evac_at(name, 2 * n))
                e.activation(sg[:], tg[:], ACT.Sigmoid).then_inc(S("ple_sig"), 1)
                square(m, n, (S("ple_added"), KD * l + n + 1))
            if l == 0:
                heads_after(m)
            root(m)

        ple(0)
        ffn(2, 4)

        for hh in range(HEADS):
            e.dma_start(strip[:, hh, :],
                        scratch[hh, P - 1:P - 1 + P * (GL - 1)].rearrange("(p x) -> p x", x=GL - 1)[:, 0:SEQ]
                        ).then_inc(S("strip_loaded"), 16)
            for b in range(2):
                for c in range(2):
                    r = b * 64 + hh * 16 + c * 8
                    o = PAST - 1
                    e.dma_start(sstrip[r:r + TB, :],
                                scratch[hh, o:o + TB * (GL - 1)].rearrange("(t x) -> t x", x=GL - 1)[:, 0:PAST + TB]
                                ).then_inc(S("strip_loaded"), 16)
        e.wait_ge(S("lam_sums"), 1)
        e.activation(nlam[:, 0:2], nlam[:, 2:4], ACT.Exp).then_inc(S("lam_exp"), 1)
        for kind in range(2):
            for n in blocks(f"qk{kind}"):
                if n == 3:
                    e.wait_ge(S("tile_evacuated"), evac_at(f"qk{kind}", 7))
                    e.dma_start(A[("dk", "sk")[kind]], ok[kind][:]).then_inc(S("kv_stored"), 16)
            for n in blocks(f"v{kind}"):
                for t in (2 * n, 2 * n + 1):
                    e.wait_ge(S("tile_evacuated"), evac_at(f"v{kind}", t))
                    e.dma_start(A[("dv", "sv")[kind]][:, t], vtmp[t][:]).then_inc(S(f"v_stored{t}"), 16)
            for n in range(4):
                dst = ov[kind][:, :, n * P:(n + 1) * P]
                copy_turned(8 + 4 * kind + n, dst[:, 0:TM, :], dst[0:SMP, TM, :])
        for t in range(4):
            e.wait_ge(S(f"v_stored{t}"), 32)

        def load_cache(job):
            kind, pair = job // PAIRS, job % PAIRS
            for b in range(2):
                for g in range(NPG):
                    n = (2 * pair + b) * NPG + g
                    pg = e.value_load(pages[0:1, n:n + 1], min_val=0, max_val=A["kc0"].shape[0] - 1)
                    e.dma_start(kc[:, b, :, g, :],
                                A[f"kc{kind}"][bass.ds(pg, 1)].rearrange("a p h s -> p (a h) s")
                                ).then_inc(S("keys_loaded"), 16)
                    e.dma_start(vc[:, b, g, :],
                                A[f"vc{kind}"][bass.ds(pg, 1)].rearrange("a s d -> (a s) d")
                                ).then_inc(S("values_loaded"), 16)

        e.wait_ge(S("pages_loaded"), 16)
        load_cache(0)

        def copy_rowsT(u, w, last):
            e.wait_ge(S("rows_turned"), u + 1)
            if u >= 2:
                e.wait_ge(S("attn_out") if u - 2 < NM else S("sample_out"),
                          u - 1 if u - 2 < NM else u - 1 - NM)
            dst, b = (sq, acc)[u % 2], 4 + u % 2
            ins = e.activation(dst[:, 0:w], ps[:, b, 0:w], ACT.Copy)
            if last:
                ins.then_inc(S("rowsT_part"), 1)
                ins = e.activation(dst[0:SMP, w:w + last], ps[0:SMP, b, w:w + last], ACT.Copy)
            ins.then_inc(S("rowsT_copied"), 1)

        def copy_attn(kind, hh, n_out):
            e.wait_ge(S("attn_out"), n_out)
            e.activation(oq[kind][:, hh, 0:SEQ], ps[:, 6 + hh % 2, :], ACT.Copy).then_inc(S("attn_copied"), 1)

        N, M = len(DIFF_STEPS), len(SB_STEPS)
        NM = N + M
        for tick in range(N + 3):
            if tick < N:
                hh, i = DIFF_STEPS[tick]
                w = (i + 1) * P
                for c in range(2):
                    e.wait_ge(S("maxed"), 2 * tick + c + 1)
                    buf = ((tg, sg), (tu, hd))[tick % 2][c]
                    e.activation(buf[:, 0:w], buf[:, 0:w], ACT.Exp, bias=st(tick, c),
                                 accum_out=st(tick, 2 + c)).then_inc(S("exped"), 1)
            if 2 <= tick < N + 2:
                u = tick - 2
                copy_rowsT(u, (DIFF_STEPS[u][1] + 1) * P, 0)
            if tick >= 3:
                hh, i = DIFF_STEPS[tick - 3]
                if i == TM - 1:
                    copy_attn(0, hh, tick - 2)

        def soft(u, width, src, k):
            buf = (tg, tu)[u % 2]
            e.wait_ge(S("scores"), 2 * N + k + 1 + (PAIRS if k >= M else 0))
            e.activation(buf[:, 0:width], src, ACT.Abs).then_inc(S("soft_step"), 1)
            e.wait_ge(S("soft_step"), 3 * k + 1)
            e.activation(buf[:, 0:width], buf[:, 0:width], ACT.Exp, scale=-1.0).then_inc(S("soft_step"), 1)
            e.wait_ge(S("soft_step"), 3 * k + 2)
            e.activation(buf[:, 0:width], buf[:, 0:width], ACT.Ln, bias=1.0).then_inc(S("soft_step"), 1)

        def weights(u, width, k):
            e.wait_ge(S("summed"), k + 1)
            buf = (tg, tu)[u % 2]
            e.activation(buf[:, 0:width], buf[:, 0:width], ACT.Exp, bias=st(k, 4)).then_inc(S("rows_done"), 1)

        for tick in range(M + 4):
            if 1 <= tick < M + 1:
                u = tick - 1
                weights(N + u, (SB_STEPS[u][2] + 1) * P, u)
            if tick < M:
                e.wait_ge(S("rows_turned"), N + max(tick - 1, 0))
                soft(N + tick, (SB_STEPS[tick][2] + 1) * P, ps[:, tick % 4, 0:(SB_STEPS[tick][2] + 1) * P], tick)
            if 3 <= tick < M + 3:
                u = tick - 3
                copy_rowsT(N + u, (SB_STEPS[u][2] + 1) * P, 0)
            if tick >= 4:
                hh, c, i = SB_STEPS[tick - 4]
                if i == TM - 1 and c == 1:
                    copy_attn(1, hh, N + tick - 3)

        for job in range(2 * PAIRS):
            kind, pair = job // PAIRS, job % PAIRS
            u = NM + job
            if kind == 0:
                e.wait_ge(S("maxed"), 2 * N + pair + 1)
                e.activation(tg[:, 0:KEYS], tg[:, 0:KEYS], ACT.Exp, bias=st(0, 0), accum_out=st(0, 2)
                             ).then_inc(S("exped"), 1)
                copy_rowsT(u, 2 * 64, 64)
            else:
                k = M + pair
                e.wait_ge(S("rows_turned"), u)
                soft(0, KEYS, ps[:, 0, 0:KEYS], k)
                weights(0, KEYS, k)
                copy_rowsT(u, 2 * P, P)
            e.wait_ge(S("sample_out"), job + 1)
            if job + 1 < 2 * PAIRS:
                load_cache(job + 1)

        for hh in range(HEADS):
            e.wait_ge(S("sample_copied"), 2 * PAIRS)
            if hh >= 2:
                e.wait_ge(S("oc_ss"), hh - 1)
            e.activation((sg, hd)[hh % 2][:], oq[0][:, hh, :], ACT.Square).then_inc(S("oc_sq"), 1)
            e.wait_ge(S("oc_ss"), hh + 1)
            if hh >= 2:
                e.wait_ge(S("oc_scaled"), hh - 1)
            e.activation(two((tg, tu)[hh % 2][:]), psn, ACT.Sqrt, scale=1.0 / P, bias=eps6[:, 0:1]
                         ).then_inc(S("oc_root"), 1)
        for j in range(KD):
            if j < HEADS:
                e.wait_ge(S("oc_scaled"), j + 1)
            e.activation(xr[:, j, :], oq[j // TM][:, j % TM, :], ACT.Copy).then_inc(S("mixr_ready"), 1)

        out_phase(("out", 1), 6)
        heads_after(6)
        root(6)
        e.wait_ge(S("kv_stored"), 32)
        ffn(3, 6)
        ple(1)
        for sem, n in (("conv_stored", 16 * (1 + TM)), ("m_stored", 16), ("C_stored", 32 * HEADS),
                       ("kv_stored", 32), ("grep_stored", 16 * HEADS)):
            e.wait_ge(S(sem), n)
        for j in range(KD):
            e.wait_ge(S("y_ready"), j + 1)
            e.dma_start(A["yT"][:, j], h[:, j, :]).then_inc(S("y_stored"), 16)
        e.wait_ge(S("y_stored"), 16 * KD)

    @block.vector
    def _(e):
        e.nop().then_inc(S("tile_evacuated"), CR_EVAC)
        e.memset(eps6[:], 1e-6).then_inc(S("ones_ready"), 1)
        e.memset(eps5[:], 1e-5).then_inc(S("ones_ready"), 1)
        e.memset(ones[:], 1.0).then_inc(S("ones_ready"), 1)
        stepped = [0]

        def step(ins):
            stepped[0] += 1
            ins.then_inc(S("dve_step"), 1)

        def settle():
            e.wait_ge(S("dve_step"), stepped[0])

        def rest(m, j):
            e.wait_ge(S("xr_ready"), j + (KD * m + 1))
            hj = h[:, bass.ds(j, 1), :].rearrange("p a t -> p (a t)")
            xj = xr[:, bass.ds(j, 1), :].rearrange("p a t -> p (a t)")
            lj = xl[:, bass.ds(j, 1), :].rearrange("p a t -> p (a t)")
            e.scalar_tensor_tensor(lj, hj, prm[:, bass.ds(j + (POFF["gains"] + m * KD), 1)], xj.bitcast(F32),
                                   ALU.mult, ALU.subtract).then_inc(S("x_ready"), 1)

        def add_square(m, j, first):
            e.wait_ge(S("sq_ready"), j + (KD * m + 1))
            if first:
                e.tensor_copy(acc[:], sq[:]).then_inc(S("acc_done"), 1)
            else:
                e.wait_ge(S("acc_done"), j + KD * m)
                e.tensor_tensor(acc[:], acc[:], sq[:], ALU.add).then_inc(S("acc_done"), 1)

        def zero_acc(m):
            if m:
                e.wait_ge(S("ss_ready"), m)
            e.memset(acc[:], 0.0).then_inc(S("acc_zero"), 1)
            e.wait_ge(S("acc_zero"), zeroed[0] + 1)
            zeroed[0] += 1

        zeroed = [0]

        def factor(m):
            e.wait_ge(S("root_ready"), m + 1)
            e.reciprocal(R[:], R[:]).then_inc(S("R_ready"), 1)
            e.wait_ge(S("R_ready"), m + 1)

        def normed(out, u, wait, scale=None):
            e.wait_ge(S("tile_done"), wait)
            if scale is None:
                ins = e.tensor_tensor(two(out), unit(u), two(R[:]), ALU.mult)
            else:
                ins = e.scalar_tensor_tensor(two(out), unit(u), scale, two(R[:]), ALU.mult, ALU.mult)
            ins.then_inc(S("tile_evacuated"), 1)

        def up_phase(n, c):
            p = ph[("up", n, c)]
            u0 = n * TOTAL_U + (CHUNKS[0] if c else 0)
            with e.Fori(0, p.nb // 2) as i:
                for s in range(2):
                    t = p.t0 + 2 * s
                    normed(tg[:], 0, i * 4 + (t + 1 + CR_TILE))
                    normed(tu[:], 1, i * 4 + (t + 2 + CR_TILE))
                    e.wait_ge(S("silu_ready"), i * 2 + (u0 + s + 1))
                    e.wait_ge(S("tile_evacuated"), i * 4 + (t + 2 + CR_EVAC))
                    e.tensor_tensor(hd[:], tu[:], sg[:], ALU.mult).then_inc(S("hidden_made"), 1)
                    e.wait_ge(S("hr_ready"), i * 2 + (u0 + s + 1))
                    r = hr[:, bass.ds(i * 2 + s, 1), :].rearrange("p a t -> p (a t)")
                    q = hl[:, bass.ds(i * 2 + s, 1), :].rearrange("p a t -> p (a t)")
                    e.tensor_tensor(q, hd[:], r.bitcast(F32), ALU.subtract).then_inc(S("hidden_ready"), 1)

        def down_phase(n, c, m_next):
            p = ph[("down", n, c)]
            with e.Fori(0, p.nb // 2) as i:
                for s in range(2):
                    j = i * 2 + s
                    e.wait_ge(S("tile_done"), i * 2 + (p.t0 + s + 1 + CR_TILE))
                    hj = h[:, bass.ds(j, 1), :].rearrange("p o (a t) -> p (o a) t", a=2)
                    e.scalar_tensor_tensor(hj, unit(s), 0.5, hj, ALU.mult, ALU.add
                                           ).then_inc(S("tile_evacuated"), 1)
                    if c == 1:
                        e.wait_ge(S("tile_evacuated"), i * 2 + (p.t0 + s + 1 + CR_EVAC))
                        rest(m_next, j)
                        e.wait_ge(S("sq_ready"), i * 2 + (KD * m_next + s + 1))
                        e.wait_ge(S("acc_done"), i * 2 + (KD * m_next + s))
                        e.tensor_tensor(acc[:], acc[:], sq[:], ALU.add).then_inc(S("acc_done"), 1)

        def ffn(n, m):
            up_phase(n, 0)
            down_phase(n, 0, None)
            up_phase(n, 1)
            zero_acc(m + 1)
            down_phase(n, 1, m + 1)
            factor(m + 1)

        e.wait_ge(S("h_loaded"), 16)
        e.wait_ge(S("prm_loaded"), 16)
        for j in range(KD):
            rest(0, j)
            add_square(0, j, j == 0)
        for hh in range(HEADS):
            e.wait_ge(S("grep_made"), hh + 1)
            if hh:
                e.wait_ge(S("grep_stored"), 16 * hh)
            e.tensor_copy(grep[:].rearrange("p (a y) -> p a y", a=2), ps[:, 6:8, 0:GL // 2]
                          ).then_inc(S("grep_copied"), 1)
        factor(0)
        ffn(0, 0)

        e.wait_ge(S("grep_stored"), 16 * HEADS)
        step(e.memset(up[:, :, 0:HIST], 0.0))
        e.memset(vn[:, :, :, P:P + 1], 1.0).then_inc(S("vn_ones"), 1)
        e.wait_ge(S("wgr_ready"), 1)
        e.tensor_tensor(wgl[:], wgraw[:], wgr[:].bitcast(F32), ALU.subtract).then_inc(S("wg_split"), 2)
        for j in range(TM):
            normed(tg[:], 0, done_at("glu", 2 * j))
            normed(tu[:], 1, done_at("glu", 2 * j + 1))
            e.wait_ge(S("glu_sig"), j + 1)
            e.wait_ge(S("tile_evacuated"), evac_at("glu", 2 * j))
            e.tensor_tensor(up[:, j, HIST:], tg[:, 0:SEQ], sg[:, 0:SEQ], ALU.mult).then_inc(S("u_ready"), 1)
            e.tensor_tensor(us[:, j, :, HIST:], tg[:, SEQ:T].rearrange("p (b t) -> p b t", b=NB),
                            sg[:, SEQ:T].rearrange("p (b t) -> p b t", b=NB), ALU.mult
                            ).then_inc(S("u_ready"), 1)
            e.wait_ge(S("u_ready"), 2 * j + 2)

        e.wait_ge(S("gates_done"), 1)
        step(e.tensor_tensor(two(rowa[:]), ps[0:4, 6:8, 0:HALF], two(R[0:4, :]), ALU.mult))
        step(e.tensor_tensor(two(rowt[:]), ps[32:36, 6:8, 0:HALF], two(R[32:36, :]), ALU.mult))
        settle()
        step(e.tensor_scalar(rowa[:], rowa[:], W("gate_b", 0, rows=4), None, ALU.add))
        e.tensor_scalar(rowt[:], rowt[:], W("gate_b", 1, rows=4), None, ALU.add).then_inc(S("row_z"), 1)
        seg = lambda row: row[:, SEQ:T].rearrange("p (b t) -> p b t", t=TB)
        step(e.memset(rowwi[:], 1.0))
        step(e.memset(rowws[:], 0.0))
        settle()
        step(e.memset(seg(rowwi)[:, :, 0:1], 0.0))
        step(e.memset(seg(rowws)[:, :, 0:1], NEG))
        e.wait_ge(S("row_act"), 3)
        e.wait_ge(S("row_z"), 1)
        step(e.scalar_tensor_tensor(rowt[:], rowt[:], 0.0, rowB[:], ALU.min, ALU.subtract))
        settle()
        step(e.tensor_tensor_scan(rowB[:], rowwi[:], rowt[:], 0.0, ALU.mult, ALU.add))
        settle()
        step(e.tensor_tensor(rowa[:], rowa[:], rowB[:], ALU.subtract))
        settle()
        step(e.tensor_copy(rowt[:], rowa[:]))
        settle()
        m0 = W("m0", 0, NB, rows=4).unsqueeze(2)
        step(e.tensor_tensor(seg(rowt)[:, :, 0:1], seg(rowa)[:, :, 0:1], m0, ALU.max))
        settle()
        step(e.tensor_tensor_scan(rowM[:], rowws[:], rowt[:], 0.0, ALU.add, ALU.max))
        settle()
        e.tensor_tensor(rowt[:], rowB[:], rowM[:], ALU.add).then_inc(S("row_m"), 1)
        e.tensor_tensor(seg(rowwi), m0.broadcast_to([4, NB, TB]), seg(rowM), ALU.subtract).then_inc(S("row_m"), 1)
        e.tensor_scalar(rowws[:, 0:SEQ], rowa[:, 0:SEQ], rowM[:, SEQ - 1:SEQ], None, ALU.subtract
                        ).then_inc(S("row_m"), 1)
        e.tensor_tensor(seg(rowws), seg(rowa), seg(rowM)[:, :, TB - 1:TB].broadcast_to([4, NB, TB]),
                        ALU.subtract).then_inc(S("row_m"), 1)

        e.wait_ge(S("hist_loaded"), 16)
        conv_steps = [0]
        accp, accs = ps[:, 6, 0:SEQ], ps[:, 7, 0:SMP].rearrange("p (b t) -> p b t", b=NB)

        def tap(j, k, outp, outs, sem=None, wait=None):
            w = prm[:, bass.ds(k + (POFF["conv_w"] + j * TAPS), 1)]
            if wait is not None:
                e.wait_ge(S("conv_step"), wait)
            inp = up[:, j, bass.ds(k, SEQ)]
            ins_ = us[:, j, :, bass.ds(k, TB)]
            if wait is None:
                a = e.tensor_scalar(outp, inp, w, W("conv_b", j), ALU.mult, ALU.add)
                b = e.tensor_scalar(outs, ins_, w, W("conv_b", j), ALU.mult, ALU.add)
            else:
                a = e.scalar_tensor_tensor(outp, inp, w, accp, ALU.mult, ALU.add)
                b = e.scalar_tensor_tensor(outs, ins_, w, accs, ALU.mult, ALU.add)
            a.then_inc(S("conv_step"), 1)
            b.then_inc(S(sem or "conv_step"), 1)

        def conv_chunk(slot):
            j, q = slot // 4, slot % 4
            k0, k1 = q * 8, min(q * 8 + 8, TAPS - 1)
            base = conv_steps[0]
            if q == 0:
                if j:
                    e.wait_ge(S("conv_done"), j)
                tap(j, 0, accp, accs)
                base += 2
                k0 = 1
            with e.Fori(0, k1 - k0) as i:
                tap(j, i + k0, accp, accs, wait=i * 2 + base)
            base += 2 * (k1 - k0)
            if q == 3:
                tap(j, TAPS - 1, cv[:, j, 0:SEQ], cv[:, j, SEQ:T].rearrange("p (b t) -> p b t", b=NB),
                    sem="conv_done", wait=base)
                base += 1
            conv_steps[0] = base

        for t in range(8):
            if t < 4:
                normed(kT[:, t, :], t % 2, done_at("kv", t), P ** -0.5)
            else:
                normed(vtmp[t - 4][:], t % 2, done_at("kv", t))
            conv_chunk(t)
        for t in range(8):
            if t < 4:
                normed(qT[:, t, :], t % 2, done_at("qo", t))
            else:
                if t > 4:
                    e.wait_ge(S("o_ready"), t - 4)
                normed(tu[:], t % 2, done_at("qo", t))
            conv_chunk(8 + t)
        e.wait_ge(S("cols_turned"), 1)
        for q in range(2):
            o = q * ST * HEADS
            e.tensor_copy(gcol[:, o:o + 16], ps[:, 4, o:o + 16]).then_inc(S("cols_copied"), 1)
            e.tensor_copy(gcol[0:SMP, o + 16:o + 20], ps[0:SMP, 4, o + 16:o + 20]).then_inc(S("cols_copied"), 1)
        e.wait_ge(S("ln_sum"), 1)
        for j in range(TM):
            e.scalar_tensor_tensor(two(cv[:, j, :]), psn, -1.0 / DA, two(cv[:, j, :]), ALU.mult, ALU.add
                                   ).then_inc(S("ln_centered"), 1)
        e.wait_ge(S("ln_root"), 1)
        step(e.reciprocal(acc[:], acc[:]))
        settle()
        for j in range(TM):
            e.tensor_tensor(cv[:, j, :], cv[:, j, :], acc[:], ALU.mult).then_inc(S("ln_scaled"), 1)
        for j in range(TM):
            e.wait_ge(S("mixr_ready"), j + 1)
            e.tensor_tensor(xl[:, j, :], cv[:, j, :], xr[:, j, :].bitcast(F32), ALU.subtract
                            ).then_inc(S("mix_ready"), 1)

        e.wait_ge(S("mix_ready"), TM)
        e.wait_ge(S("cols_copied"), 4)
        for hh in range(HEADS):
            e.wait_ge(S("bcast_ready"), hh + 1)
            step(e.tensor_copy(smp[:, 0:3 * SMP], ps[:, 6, 0:3 * SMP]))
            e.wait_ge(S("C0_loaded"), 16 * (hh + 1))
            qs = qT[:, hh, SEQ:T].rearrange("p (b t) -> p b t", b=NB)
            e.tensor_tensor(smp[:, 3 * SMP:].rearrange("p (b t) -> p b t", b=NB), qs,
                            C0[:, :, P:P + 1].broadcast_to([P, NB, TB]), ALU.mult).then_inc(S("qn_ready"), 1)
            wcol = lambda i, r=P: gcol[0:r, (ST + i) * HEADS + hh:(ST + i) * HEADS + hh + 1]
            for i in range(TM):
                step(e.tensor_scalar(kw[:, i, :], kn[:, i, hh, :], wcol(i), None, ALU.mult))
            step(e.tensor_scalar(wsm[:], C("blk_col", rows=SMP), wcol(TM, SMP), None, ALU.mult))
            settle()
            e.tensor_tensor(kwm[:], kn[0:SMP, TM, hh, :].unsqueeze(1).broadcast_to([SMP, NB, P]),
                            wsm[:].unsqueeze(2).broadcast_to([SMP, NB, P]), ALU.mult).then_inc(S("kw_ready"), 1)

            def gap(i):
                k = ST * hh + i
                if k >= 2:
                    e.wait_ge(S("decay_ready"), k - 1)
                r, w = (P, SEQ - i * P) if i < TM else (SMP, SMP)
                src = ps[:, 0, i * P:SEQ] if i < TM else smp[0:SMP, 0:SMP]
                a = gcol[0:r, i * HEADS + hh:i * HEADS + hh + 1]
                e.tensor_scalar(Xs[0:r, i % 2, 0:w], src, a, 0.0, ALU.subtract, ALU.max
                                ).then_inc(S("gap_ready"), 1)

            def weigh(i):
                k = ST * hh + i
                r, w = (P, SEQ - i * P) if i < TM else (SMP, SMP)
                e.wait_ge(S("decay_ready"), k + 1)
                e.wait_ge(S("s_ready"), k + 1)
                if k >= 2:
                    e.wait_ge(S("pv_done"), k - 1)
                pm = Pm[i % 2]
                step(e.tensor_tensor(pm[0:r, 0:w], ps[0:r, 4 + i % 2, 0:w], Ds[0:r, i % 2, 0:w], ALU.mult))
                settle()
                m = C("cm") if i < TM else C("blk_ml", rows=SMP)
                n = P if i < TM else SMP
                e.tensor_tensor(pm[0:r, 0:n], pm[0:r, 0:n], m, ALU.mult).then_inc(S("p_ready"), 1)

            gap(0)
            for i in range(ST):
                if i + 1 < ST:
                    gap(i + 1)
                weigh(i)
            e.wait_ge(S("em_copied"), hh + 1)
            e.wait_ge(S("pv_done"), ST * (hh + 1))
            e.wait_ge(S("inter_ready"), hh + 1)
            if hh:
                e.wait_ge(S("mixr_ready"), TM + hh)
            o5, wi = 5 * SMP, smp[:, 2 * SMP:3 * SMP]
            step(e.tensor_scalar(tu[:, 0:SEQ], ps[:, 3, 0:SEQ], -1.0, None, ALU.mult))
            step(e.tensor_tensor(tu[:, SEQ:T], ps[:, 6, o5 + SMP:o5 + 2 * SMP], wi, ALU.mult))
            step(e.tensor_tensor(acc[:, SEQ:T], ps[:, 6, o5:o5 + SMP], wi, ALU.mult))
            settle()
            step(e.tensor_tensor(tu[:, 0:SEQ], tu[:, 0:SEQ], ps[:, 3, 0:SEQ], ALU.max))
            step(e.tensor_tensor(tu[:, SEQ:T], tu[:, SEQ:T], ps[:, 6, 4 * SMP:5 * SMP], ALU.add))
            step(e.tensor_tensor(acc[:, SEQ:T], acc[:, SEQ:T], ps[:, 6, 3 * SMP:4 * SMP], ALU.add))
            settle()
            step(e.scalar_tensor_tensor(tu[:, SEQ:T], tu[:, SEQ:T], -1.0, tu[:, SEQ:T], ALU.mult, ALU.max))
            settle()
            step(e.tensor_tensor(tu[:, 0:SEQ], tu[:, 0:SEQ], hd[:, 0:SEQ], ALU.max))
            step(e.tensor_tensor(tu[:, SEQ:T], tu[:, SEQ:T], smp[:, SMP:2 * SMP], ALU.max))
            settle()
            step(e.reciprocal(tu[:], tu[:]))
            settle()
            e.tensor_tensor(acc[:, 0:SEQ], ps[:, 2, 0:SEQ], tu[:, 0:SEQ], ALU.mult).then_inc(S("h_read"), 1)
            step(e.tensor_tensor(acc[:, SEQ:T], acc[:, SEQ:T], tu[:, SEQ:T], ALU.mult))
            settle()
            e.wait_ge(S("h_read"), hh + 1)
            e.wait_ge(S("o_ready"), HEADS)
            e.tensor_tensor(sq[:], acc[:], oT[:, hh, :], ALU.mult).then_inc(S("b_out"), 1)
            e.wait_ge(S("state_ready"), hh + 1)
            if hh:
                e.wait_ge(S("C_stored"), 32 * hh)
            step(e.tensor_copy(Cp[:], ps[:, 7, 0:P + 1]))
            for b in range(NB):
                o = (b % 3) * (P + 1)
                d = smp[:, 2 * SMP + b * TB + TB - 1:2 * SMP + b * TB + TB]
                ins = e.scalar_tensor_tensor(Cn[:, b, :], C0[:, b, :], d, ps[:, b // 3, o:o + P + 1],
                                             ALU.mult, ALU.add)
                if b < NB - 1:
                    step(ins)
            settle()
            ins.then_inc(S("head_done"), 1)
            e.wait_ge(S("mixr_ready"), TM + hh + 1)
            e.wait_ge(S("b_out"), hh + 1)
            e.tensor_tensor(xl[:, TM + hh, :], sq[:], xr[:, TM + hh, :].bitcast(F32), ALU.subtract
                            ).then_inc(S("mix_ready"), 1)

        def rests(m):
            for j in range(KD):
                rest(m, j)

        def out_and_norm(name, m):
            zero_acc(m)
            for j in range(KD):
                e.wait_ge(S("tile_done"), done_at(name, j))
                e.tensor_tensor(two(h[:, j, :]), unit(j % 2), two(h[:, j, :]), ALU.add
                                ).then_inc(S("tile_evacuated"), 1)
                add_square(m, j, False)
            rests(m)
            factor(m)

        out_and_norm(("out", 0), 2)
        ffn(1, 2)

        def ple(l):
            name, m = ("ple", l), 4 * l + 4
            e.wait_ge(S("pr_ready"), l + 1)
            e.tensor_tensor(pl[:], praw[:], pr[:].bitcast(F32), ALU.subtract).then_inc(S("p_split"), 1)
            zero_acc(m)
            for j in range(KD):
                normed(tg[:], 0, done_at(name, 2 * j))
                e.wait_ge(S("ple_sig"), KD * l + j + 1)
                e.wait_ge(S("tile_done"), done_at(name, 2 * j + 1))
                e.tensor_tensor(two(tu[:]), unit(1), two(sg[:]), ALU.mult).then_inc(S("tile_evacuated"), 1)
                e.wait_ge(S("tile_evacuated"), evac_at(name, 2 * j + 1))
                e.tensor_tensor(h[:, j, :], h[:, j, :], tu[:], ALU.add).then_inc(S("ple_added"), 1)
                add_square(m, j, False)
            if l == 0:
                rests(m)
            factor(m)

        ple(0)
        ffn(2, 4)

        lp = W("lam", 0, 256)
        lpv = lp.rearrange("p (a b d) -> p a b d", a=2, b=2)
        step(e.tensor_tensor(lamt[:].rearrange("p (a d) -> p a d", a=2), lpv[:, :, 0, :], lpv[:, :, 1, :], ALU.mult))
        settle()
        e.tensor_reduce(nlam[:, 2:4], lamt[:].rearrange("p (a d) -> p a d", a=2), AX.X, ALU.add
                        ).then_inc(S("lam_sums"), 1)
        e.wait_ge(S("lam_exp"), 1)
        step(e.tensor_tensor(nlam[:, 4:5], nlam[:, 1:2], nlam[:, 0:1], ALU.subtract))
        settle()
        step(e.tensor_scalar(nlam[:, 4:5], nlam[:, 4:5], -LAM_INIT, None, ALU.add))
        settle()
        step(e.scalar_tensor_tensor(nlam[:, 5:6], C("half1"), nlam[:, 4:5], C("half0"), ALU.mult, ALU.add))
        e.wait_ge(S("strip_loaded"), 16 * HEADS * 5)
        for hh in range(HEADS):
            step(e.tensor_tensor(strip[:, hh, SEQ - P:SEQ], strip[:, hh, SEQ - P:SEQ], C("neg_incl"), ALU.add))
        for pair in range(PAIRS):
            step(e.tensor_tensor(sbias[:, pair * SMP:(pair + 1) * SMP].rearrange("p (b t) -> p b t", b=NB),
                                 C("dneg", pair * SMP, (pair + 1) * SMP).rearrange("p (b t) -> p b t", b=NB),
                                 sstrip[:, PAST:PAST + TB].unsqueeze(1).broadcast_to([P, NB, TB]), ALU.add))
        step(e.memset(qbd[:], 0.0))
        for kind in range(2):
            for t in range(8):
                dst = (oq, ok)[t // 4][kind][:, t % 4, :]
                normed(dst, t % 2, done_at(f"qk{kind}", t), 0.125 if t < 4 else None)
            for t in range(4):
                if kind:
                    e.wait_ge(S("turned"), 12)
                    e.wait_ge(S(f"v_stored{t}"), 16)
                normed(vtmp[t][:], t % 2, done_at(f"v{kind}", t))
        N, M = len(DIFF_STEPS), len(SB_STEPS)
        NM = N + M
        for t in range(4):
            e.wait_ge(S(f"v_stored{t}"), 32)
        e.wait_ge(S("turned"), 16)

        def bias_and_max(k, q, parity, buf, w, parts):
            for n, (a, b, src, bias) in enumerate(parts):
                ins = e.tensor_tensor(buf[:, a:b], src, bias, ALU.add)
                if n < len(parts) - 1:
                    step(ins)
            settle()
            ins.then_inc(S("biased"), 1)
            e.wait_ge(S("biased"), k + 1)
            e.tensor_reduce(st(parity, q), buf[:, 0:w], AX.X, ALU.max, negate=True).then_inc(S("maxed"), 1)

        for tick in range(N + 1):
            if tick >= 1:
                u = tick - 1
                w = (DIFF_STEPS[u][1] + 1) * P
                b0, b1 = ((tg, sg), (tu, hd))[u % 2]
                e.wait_ge(S("exped"), 2 * u + 2)
                step(e.reciprocal(tiny[:, 5 * (u % 2) + 2:5 * (u % 2) + 4], tiny[:, 5 * (u % 2) + 2:5 * (u % 2) + 4]))
                settle()
                step(e.tensor_scalar(b0[:, 0:w], b0[:, 0:w], st(u, 2), None, ALU.mult))
                step(e.tensor_scalar(st(u, 3), st(u, 3), nlam[:, 4:5], None, ALU.mult))
                settle()
                e.scalar_tensor_tensor(b0[:, 0:w], b1[:, 0:w], st(u, 3), b0[:, 0:w], ALU.mult, ALU.add
                                       ).then_inc(S("rows_done"), 1)
            if tick < N:
                hh, i = DIFF_STEPS[tick]
                w = (i + 1) * P
                if tick >= 2:
                    e.wait_ge(S("rows_turned"), tick - 1)
                for c in range(2):
                    e.wait_ge(S("scores"), 2 * tick + c + 1)
                    src = ps[:, 2 * (tick % 2) + c, 0:w]
                    bias_and_max(2 * tick + c, c, tick, ((tg, sg), (tu, hd))[tick % 2][c], w,
                                 [(0, w, src, strip[:, hh, SEQ - w:SEQ])])

        e.wait_ge(S("rows_turned"), N)
        for b in (sg, hd):
            step(e.memset(b[:, 0:1], 0.0))

        def sums(k, buf, scan, src, w, a, b, mul, neg):
            e.wait_ge(S("soft_step"), 3 * k + 3)
            step(e.scalar_tensor_tensor(buf[:, 0:w], src, 0.0, buf[:, 0:w], ALU.max, ALU.add))
            settle()
            step(e.tensor_tensor(buf[:, a:b], buf[:, a:b], mul, ALU.mult))
            if k >= 2:
                e.wait_ge(S("rows_done"), rows_before(k - 2))
            settle()
            step(e.tensor_tensor_scan(scan[:, 1:w + 1], ones_row(w), buf[:, 0:w], 0.0, ALU.mult, ALU.add))
            settle()
            step(e.tensor_tensor(buf[:, 0:w], src, scan[:, 0:w], ALU.add))
            step(e.tensor_scalar(st(k, 4), scan[:, w:w + 1], -1.0, None, ALU.mult))
            settle()
            e.tensor_tensor(buf[:, a:b], buf[:, a:b], neg, ALU.add).then_inc(S("summed"), 1)

        def rows_before(k):
            return N + k + 1 + (PAIRS if k >= M else 0)

        def ones_row(w):
            return ones[:, 0:1].broadcast_to([P, w])

        for k in range(M):
            hh, c, i = SB_STEPS[k]
            w = (i + 1) * P
            sums(k, (tg, tu)[k % 2], (sg, hd)[k % 2], ps[:, k % 4, 0:w], w, w - P, w, C("sb_mul"), C("sb_neg"))

        for job in range(2 * PAIRS):
            kind, pair = job // PAIRS, job % PAIRS
            if job:
                e.wait_ge(S("sample_out"), job)
            for b in range(2):
                for c in range(2):
                    src = oq[kind][64 * c:64 * c + 64, :, SEQ + (2 * pair + b) * TB:SEQ + (2 * pair + b + 1) * TB]
                    dst = qbd[64 * c:64 * c + 64, b, :].rearrange("p (h x) -> p h x", x=80)[:, :, c * 8:c * 8 + 8]
                    ins = e.tensor_copy(dst, src)
                    if (b, c) != (1, 1):
                        step(ins)
            settle()
            ins.then_inc(S("qbd_ready"), 1)
            if kind == 0:
                e.wait_ge(S("rows_turned"), NM + pair)
                e.wait_ge(S("scores"), 2 * N + M + pair + 1)
                bias_and_max(2 * N + pair, 0, 0, tg, KEYS,
                             [(0, PAST, ps[:, 0, 0:PAST], sstrip[:, 0:PAST]),
                              (PAST, KEYS, ps[:, 0, PAST:KEYS], sbias[:, pair * SMP:(pair + 1) * SMP])])
                e.wait_ge(S("exped"), 2 * N + pair + 1)
                step(e.reciprocal(st(0, 2), st(0, 2)))
                settle()
                step(e.tensor_tensor(st(0, 2), st(0, 2), nlam[:, 5:6], ALU.mult))
                settle()
                e.tensor_scalar(tg[:, 0:KEYS], tg[:, 0:KEYS], st(0, 2), None, ALU.mult).then_inc(S("rows_done"), 1)
            else:
                k = M + pair
                sums(k, tg, (sg, hd)[k % 2], ps[:, 0, 0:KEYS], KEYS, PAST, KEYS,
                     C("smul", pair * SMP, (pair + 1) * SMP), C("sneg", pair * SMP, (pair + 1) * SMP))
            e.wait_ge(S("sample_out"), job + 1)
            t0 = SEQ + 2 * pair * TB
            if kind == 0:
                ins = e.tensor_copy(oq[0][:, :, t0:t0 + 2 * TB].rearrange("p h (b t) -> p h b t", b=2),
                                    ps[:, 6, 0:64].rearrange("p (b h t) -> p h b t", b=2, h=HEADS))
            else:
                for c in range(2):
                    ins = e.tensor_copy(oq[1][64 * c:64 * c + 64, :, t0:t0 + 2 * TB].rearrange("p h (b t) -> p h b t", b=2),
                                        ps[64 * c:64 * c + 64, 6, 0:128].rearrange("p (b h c t) -> p c h b t", b=2, h=HEADS, c=2)[:, c])
                    if c == 0:
                        step(ins)
                settle()
            ins.then_inc(S("sample_copied"), 1)

        for hh in range(HEADS):
            buf = (tg, tu)[hh % 2]
            e.wait_ge(S("oc_root"), hh + 1)
            if hh == 0:
                e.wait_ge(S("sample_copied"), 2 * PAIRS)
            step(e.reciprocal(buf[:], buf[:]))
            settle()
            step(e.tensor_tensor(oq[0][:, hh, :], oq[0][:, hh, :], buf[:], ALU.mult))
            settle()
            e.tensor_scalar(oq[0][:, hh, :], oq[0][:, hh, :], W("head_g", hh), 1.0 - LAM_INIT, ALU.mult, ALU.mult
                            ).then_inc(S("oc_scaled"), 1)
        for j in range(KD):
            e.wait_ge(S("mixr_ready"), KD + j + 1)
            e.tensor_tensor(xl[:, j, :], oq[j // TM][:, j % TM, :], xr[:, j, :].bitcast(F32), ALU.subtract
                            ).then_inc(S("mix_ready"), 1)
        out_and_norm(("out", 1), 6)
        ffn(3, 6)
        ple(1)
        for j in range(KD):
            g = W("gains", 8 * KD + j)
            e.scalar_tensor_tensor(h[:, j, :], h[:, j, :], g, R[:], ALU.mult, ALU.mult).then_inc(S("y_ready"), 1)

    return ctx


def constants():
    c = np.zeros((P, CW), np.float32)

    def put(name, a):
        c[:a.shape[0], COFF[name]:COFF[name] + a.shape[1]] = a

    p, j = np.arange(P)[:, None], np.arange(P)[None, :]
    put("ident", np.eye(P, dtype=np.float32))
    put("cm", (j >= p).astype(np.float32))
    put("neg_incl", np.where(j > p, NEG, 0.0).astype(np.float32))
    put("sb_mul", (j < p).astype(np.float32))
    put("sb_neg", np.where(j >= p, NEG, 0.0).astype(np.float32))
    s, t = np.arange(SMP)[:, None], np.arange(SMP)[None, :]
    put("blk_ml", ((s // TB == t // TB) & (t >= s)).astype(np.float32))
    put("blk_col", (s // TB == np.arange(NB)[None, :]).astype(np.float32))
    row = np.arange(P)
    b2, tq = row // 64, row % TB
    for pair in range(PAIRS):
        own = t // TB == (2 * pair + b2)[:, None]
        incl = own & (t % TB <= tq[:, None])
        strict = own & (t % TB < tq[:, None])
        o = pair * SMP
        c[:, COFF["dneg"] + o:COFF["dneg"] + o + SMP] = np.where(incl, 0.0, NEG)
        c[:, COFF["smul"] + o:COFF["smul"] + o + SMP] = strict
        c[:, COFF["sneg"] + o:COFF["sneg"] + o + SMP] = np.where(strict, 0.0, NEG)
    head, half = (row % 64) // 16, (row % 16) // 8
    put("fold", ((b2 * 32 + head * 8 + tq)[:, None] == np.arange(64)[None, :]).astype(np.float32))
    put("half0", (half == 0).astype(np.float32)[:, None])
    put("half1", (half == 1).astype(np.float32)[:, None])
    sel = np.zeros((4, 4, P), np.float32)
    for q in range(4):
        sel[q, q] = 1
    put("sel", sel.reshape(4, -1))
    n = np.maximum(SEQ - 1 - np.arange(GL), 0)
    exact = 16
    nf = np.maximum(n, 1).astype(np.float32)
    large = exact + (np.log(nf / exact) / np.float32(np.log(128 / exact)) * (32 - exact)).astype(np.int32)
    bucket = np.where(n < exact, n, np.minimum(large, 31))
    onehot = (bucket[None, :] == np.arange(32)[:, None]).astype(np.float32)
    return c, onehot


def tiles_of(w, nk):
    nj = w.shape[1] // P
    return np.ascontiguousarray(w.reshape(nk, P, nj, P).transpose(2, 1, 0, 3))


def feature_major(a):
    return np.ascontiguousarray(a.reshape(a.shape[0], -1, P).transpose(2, 1, 0))


def by_partition(v):
    return np.ascontiguousarray(v.reshape(-1, P).T)


def kernel(**inputs):
    import concourse.bacc as bacc
    from concourse.bass_utils import run_bass_kernel_spmd

    I = {k: np.asarray(v) for k, v in inputs.items()}
    c, onehot = constants()
    a = {"cst": c, "bone": onehot}
    both = lambda x, y: np.concatenate([x.reshape(SEQ, -1), y.reshape(SMP, -1)], 0)
    a["xT"] = feature_major(both(I["x_prompt"], I["x_sample"]))
    a["pT"] = np.stack([feature_major(both(I["p_prompt"][l], I["p_sample"][l])) for l in range(2)])

    up, d0, d1, ple = [], [], [], []
    for l in range(2):
        for wi, wo in ((I["ffn1_wi"][l], I["ffn1_wo"][l]), (I["ffn2_wi"][l], I["ffn2_wo"][l])):
            t = tiles_of(wi, KD)
            nt = t.shape[0] // 2
            up.append(np.stack([t[:nt], t[nt:]], 2).reshape(nt, P, -1))
            t = tiles_of(wo, DFF // P)
            d0.append(t[:, :, :CHUNKS[0]].reshape(KD, P, -1))
            d1.append(t[:, :, CHUNKS[0]:].reshape(KD, P, -1))
        g, q = tiles_of(I["ple_wg"][l], KD), tiles_of(I["ple_wp"][l], KP)
        ple.append(np.concatenate([g.reshape(KD, P, -1), q.reshape(KD, P, -1)], 2))
    pairs = lambda t: t.reshape(-1, 2, P, KD * P).transpose(0, 2, 1, 3).reshape(-1, P, 2 * KD * P)
    ev = I["ev_w_in"][0]
    t = tiles_of(np.ascontiguousarray(ev[:, :24 * P]), KD)
    val, gate, q, k, v, o = (t[4 * n:4 * n + 4] for n in range(6))
    ev_t = np.concatenate([np.stack([val, gate], 1).reshape(8, *t.shape[1:]), k, v, q, o])
    od_t = tiles_of(I["od_w_in"][0], KD)
    a["up"], a["down0"], a["down1"], a["ple"] = (np.concatenate(x) for x in (up, d0, d1, ple))
    cq, ck, cvv, sq_, sk, sv = (od_t[4 * n:4 * n + 4] for n in range(6))
    a["mixin"] = np.concatenate([pairs(ev_t), pairs(np.concatenate([cq, ck, cvv, sq_, sk, sv]))])
    a["mixout"] = np.concatenate([pairs(tiles_of(I["ev_w_out"][0], KD)), pairs(tiles_of(I["od_w_out"][0], KD))])
    wg = np.zeros((P, KD, 36), np.float32)
    gates = ev[:, 24 * P:].reshape(KD, P, 8).transpose(1, 0, 2)
    wg[:, :, 0:4], wg[:, :, 32:36] = gates[:, :, 0:4], gates[:, :, 4:8]
    a["wg"] = wg

    prm = np.zeros((P, PW), np.float32)

    def put(name, x, at=0):
        prm[:x.shape[0], POFF[name] + at:POFF[name] + at + x.shape[1]] = x

    for l in range(2):
        for n, name in enumerate(("ffn_norm1", "mix_norm", "ffn_norm2", "ple_norm")):
            put("gains", by_partition(I[name][l]), (4 * l + n) * KD)
    put("gains", by_partition(I["final_norm"]), 8 * KD)
    put("conv_w", I["ev_conv_w"][0].reshape(TAPS, TM, P).transpose(2, 1, 0).reshape(P, -1))
    put("conv_b", by_partition(I["ev_conv_b"][0]))
    put("ln_g", by_partition(I["ev_ln_g"][0]))
    put("ln_b", by_partition(I["ev_ln_b"][0]))
    put("gate_b", I["ev_gate_b"][0].reshape(2, 4).T)
    put("head_g", by_partition(I["od_head_g"][0]))
    put("lam", np.broadcast_to(I["od_lambda"][0].reshape(1, 256), (P, 256)))
    put("m0", I["state_mlstm_m"][0].T)
    a["prm"] = prm
    a["hist"] = np.ascontiguousarray(I["state_conv"][0].reshape(NB, HIST, TM, P).transpose(3, 2, 0, 1))
    st = np.concatenate([I["state_mlstm_C"][0], I["state_mlstm_n"][0][..., None]], -1)
    a["C0"] = np.ascontiguousarray(st.transpose(1, 2, 0, 3))
    a["brel"] = np.ascontiguousarray(np.repeat(I["rel_bias"], P, axis=1))
    a["pages"] = I["page_table"].reshape(1, -1)
    for kind, name in enumerate(("diff", "sb")):
        kk = I[f"cache_{name}_k"][0]
        a[f"kc{kind}"] = np.ascontiguousarray(kk.reshape(-1, PAGE, HEADS, P).transpose(0, 3, 2, 1))
        a[f"vc{kind}"] = np.ascontiguousarray(I[f"cache_{name}_v"][0].reshape(-1, PAGE, DA))

    nc = bacc.Bacc("TRN2", target_bir_lowering=False, num_devices=1, dynamic_dma_scratch_size=1024)
    A = {n: nc.dram_tensor(f"in_{n}", x.shape, mybir.dt.from_np(x.dtype), kind="ExternalInput").ap()
         for n, x in a.items()}
    outs = dict(yT=(P, KD, T), conv_p=(P, TM, HIST), conv_s=(P, TM, NB, HIST), Cp=(HEADS, P, P + 1),
                Cs=(HEADS, P, NB, P + 1), mrow=(HEADS, T), dk=(P, TM, T), dv=(P, TM, T), sk=(P, TM, T), sv=(P, TM, T))
    for n, shape in outs.items():
        A[n] = nc.dram_tensor(f"out_{n}", shape, F32, kind="ExternalOutput").ap()
    A["scratch"] = nc.dram_tensor("scratch", (HEADS, P * GL), F32, kind="Internal").ap()
    build(nc, A).close()
    r = run_bass_kernel_spmd(nc, [{f"in_{n}": x for n, x in a.items()}], core_ids=[0]).results[0]
    O = {n: r[f"out_{n}"] for n in outs}

    def token_major(x):
        t = x.transpose(2, 1, 0).reshape(T, -1)
        return t[:SEQ], t[SEQ:]

    yp, ys = token_major(O["yT"])
    res = [yp.reshape(1, SEQ, D), ys.reshape(NB, TB, D)]
    res.append(O["conv_p"].transpose(2, 1, 0).reshape(1, 1, HIST, DA))
    res.append(O["conv_s"].transpose(2, 3, 1, 0).reshape(1, NB, HIST, DA))
    cs = O["Cs"].transpose(2, 0, 1, 3)
    res += [O["Cp"][None, None, :, :, :P], cs[None, ..., :P], O["Cp"][None, None, :, :, P], cs[None, ..., P]]
    res += [O["mrow"][:, SEQ - 1].reshape(1, 1, HEADS), O["mrow"][:, SEQ + TB - 1::TB].T[None]]
    for n, sh in (("dk", (HEADS, P)), ("dv", (HEADS, P)), ("sk", (8, 64)), ("sv", (8, 64))):
        kp, ks = token_major(O[n])
        res += [kp.reshape(1, 1, SEQ, *sh), ks.reshape(1, NB, TB, *sh)]
    return tuple(np.ascontiguousarray(x) for x in res)
```

```python
from contextlib import ExitStack

import numpy as np
import concourse.bass as bass
from concourse import mybir

F32 = mybir.dt.float32
F32R = mybir.dt.float32r
I32 = mybir.dt.int32
ALU = mybir.AluOpType
ACT = mybir.ActivationFunctionType
AX = mybir.AxisListType

P = 128
D = 1024
SEQ = 512
NB, TB = 8, 8
SMP = NB * TB
T = SEQ + SMP
HALF = T // 2
KD = D // P
DFF = 2816
CHUNKS = (12, 10)
assert sum(CHUNKS) * P == DFF
HIST = 30
TAPS = 31
HEADS = 4
DA = 512
TM = DA // P
PAST, PAGE = 256, 128
NPG = PAST // PAGE
PLE = 256
KP = PLE // P
KEYS = PAST + SMP
PAIRS = NB // 2
GL = 640
NEG = -1e30
LAM_INIT = 0.8 - 0.6 * float(np.exp(-0.3))
ST = T // P + 1
BLK = 2048

CONST = dict(ident=128, cm=128, neg_incl=128, sb_neg=128, blk_ml=64, blk_col=8,
             dneg=4 * 64, sneg=4 * 64, fold=64, half0=1, half1=1,
             sel=4 * 128)
COFF = {}
_o = 0
for _n, _w in CONST.items():
    COFF[_n] = _o
    _o += _w
CW = _o
PARAM = dict(gains=9 * KD, conv_w=TM * TAPS, conv_b=TM, ln_g=TM, ln_b=TM, gate_b=2, head_g=TM,
             lam=256, m0=8)
POFF = {}
_o = 0
for _n, _w in PARAM.items():
    POFF[_n] = _o
    _o += _w
PW = _o


class Phase:
    blocks = tiles = 0

    def __init__(self, src, at, nb, ks):
        self.src, self.at, self.nb, self.ks = src, at, nb, ks
        self.width = sum(ks) * P
        self.n0, self.t0, self.T = Phase.blocks, Phase.tiles, len(ks)
        Phase.blocks += nb
        Phase.tiles += nb * len(ks)
        assert nb % 2 == 0 and (nb * len(ks)) % 2 == 0 and self.width <= BLK


def schedule():
    Phase.blocks = Phase.tiles = 0
    ph = {}
    order = []

    def add(name, *a):
        ph[name] = Phase(*a)
        order.append(name)

    def ffn(n):
        at = 0
        for c, k in enumerate(CHUNKS):
            add(("up", n, c), "up", n * sum(CHUNKS) + at, k, (KD, KD))
            at += k
            add(("down", n, c), f"down{c}", n * KD, KD, (k,))

    for l in range(2):
        ffn(2 * l)
        if l == 0:
            add("glu", "mixin", 0, 4, (KD, KD))
            add("kv", "mixin", 4, 4, (KD, KD))
            add("qo", "mixin", 8, 4, (KD, KD))
        else:
            add("qk0", "mixin", 12, 4, (KD, KD))
            add("v0", "mixin", 16, 2, (KD, KD))
            add("qk1", "mixin", 18, 4, (KD, KD))
            add("v1", "mixin", 22, 2, (KD, KD))
        add(("out", l), "mixout", l * 4, 4, (KD, KD))
        ffn(2 * l + 1)
        add(("ple", l), "ple", l * KD, KD, (KD, KP))
    return ph, order


def build(nc, A):
    ph, order = schedule()
    ctx = ExitStack()
    sems = {}

    def S(name):
        if name not in sems:
            sems[name] = ctx.enter_context(nc.semaphore(name))
        return sems[name]

    top = [(nc.sbuf_base + 31) // 32 * 32]
    END = nc.sbuf_base + nc.sbuf_bytes_remaining

    def sb(name, shape, dt=F32, at=None):
        size = (int(np.prod(shape[1:])) * 4 + 31) // 32 * 32
        if at is None:
            a = top[0]
            top[0] += size
        else:
            a = at[0]
            at[0] += size
        assert a + size <= END, (name, a + size - END)
        return nc.alloc_sbuf_tensor_at(name, shape, dt, offset=a)

    h = sb("h", [P, KD, T])
    XR_AT = top[0]
    xr = sb("xr", [P, KD, T], F32R)
    xl = sb("xl", [P, KD, T], F32R)
    raw = [sb(f"raw{s}", [P, BLK]) for s in range(2)]
    wr, wl, W_AT = [], [], []
    for s in range(2):
        W_AT.append(top[0])
        wr.append(sb(f"wr{s}", [P, BLK], F32R))
        wl.append(sb(f"wl{s}", [P, BLK], F32R))
    R = sb("R", [P, T])
    tg, sg, tu, hd, sq, acc = (sb(n, [P, T]) for n in ("tg", "sg", "tu", "hd", "sq", "acc"))
    cst = sb("cst", [P, CW])
    prm = sb("prm", [P, PW])
    ones = sb("ones", [P, P])
    eps6 = sb("eps6", [P, 1])
    eps5 = sb("eps5", [P, 1])
    pages = sb("pages", [1, NB * NPG], I32)
    tiny = sb("tiny", [P, 64])
    ZONE = top[0]
    vtmp = [hd, sq, tg, sg]

    z = [ZONE]
    hr = sb("hr", [P, max(CHUNKS), T], F32R, at=z)
    hl = sb("hl", [P, max(CHUNKS), T], F32R, at=z)
    brel = sb("brel", [32, HEADS * P], at=z)
    bone = sb("bone", [32, GL], at=z)
    grep = sb("grep", [P, GL], at=z)
    z = [ZONE]
    praw = sb("praw", [P, KP, T], at=z)
    pr = sb("pr", [P, KP, T], F32R, at=z)
    pl = sb("pl", [P, KP, T], F32R, at=z)
    z = [ZONE]
    up = sb("up", [P, TM, HIST + SEQ], at=z)
    us = sb("us", [P, TM, NB, HIST + TB], at=z)
    z2 = [ZONE]
    C0 = sb("C0", [P, NB, P + 1], at=z2)
    Cn = sb("Cn", [P, NB, P + 1], at=z2)
    Cp = sb("Cp", [P, P + 1], at=z2)
    kw = sb("kw", [P, TM, P], at=z2)
    assert z2[0] <= z[0]
    cv = sb("cv", [P, TM, T], at=z)
    z3 = [z[0] - TM * T * 4]
    Xs = sb("Xs", [P, 2, SEQ], at=z3)
    Ds = sb("Ds", [P, 2, SEQ], at=z3)
    assert z3[0] <= z[0]
    qT = sb("qT", [P, HEADS, T], at=z)
    kT = sb("kT", [P, HEADS, T], at=z)
    oT = sb("oT", [P, HEADS, T], at=z)
    kn = sb("kn", [P, ST, HEADS, P], at=z)
    vn = sb("vn", [P, ST, HEADS, P + 1], at=z)
    rowt, rowB, rowa, rowM, rowem, rowwi, rowws = (
        sb(n, [HEADS, T], at=z) for n in ("rowt", "rowB", "rowa", "rowM", "rowem", "rowwi", "rowws"))
    gcol = sb("gcol", [P, 2 * ST * HEADS], at=z)
    wgraw = sb("wgraw", [P, KD, 36], at=z)
    wgr = sb("wgr", [P, KD, 36], F32R, at=z)
    wgl = sb("wgl", [P, KD, 36], F32R, at=z)
    kwm = sb("kwm", [SMP, NB, P], at=z)
    smp = sb("smp", [P, 4 * SMP], at=z)
    wsm = sb("wsm", [SMP, NB], at=z)
    ENDS = [z[0]]
    Pm = [tg, sg]
    z = [ZONE]
    oq = [sb(f"oq{i}", [P, TM, T], at=z) for i in range(2)]
    ok = [sb(f"ok{i}", [P, TM, T], at=z) for i in range(2)]
    ov = [sb(f"ov{i}", [P, ST, DA], at=z) for i in range(2)]
    strip = sb("strip", [P, HEADS, SEQ], at=z)
    sstrip = sb("sstrip", [P, PAST + TB], at=z)
    sbias = sb("sbias", [P, PAIRS * SMP], at=z)
    kc = [sb("kc0", [P, 2, HEADS, NPG, PAGE], at=z),
          nc.alloc_sbuf_tensor_at("kc1", [P, 2, HEADS, NPG, PAGE], F32, offset=XR_AT)]
    vc = [sb("vc0", [P, 2, NPG, DA], at=z),
          nc.alloc_sbuf_tensor_at("vc1", [P, 2, NPG, DA], F32, offset=XR_AT + KD * T * 4)]
    qbd = sb("qbd", [P, 2, 5 * 64], at=z)
    rows, rowsT = ([nc.alloc_sbuf_tensor_at(f"{n}{k}", [P, SEQ], F32, offset=W_AT[1] + (q * 4 + k) * SEQ * 4)
                    for k in range(4)] for q, n in enumerate(("rows", "rowsT")))
    assert 4 * SEQ <= BLK
    rows2 = [tg, sg, tu, hd]
    srow = sq
    nlam = sb("nlam", [P, 8], at=z)
    lamt = sb("lamt", [P, 128], at=z)
    ENDS.append(z[0])
    assert max(ENDS) <= END, ("zone", [END - x for x in ENDS])

    ps = ctx.enter_context(nc.psum_tensor("ps", [P, 8, 512], F32))

    def unit(u):
        return ps[:, 2 * u:2 * u + 2, 0:HALF]

    def two(ap):
        return ap.rearrange("p (a t) -> p a t", a=2)

    psn = ps[:, 4:6, 0:HALF]

    def C(name, a=0, b=None, rows=P):
        o = COFF[name]
        return cst[0:rows, o + a:o + (CONST[name] if b is None else b)]

    def W(name, a, b=None, rows=P):
        o = POFF[name]
        return prm[0:rows, o + a:o + (a + 1 if b is None else b)]

    scratch = A["scratch"]

    CR_TILE = 1
    CR_EVAC = 2

    def done_at(p, t):
        return ph[p].t0 + t + 1 + CR_TILE

    def evac_at(p, t):
        return ph[p].t0 + t + 1 + CR_EVAC

    TOTAL_U = sum(CHUNKS)

    def st(k, q):
        o = 5 * (k % 4) + q
        return tiny[:, o:o + 1]

    SAMPLES = TM
    MAPS = [(0, hh, 0, i) for hh in range(HEADS) for i in (0, SAMPLES, 1, 2, 3)]
    N = len(MAPS)
    MAPS += [(1, hh, c, i) for hh in range(HEADS)
             for i, c in ((0, 0), (0, 1), (SAMPLES, 0), (1, 0), (1, 1), (2, 0), (2, 1), (3, 0), (3, 1))]
    NM = len(MAPS)
    SAMPLE_AT = [u for u, m in enumerate(MAPS) if m[3] == SAMPLES]

    def width(u):
        i = MAPS[u][3]
        return KEYS if i == SAMPLES else (i + 1) * P

    def softmaxes(u):
        return sum(1 if m[3] == SAMPLES else 2 for m in MAPS[:min(u, N)])

    def score_count(u):
        return softmaxes(u) + max(u - N, 0)

    def score_bank(u, c):
        return 2 * (u % 2) + (c if u < N else u // 2 % 2)

    def out_bank(u):
        kind, hh, c, i = MAPS[u]
        return 6 + (hh + (i == SAMPLES)) % 2

    def rows_done(u):
        return (S("probs_done"), u + 1) if u < N else (S("weights_done"), u - N + 1)

    def rowsT_copied(u):
        return (S("probsT_copied"), u + 1) if u < N else (S("weightsT_copied"), u - N + 1)

    def copy_rowsT(e, u):
        e.wait_ge(S("rows_turned"), u + 1)
        if u >= 4:
            e.wait_ge(S("values_done"), u - 3)
        dst, b = rowsT[u % 4], 4 + u % 2
        copy = (lambda o, i: e.activation(o, i, ACT.Copy)) if u < N else e.tensor_copy
        w = width(u)
        if MAPS[u][3] == SAMPLES:
            pitch = P if u >= N else 64
            w = NPG * pitch
            copy(dst[0:SMP, w:w + pitch], ps[0:SMP, b, w:w + pitch]).then_inc(S("rowsT_part"), 1)
            e.wait_ge(S("rowsT_part"), SAMPLE_AT.index(u) + 1)
        copy(dst[:, 0:w], ps[:, b, 0:w]).then_inc(rowsT_copied(u)[0], 1)

    block = ctx.enter_context(nc.Block())

    @block.sync
    def _(e):
        e.dma_start(h[:], A["xT"]).then_inc(S("h_loaded"), 16)
        e.dma_start(prm[:], A["prm"]).then_inc(S("prm_loaded"), 16)
        e.dma_start(cst[:], A["cst"]).then_inc(S("cst_loaded"), 16)
        e.dma_start(pages[:], A["pages"]).then_inc(S("pages_loaded"), 16)
        for name in order:
            p = ph[name]
            with e.Fori(0, p.nb // 2) as i:
                for s in range(2):
                    e.wait_ge(S(f"w_split{s}"), i + (p.n0 // 2 + 1))
                    e.dma_start(raw[s][:, 0:p.width],
                                A[p.src][bass.ds(i * 2 + (p.at + s), 1)].rearrange("a p w -> p (a w)")
                                ).then_inc(S(f"raw_loaded{s}"), 16)

    @block.gpsimd
    def _(e):
        for s in range(2):
            e.memset(raw[s][:], 0.0).then_inc(S(f"w_split{s}"), 1)
        for name in order:
            p = ph[name]
            with e.Fori(0, p.nb // 2) as i:
                for s in range(2):
                    e.wait_ge(S("w_rounded"), i * 2 + (p.n0 + s + 1))
                    e.tensor_tensor(wl[s][:, 0:p.width], raw[s][:, 0:p.width],
                                    wr[s][:, 0:p.width].bitcast(F32), ALU.subtract
                                    ).then_inc(S(f"w_split{s}"), 1)

    @block.tensor
    def _(e):
        e.nop().then_inc(S("tile_done"), CR_TILE)

        def mm3(out, wrt, wlt, xrt, xlt, first, last):
            e.matmul(out, wrt, xrt, start=first, stop=False)
            e.matmul(out, wrt, xlt, start=False, stop=False)
            return e.matmul(out, wlt, xrt, start=False, stop=last)

        def gemm(name, rhs, ready):
            p = ph[name]
            with e.Fori(0, p.nb // 2) as i:
                for s in range(2):
                    e.wait_ge(S(f"w_split{s}"), i + (p.n0 // 2 + 2))
                    off = 0
                    for tile, kn_ in enumerate(p.ks):
                        t = s * p.T + tile
                        u = t % 2
                        e.wait_ge(S("tile_evacuated"), i * (2 * p.T) + (p.t0 + t - 2 + 1 + CR_EVAC))
                        for k in range(kn_):
                            need = ready(tile, k) if s == 0 else None
                            if need:
                                e.wait_ge(S(need[0]), need[1])
                            a, b = off + k * P, off + (k + 1) * P
                            r, q = rhs(tile, k)
                            for hf in range(2):
                                x0, x1 = hf * HALF, (hf + 1) * HALF
                                mm = mm3(ps[:, 2 * u + hf, 0:HALF], wr[s][:, a:b], wl[s][:, a:b],
                                         r[:, x0:x1], q[:, x0:x1], k == 0, k == kn_ - 1)
                        off += kn_ * P
                        mm.then_inc(S("tile_done"), 1)

        def xin(tile, k):
            return xr[:, k, :], xl[:, k, :]

        def norm_sum(m):
            e.wait_ge(S("acc_done"), KD * (m + 1))
            if m:
                e.wait_ge(S("root_ready"), m)
            for hf in range(2):
                mm = e.matmul(ps[:, 4 + hf, 0:HALF], ones[:], acc[:, hf * HALF:(hf + 1) * HALF],
                              start=True, stop=True)
            mm.then_inc(S("ss_ready"), 1)

        def x_of(m):
            return lambda tile, k: ("x_ready", KD * m + k + 1) if tile == 0 else None

        no_wait = lambda tile, k: None

        def ffn(n, m):
            hid = n * TOTAL_U
            for c, kc_ in enumerate(CHUNKS):
                gemm(("up", n, c), xin, x_of(m) if c == 0 else no_wait)
                hid += kc_
                gemm(("down", n, c), lambda tile, k: (hr[:, k, :], hl[:, k, :]),
                     lambda tile, k, hid=hid, kc_=kc_: {0: ("hidden_ready", hid - 1),
                                                        kc_ - 1: ("hidden_ready", hid)}.get(k))

        e.wait_ge(S("ones_ready"), 3)
        e.wait_ge(S("bias_loaded"), 32)
        for hh in range(HEADS):
            if hh:
                e.wait_ge(S("grep_copied"), hh)
            for hf in range(2):
                mm = e.matmul(ps[:, 6 + hf, 0:GL // 2], brel[:, hh * P:(hh + 1) * P],
                              bone[:, hf * (GL // 2):(hf + 1) * (GL // 2)], start=True, stop=True)
            mm.then_inc(S("grep_made"), 1)

        norm_sum(0)
        ffn(0, 0)
        norm_sum(1)

        gemm("glu", xin, x_of(1))
        e.wait_ge(S("wg_split"), 2)
        for hf in range(2):
            for k in range(KD):
                mm = mm3(ps[0:36, 6 + hf, 0:HALF], wgr[:, k, :], wgl[:, k, :],
                         xr[:, k, hf * HALF:(hf + 1) * HALF], xl[:, k, hf * HALF:(hf + 1) * HALF],
                         k == 0, k == KD - 1)
        mm.then_inc(S("gates_done"), 1)
        gemm("kv", xin, no_wait)

        def turn(src, phase, t, n):
            e.wait_ge(S("tile_evacuated"), evac_at(phase, t))
            if n:
                e.wait_ge(S("turned_copied"), 2 * n)
            else:
                e.wait_ge(S("root_ready"), 2)
            for i in range(ST):
                w = P if i < ST - 1 else SMP
                mm = e.transpose(ps[0:w, 4 + i // 4, (i % 4) * P:(i % 4 + 1) * P],
                                 src[:, i * P:i * P + w], C("ident"))
            mm.then_inc(S("turned"), 1)

        for n in range(8):
            turn(kT[:, n, :] if n < 4 else vtmp[n - 4][:], "kv", n, n)
        e.wait_ge(S("rows_exp"), 3)
        e.wait_ge(S("turned_copied"), 16)
        for q, row in enumerate((rowa, rowws)):
            for i in range(ST):
                w = P if i < ST - 1 else SMP
                o = (q * ST + i) * HEADS
                mm = e.transpose(ps[0:w, 4, o:o + HEADS], row[:, i * P:i * P + w],
                                 C("ident", 0, 4, rows=4))
        mm.then_inc(S("cols_turned"), 1)
        gemm("qo", xin, no_wait)

        e.wait_ge(S("conv_done"), TM)
        e.wait_ge(S("cols_copied"), 4)
        for j in range(TM):
            for hf in range(2):
                mm = e.matmul(ps[:, 4 + hf, 0:HALF], ones[:], cv[:, j, hf * HALF:(hf + 1) * HALF],
                              start=j == 0, stop=j == TM - 1)
        mm.then_inc(S("ln_sum"), 1)
        for j in range(TM):
            e.wait_ge(S("ln_sq"), j + 1)
            if j == 0:
                e.wait_ge(S("ln_centered"), TM)
            for hf in range(2):
                mm = e.matmul(ps[:, 4 + hf, 0:HALF], ones[:], (hd, sq)[j % 2][:, hf * HALF:(hf + 1) * HALF],
                              start=j == 0, stop=j == TM - 1)
            mm.then_inc(S("ln_var"), 1)

        e.wait_ge(S("tile_evacuated"), evac_at("qo", 7))
        e.wait_ge(S("ln_root"), 1)
        e.wait_ge(S("vn_ones"), 1)
        for hh in range(HEADS):
            if hh:
                e.wait_ge(S("head_done"), hh)
            sel = C("sel", hh * P, (hh + 1) * P, rows=4)
            e.matmul(ps[:, 0, 0:SEQ], sel, rowM[:, 0:SEQ], start=True, stop=True)
            e.matmul(ps[:, 1, 0:SEQ], sel, rowem[:, 0:SEQ], start=True, stop=True)
            for q, row in enumerate((rowM, rowem, rowwi)):
                mm = e.matmul(ps[:, 6, SMP * q:SMP * (q + 1)], sel, row[:, SEQ:T], start=True, stop=True)
            mm.then_inc(S("bcast_ready"), 1)
            q_, k_ = qT[:, hh, :], kT[:, hh, :]

            def scores(i):
                w = P if i < ST - 1 else SMP
                n0 = i * P
                n1 = SEQ if i < ST - 1 else T
                if i >= 2:
                    e.wait_ge(S("p_ready"), ST * hh + i - 1)
                e.matmul(ps[0:w, 4 + i % 2, 0:n1 - n0], k_[:, n0:n0 + w], q_[:, n0:n1],
                         start=True, stop=True).then_inc(S("s_ready"), 1)

            def values(i):
                n0 = i * P
                e.wait_ge(S("p_ready"), ST * hh + i + 1)
                if i < ST - 1:
                    e.matmul(ps[:, 2, n0:SEQ], vn[:, i, hh, 0:P], Pm[i % 2][:, 0:SEQ - n0],
                             start=i == 0, stop=i == ST - 2)
                    e.matmul(ps[:, 3, n0:SEQ], ones[:], Pm[i % 2][:, 0:SEQ - n0],
                             start=i == 0, stop=i == ST - 2).then_inc(S("pv_done"), 1)
                else:
                    o = 3 * SMP
                    e.matmul(ps[:, 6, o:o + SMP], vn[0:SMP, i, hh, 0:P], Pm[i % 2][0:SMP, 0:SMP],
                             start=True, stop=True)
                    e.matmul(ps[:, 6, o + SMP:o + 2 * SMP], ones[0:SMP, :], Pm[i % 2][0:SMP, 0:SMP],
                             start=True, stop=True).then_inc(S("pv_done"), 1)

            scores(0)
            scores(1)
            for i in range(ST):
                values(i)
                if i + 2 < ST:
                    scores(i + 2)
            e.wait_ge(S("qn_ready"), hh + 1)
            for b in range(NB):
                o = 5 * SMP + b * TB
                e.matmul(ps[:, 6, o:o + TB], C0[:, b, 0:P], q_[:, SEQ + b * TB:SEQ + (b + 1) * TB],
                         start=True, stop=True)
            e.matmul(ps[:, 6, 6 * SMP:7 * SMP], ones[:], smp[:, 3 * SMP:4 * SMP], start=True, stop=True
                     ).then_inc(S("inter_ready"), 1)
            e.wait_ge(S("kw_ready"), hh + 1)
            for i in range(TM):
                mm = e.matmul(ps[:, 7, 0:P + 1], kw[:, i, :], vn[:, i, hh, :], start=i == 0, stop=i == TM - 1)
            e.wait_ge(S("h_read"), hh + 1)
            for b in range(NB):
                o = (b % 3) * (P + 1)
                mm = e.matmul(ps[:, b // 3, o:o + P + 1], kwm[:, b, :], vn[0:SMP, ST - 1, hh, :],
                              start=True, stop=True)
            mm.then_inc(S("state_ready"), 1)

        e.wait_ge(S("head_done"), HEADS)
        gemm(("out", 0), xin, lambda tile, k: ("mix_ready", k + 1) if tile == 0 else None)
        norm_sum(2)
        ffn(1, 2)
        norm_sum(3)

        def ple(l):
            gemm(("ple", l), lambda tile, k: (xr[:, k, :], xl[:, k, :]) if tile == 0
                 else (pr[:, k, :], pl[:, k, :]),
                 lambda tile, k: ("x_ready", KD * (4 * l + 3) + k + 1) if tile == 0 else ("p_split", l + 1))

        ple(0)
        norm_sum(4)
        ffn(2, 4)
        norm_sum(5)

        gemm("qk0", xin, x_of(5))
        gemm("v0", xin, no_wait)
        e.wait_ge(S("root_ready"), 6)
        for n in range(4):
            turn(vtmp[n][:], "v0", n, 8 + n)
        gemm("qk1", xin, no_wait)
        gemm("v1", xin, no_wait)
        for n in range(4):
            turn(vtmp[n][:], "v1", n, 12 + n)
        e.wait_ge(S("turned_copied"), 32)
        e.wait_ge(S("tile_evacuated"), evac_at("v1", 3))

        def turn_rows(u, src, w, other=None):
            e.wait_ge(*rows_done(u))
            if u >= 2:
                e.wait_ge(*rowsT_copied(u - 2))
            nblk = (w + P - 1) // P
            for b in range(nblk):
                wb = min(P, w - b * P)
                if other is None:
                    mm = e.transpose(ps[0:wb, 4 + u % 2, b * P:(b + 1) * P], src[:, b * P:b * P + wb], C("ident"))
                else:
                    mm = e.matmul(ps[0:wb, 4 + u % 2, b * 64:(b + 1) * 64], src[:, b * P:b * P + wb], other,
                                  start=True, stop=True)
            mm.then_inc(S("rows_turned"), 1)

        for tick in range(NM + 5):
            if tick < NM:
                u = tick
                kind, hh, c, i = MAPS[u]
                w = width(u)
                if i == SAMPLES:
                    job = kind * PAIRS + hh
                    e.wait_ge(S("qbd_ready"), job + 1)
                    e.wait_ge(S(f"keys_loaded{job % 2}"), 16 * 2 * NPG * (job // 2 + 1))
                if u >= N + 4:
                    e.wait_ge(S("summed"), u - 4 - N + 1)
                elif u >= 2:
                    e.wait_ge(S("biased"), softmaxes(min(u - 1, N)))
                if i == SAMPLES:
                    bank = score_bank(u, 0)
                    for b in range(2):
                        r = slice(64 * b, 64 * b + 64)
                        for hh_ in range(HEADS):
                            e.matmul(ps[r, bank, 0:PAST], qbd[:, b, hh_ * 64:(hh_ + 1) * 64],
                                     kc[job % 2][:, b, hh_, :, :].rearrange("p g s -> p (g s)"),
                                     start=hh_ == 0, stop=hh_ == HEADS - 1)
                        if kind:
                            e.matmul(ps[r, bank, PAST:KEYS], C("ident")[:, r], C("sneg", hh * SMP, (hh + 1) * SMP),
                                     start=True, stop=False)
                        for hh_ in range(HEADS):
                            mm = e.matmul(ps[r, bank, PAST:KEYS], qbd[:, b, hh_ * 64:(hh_ + 1) * 64],
                                          ok[kind][:, hh_, SEQ:T], start=hh_ == 0 and kind == 0,
                                          stop=hh_ == HEADS - 1)
                    mm.then_inc(S("scores"), 1)
                else:
                    for c_ in range(2) if kind == 0 else (c,):
                        r, bank = slice(64 * c_, 64 * c_ + 64), score_bank(u, c_)
                        q_ = oq[kind][r, hh, i * P:(i + 1) * P]
                        if kind == 0:
                            mm = e.matmul(ps[:, bank, 0:w], q_, ok[kind][r, hh, 0:w], start=True, stop=True)
                        else:
                            if i:
                                e.matmul(ps[:, bank, 0:w - P], q_, ok[kind][r, hh, 0:w - P], start=True, stop=True)
                            e.matmul(ps[:, bank, w - P:w], C("ident"), C("sb_neg"), start=True, stop=False)
                            mm = e.matmul(ps[:, bank, w - P:w], q_, ok[kind][r, hh, w - P:w], start=False, stop=True)
                        mm.then_inc(S("scores"), 1)
            if 3 <= tick < NM + 3:
                u = tick - 3
                turn_rows(u, rows[u % 4], width(u),
                          C("fold") if u < N and MAPS[u][3] == SAMPLES else None)
            if 4 <= tick < NM + 4:
                u = tick - 4
                kind, hh, c, i = MAPS[u]
                bank, rt = out_bank(u), rowsT[u % 4]
                e.wait_ge(*rowsT_copied(u))
                if i == SAMPLES:
                    job = kind * PAIRS + hh
                    e.wait_ge(S(f"values_loaded{job % 2}"), 16 * 2 * NPG * (job // 2 + 1))
                    if job:
                        e.wait_ge(S("attn_copied"), job)
                    n, pitch = (64, P) if kind else (32, 64)
                    for b in range(2):
                        for g in range(NPG + 1):
                            r = P if g < NPG else SMP
                            o = g * pitch + b * n
                            mm = e.matmul(ps[b * n:(b + 1) * n, bank, :], rt[0:r, o:o + n],
                                          vc[job % 2][:, b, g, :] if g < NPG else ov[kind][0:SMP, ST - 1, :],
                                          start=g == 0, stop=g == NPG)
                else:
                    if i == 0 and c == 0 and kind * HEADS + hh:
                        e.wait_ge(S("sample_copied"), kind * HEADS + hh)
                    f, r = ((slice(hh * P, (hh + 1) * P), slice(0, P)) if kind == 0 else
                               (slice((2 * hh + c) * 64, (2 * hh + c + 1) * 64), slice(64 * c, 64 * c + 64)))
                    for b in range(i + 1):
                        mm = e.matmul(ps[r, bank, i * P:(i + 1) * P], ov[kind][:, b, f],
                                      rt[:, b * P:(b + 1) * P], start=b == 0, stop=b == i)
                mm.then_inc(S("values_done"), 1)
            if tick - 6 in SAMPLE_AT:
                u = tick - 6
                kind, pair = MAPS[u][0:2]
                n = 64 if kind else 32
                e.wait_ge(S("sample_rows"), SAMPLE_AT.index(u) + 1)
                for hh in range(HEADS):
                    pick = C("ident", 0, 2 * n, rows=2 * n).rearrange("p (b h x) -> p h b x", b=2, h=HEADS)[:, hh]
                    mm = e.matmul(ps[:, out_bank(u), hh * n // 2:(hh + 1) * n // 2],
                                  srow[0:2 * n, hh * P:(hh + 1) * P], pick, start=True, stop=True)
                mm.then_inc(S("sample_turned"), 1)

        for hh in range(HEADS):
            e.wait_ge(S("oc_sq"), hh + 1)
            if hh:
                e.wait_ge(S("oc_root"), hh)
            for hf in range(2):
                mm = e.matmul(ps[:, 4 + hf, 0:HALF], ones[:], (sg, hd)[hh % 2][:, hf * HALF:(hf + 1) * HALF],
                              start=True, stop=True)
            mm.then_inc(S("oc_ss"), 1)
        e.wait_ge(S("oc_root"), HEADS)
        gemm(("out", 1), xin, lambda tile, k: ("mix_ready", KD + k + 1) if tile == 0 else None)
        norm_sum(6)
        ffn(3, 6)
        norm_sum(7)
        ple(1)
        norm_sum(8)

    @block.scalar
    def _(e):
        def width_after(name):
            at = order.index(name) + 1
            return ph[order[at]].width if at < len(order) else 0

        def round_block(name, i, s, first=False):
            p = ph[name]
            if first:
                k, slot = p.n0 // 2 + 1, 0
                e.wait_ge(S("raw_loaded0"), 16 * k)
                w = p.width
            else:
                slot = 1 - s
                e.wait_ge(S(f"raw_loaded{slot}"), i * 16 + 16 * (p.n0 // 2 + 1 + s))
                e.wait_ge(S("tile_done"), i * (2 * p.T) + (p.t0 + p.T * s + CR_TILE))
                w = max(p.width, width_after(name)) if s == 1 else p.width
            e.activation(wr[slot][:, 0:w], raw[slot][:, 0:w], ACT.Copy).then_inc(S("w_rounded"), 1)

        def blocks(name):
            p = ph[name]
            for n in range(p.nb):
                if not (name == order[-1] and n == p.nb - 1):
                    round_block(name, n // 2, n % 2)
                yield n

        def square(m, j, wait):
            if wait:
                e.wait_ge(*wait)
            if m or not isinstance(j, int) or j:
                e.wait_ge(S("acc_done"), j + KD * m)
            if not isinstance(j, int):
                e.nop(nofuse=True)
            hj = h[:, bass.ds(j, 1), :].rearrange("p a t -> p (a t)")
            e.activation(sq[:], hj, ACT.Square).then_inc(S("sq_ready"), 1)

        def head(m, j, wait=None):
            if wait:
                e.wait_ge(*wait)
                e.nop(nofuse=True)
            hj = h[:, bass.ds(j, 1), :].rearrange("p a t -> p (a t)")
            xj = xr[:, bass.ds(j, 1), :].rearrange("p a t -> p (a t)")
            g0 = POFF["gains"] + m * KD
            e.activation(xj, hj, ACT.Copy, scale=prm[:, bass.ds(j + g0, 1)]).then_inc(S("xr_ready"), 1)

        def root(m):
            e.wait_ge(S("ss_ready"), m + 1)
            e.activation(two(R[:]), psn, ACT.Sqrt, scale=1.0 / D, bias=eps6[:, 0:1]).then_inc(S("root_ready"), 1)

        def up_phase(n, c):
            p = ph[("up", n, c)]
            u0 = n * TOTAL_U + (CHUNKS[0] if c else 0)
            with e.Fori(0, p.nb // 2) as i:
                for s in range(2):
                    round_block(("up", n, c), i, s)
                    e.wait_ge(S("tile_evacuated"), i * 4 + (p.t0 + 2 * s + 1 + CR_EVAC))
                    e.activation(sg[:], tg[:], ACT.Silu).then_inc(S("silu_ready"), 1)
                    e.wait_ge(S("hidden_made"), i * 2 + (u0 + s + 1))
                    e.nop(nofuse=True)
                    e.activation(hr[:, bass.ds(i * 2 + s, 1), :].rearrange("p a t -> p (a t)"), hd[:], ACT.Copy
                                 ).then_inc(S("hr_ready"), 1)

        def down_phase(n, c, m_next):
            p = ph[("down", n, c)]
            with e.Fori(0, p.nb // 2) as i:
                for s in range(2):
                    round_block(("down", n, c), i, s)
                    if c == 1:
                        w = (S("tile_evacuated"), i * 2 + (p.t0 + s + 1 + CR_EVAC))
                        head(m_next, i * 2 + s, w)
                        square(m_next, i * 2 + s, None)

        def ffn(n, m):
            up_phase(n, 0)
            down_phase(n, 0, None)
            up_phase(n, 1)
            down_phase(n, 1, m + 1)
            root(m + 1)

        e.dma_start(brel[:], A["brel"]).then_inc(S("bias_loaded"), 16)
        e.dma_start(bone[:], A["bone"]).then_inc(S("bias_loaded"), 16)
        e.wait_ge(S("h_loaded"), 16)
        e.wait_ge(S("prm_loaded"), 16)
        for j in range(KD):
            head(0, j)
            square(0, j, (S("h_loaded"), 16))
        round_block(order[0], 0, 0, first=True)
        for hh in range(HEADS):
            e.wait_ge(S("grep_copied"), hh + 1)
            e.dma_start(scratch[hh].rearrange("(p y) -> p y", p=P), grep[:]).then_inc(S("grep_stored"), 16)
        e.wait_ge(S("ones_ready"), 3)
        root(0)
        ffn(0, 0)

        e.dma_start(wgraw[:], A["wg"]).then_inc(S("wg_loaded"), 16)
        e.dma_start(us[:, :, :, 0:HIST], A["hist"]).then_inc(S("hist_loaded"), 16)
        e.wait_ge(S("wg_loaded"), 16)
        e.activation(wgr[:], wgraw[:], ACT.Copy).then_inc(S("wgr_ready"), 1)
        for n in blocks("glu"):
            e.wait_ge(S("tile_evacuated"), evac_at("glu", 2 * n + 1))
            e.activation(sg[:], tu[:], ACT.Sigmoid).then_inc(S("glu_sig"), 1)
        e.wait_ge(S("u_ready"), 2 * TM)
        e.dma_start(A["conv_p"], up[:, :, SEQ:SEQ + HIST]).then_inc(S("conv_stored"), 16)
        e.wait_ge(S("hist_loaded"), 16)
        for j in range(TM):
            e.dma_start(A["conv_s"][:, j], us[:, j, :, TB:TB + HIST]).then_inc(S("conv_stored"), 16)
        for n in blocks("kv"):
            if n == 0:
                e.preload_act_table_set("natural_log_exp_and_others")
                e.wait_ge(S("row_z"), 1)
                e.activation(rowB[:], rowt[:], ACT.Abs).then_inc(S("row_act"), 1)
                e.wait_ge(S("row_act"), 1)
                e.activation(rowB[:], rowB[:], ACT.Exp, scale=-1.0).then_inc(S("row_act"), 1)
                e.wait_ge(S("row_act"), 2)
                e.activation(rowB[:], rowB[:], ACT.Ln, bias=1.0).then_inc(S("row_act"), 1)
            if n == 1:
                e.wait_ge(S("row_m"), 1)
                e.dma_start(A["mrow"], rowt[:]).then_inc(S("m_stored"), 16)
                e.activation(rowem[:], rowt[:], ACT.Exp, scale=-1.0).then_inc(S("rows_exp"), 1)
                e.wait_ge(S("row_m"), 2)
                e.activation(rowwi[:, SEQ:T], rowwi[:, SEQ:T], ACT.Exp).then_inc(S("rows_exp"), 1)
                e.wait_ge(S("row_m"), 4)
                e.activation(rowws[:], rowws[:], ACT.Exp).then_inc(S("rows_exp"), 1)

        def copy_turned(n, full, part):
            e.wait_ge(S("turned"), n + 1)
            e.activation(full, ps[:, 4, :].rearrange("p (i d) -> p i d", d=P), ACT.Copy
                         ).then_inc(S("turned_copied"), 1)
            e.activation(part, ps[0:SMP, 5, 0:P], ACT.Copy).then_inc(S("turned_copied"), 1)

        for n in range(8):
            dst = kn[:, :, n, :] if n < 4 else vn[:, :, n - 4, 0:P]
            copy_turned(n, dst[:, 0:TM, :], dst[0:SMP, TM, :])
        for n in blocks("qo"):
            if n >= 2:
                for o in (2 * (n - 2), 2 * (n - 2) + 1):
                    e.wait_ge(S("tile_evacuated"), evac_at("qo", 4 + o))
                    e.activation(oT[:, o, :], tu[:], ACT.Sigmoid).then_inc(S("o_ready"), 1)
        e.wait_ge(S("conv_stored"), 16 * (1 + TM))
        for j in range(TM):
            e.wait_ge(S("ln_centered"), j + 1)
            if j >= 2:
                e.wait_ge(S("ln_var"), j - 1)
            e.activation((hd, sq)[j % 2][:], cv[:, j, :], ACT.Square).then_inc(S("ln_sq"), 1)
        e.wait_ge(S("ln_var"), TM)
        e.activation(two(acc[:]), psn, ACT.Sqrt, scale=1.0 / DA, bias=eps5[:, 0:1]).then_inc(S("ln_root"), 1)
        for j in range(TM):
            e.wait_ge(S("ln_scaled"), j + 1)
            e.activation(cv[:, j, :], cv[:, j, :], ACT.Silu, scale=W("ln_g", j), bias=W("ln_b", j)
                         ).then_inc(S("conv_out"), 1)
            e.wait_ge(S("conv_out"), j + 1)
            e.activation(xr[:, j, :], cv[:, j, :], ACT.Copy).then_inc(S("mixr_ready"), 1)
        def load_state(hh):
            e.dma_start(C0[:], A["C0"][hh]).then_inc(S("C0_loaded"), 16)

        load_state(0)
        for hh in range(HEADS):
            e.wait_ge(S("bcast_ready"), hh + 1)
            if hh == 0:
                e.wait_ge(S("mix_ready"), TM)
            else:
                e.wait_ge(S("head_done"), hh)
            e.activation(hd[:, 0:SEQ], ps[:, 1, 0:SEQ], ACT.Copy).then_inc(S("em_copied"), 1)
            for i in range(ST):
                w = SEQ - i * P if i < TM else SMP
                r = P if i < TM else SMP
                e.wait_ge(S("gap_ready"), ST * hh + i + 1)
                e.activation(Ds[0:r, i % 2, 0:w], Xs[0:r, i % 2, 0:w], ACT.Exp, scale=-1.0
                             ).then_inc(S("decay_ready"), 1)
            e.wait_ge(S("b_out"), hh + 1)
            e.activation(xr[:, TM + hh, :], sq[:], ACT.Copy).then_inc(S("mixr_ready"), 1)
            e.wait_ge(S("head_done"), hh + 1)
            e.dma_start(A["Cp"][hh], Cp[:]).then_inc(S("C_stored"), 16)
            e.dma_start(A["Cs"][hh], Cn[:]).then_inc(S("C_stored"), 16)
            if hh + 1 < HEADS:
                load_state(hh + 1)

        def out_phase(name, m):
            for n in blocks(name):
                for j in (2 * n, 2 * n + 1):
                    square(m, j, (S("tile_evacuated"), evac_at(name, j)))

        def heads_after(m):
            for j in range(KD):
                head(m, j)

        out_phase(("out", 0), 2)
        heads_after(2)
        root(2)
        e.wait_ge(S("C_stored"), 32 * HEADS)
        e.wait_ge(S("m_stored"), 16)
        ffn(1, 2)

        def ple(l):
            m = 4 * l + 4
            e.dma_start(praw[:], A["pT"][l]).then_inc(S("p_loaded"), 16)
            name = ("ple", l)
            for n in blocks(name):
                if n == 0:
                    e.wait_ge(S("p_loaded"), 16 * (l + 1))
                    e.activation(pr[:], praw[:], ACT.Copy).then_inc(S("pr_ready"), 1)
                e.wait_ge(S("tile_evacuated"), evac_at(name, 2 * n))
                e.activation(sg[:], tg[:], ACT.Sigmoid).then_inc(S("ple_sig"), 1)
                square(m, n, (S("ple_added"), KD * l + n + 1))
            if l == 0:
                heads_after(m)
            root(m)

        ple(0)
        ffn(2, 4)

        for hh in range(HEADS):
            e.dma_start(strip[:, hh, :],
                        scratch[hh, P - 1:P - 1 + P * (GL - 1)].rearrange("(p x) -> p x", x=GL - 1)[:, 0:SEQ]
                        ).then_inc(S("strip_loaded"), 16)
            for b in range(2):
                for c in range(2):
                    r = b * 64 + hh * 16 + c * 8
                    o = PAST - 1
                    e.dma_start(sstrip[r:r + TB, :],
                                scratch[hh, o:o + TB * (GL - 1)].rearrange("(t x) -> t x", x=GL - 1)[:, 0:PAST + TB]
                                ).then_inc(S("strip_loaded"), 16)
        e.preload_act_table_set("natural_log_exp_and_others")
        e.wait_ge(S("lam_sums"), 1)
        e.activation(nlam[:, 0:2], nlam[:, 2:4], ACT.Exp).then_inc(S("lam_exp"), 1)
        for kind in range(2):
            for n in blocks(f"qk{kind}"):
                if n == 3:
                    e.wait_ge(S("tile_evacuated"), evac_at(f"qk{kind}", 7))
                    e.dma_start(A[("dk", "sk")[kind]], ok[kind][:]).then_inc(S("kv_stored"), 16)
            for n in blocks(f"v{kind}"):
                for t in (2 * n, 2 * n + 1):
                    e.wait_ge(S("tile_evacuated"), evac_at(f"v{kind}", t))
                    e.dma_start(A[("dv", "sv")[kind]][:, t], vtmp[t][:]).then_inc(S(f"v_stored{t}"), 16)
            for n in range(4):
                dst = ov[kind][:, :, n * P:(n + 1) * P]
                copy_turned(8 + 4 * kind + n, dst[:, 0:TM, :], dst[0:SMP, TM, :])
        for t in range(4):
            e.wait_ge(S(f"v_stored{t}"), 32)

        def load_cache(job):
            kind, pair = job // PAIRS, job % PAIRS
            for b in range(2):
                for g in range(NPG):
                    n = (2 * pair + b) * NPG + g
                    pg = e.value_load(pages[0:1, n:n + 1], min_val=0, max_val=A["kc0"].shape[0] - 1)
                    e.dma_start(kc[job % 2][:, b, :, g, :],
                                A[f"kc{kind}"][bass.ds(pg, 1)].rearrange("a p h s -> p (a h) s")
                                ).then_inc(S(f"keys_loaded{job % 2}"), 16)
                    e.dma_start(vc[job % 2][:, b, g, :],
                                A[f"vc{kind}"][bass.ds(pg, 1)].rearrange("a s d -> (a s) d")
                                ).then_inc(S(f"values_loaded{job % 2}"), 16)

        e.wait_ge(S("pages_loaded"), 16)
        load_cache(0)
        e.wait_ge(S("tile_done"), done_at("v1", 3))
        load_cache(1)

        def soft(u):
            w = width(u)
            buf, k = rows[u % 4], u - N
            e.wait_ge(S("rows_turned"), u - 3)
            e.wait_ge(S("scores"), score_count(u + 1))
            e.activation(buf[:, 0:w], ps[:, score_bank(u, 0), 0:w], ACT.Abs).then_inc(S("soft_step"), 1)
            e.wait_ge(S("soft_step"), 3 * k + 1)
            e.activation(buf[:, 0:w], buf[:, 0:w], ACT.Exp, scale=-1.0).then_inc(S("soft_step"), 1)
            e.wait_ge(S("soft_step"), 3 * k + 2)
            e.activation(buf[:, 0:w], buf[:, 0:w], ACT.Ln, bias=1.0).then_inc(S("soft_step"), 1)

        for tick in range(NM + 5):
            if tick < N:
                w = width(tick)
                for c in range(1 if MAPS[tick][3] == SAMPLES else 2):
                    e.wait_ge(S("maxed"), softmaxes(tick) + c + 1)
                    buf = (rows, rows2)[c][tick % 4]
                    e.activation(buf[:, 0:w], buf[:, 0:w], ACT.Exp, bias=st(tick, c),
                                 accum_out=st(tick, 2 + c)).then_inc(S("exped"), 1)
            elif tick < NM:
                soft(tick)
            u = tick - 1
            if N <= u < NM:
                e.wait_ge(S("summed"), u - N + 1)
                buf = rows[u % 4]
                e.activation(buf[:, 0:width(u)], buf[:, 0:width(u)], ACT.Exp, bias=st(u, 4)
                             ).then_inc(S("weights_done"), 1)
            if 3 <= tick < N + 3:
                u = tick - 3
                copy_rowsT(e, u)
            if 5 <= tick:
                u = tick - 5
                kind, hh, c, i = MAPS[u]
                job = kind * PAIRS + hh
                if i == SAMPLES:
                    e.wait_ge(S("values_done"), u + 1)
                    n = 128 if kind else 64
                    if job:
                        e.wait_ge(S("sample_turned"), job)
                    e.activation(srow[0:n, 0:DA], ps[0:n, out_bank(u), :], ACT.Copy).then_inc(S("sample_rows"), 1)
                    if job + 2 < 2 * PAIRS:
                        load_cache(job + 2)
                if i == TM - 1 and c == kind:
                    e.wait_ge(S("values_done"), u + 1)
                    e.activation(oq[kind][:, hh, 0:SEQ], ps[:, out_bank(u), :], ACT.Copy
                                 ).then_inc(S("attn_copied"), 1)

        for hh in range(HEADS):
            if hh == 0:
                e.wait_ge(S("sample_copied"), 2 * PAIRS)
                e.wait_ge(S("attn_copied"), 2 * HEADS)
                e.wait_ge(S("rows_turned"), NM)
            if hh >= 2:
                e.wait_ge(S("oc_ss"), hh - 1)
            e.activation((sg, hd)[hh % 2][:], oq[0][:, hh, :], ACT.Square).then_inc(S("oc_sq"), 1)
            e.wait_ge(S("oc_ss"), hh + 1)
            if hh >= 2:
                e.wait_ge(S("oc_scaled"), hh - 1)
            e.activation(two((tg, tu)[hh % 2][:]), psn, ACT.Sqrt, scale=1.0 / P, bias=eps6[:, 0:1]
                         ).then_inc(S("oc_root"), 1)
        for j in range(KD):
            if j < HEADS:
                e.wait_ge(S("oc_scaled"), j + 1)
            e.activation(xr[:, j, :], oq[j // TM][:, j % TM, :], ACT.Copy).then_inc(S("mixr_ready"), 1)

        out_phase(("out", 1), 6)
        heads_after(6)
        root(6)
        e.wait_ge(S("kv_stored"), 32)
        ffn(3, 6)
        ple(1)
        for sem, n in (("conv_stored", 16 * (1 + TM)), ("m_stored", 16), ("C_stored", 32 * HEADS),
                       ("kv_stored", 32), ("grep_stored", 16 * HEADS)):
            e.wait_ge(S(sem), n)
        for j in range(KD):
            e.wait_ge(S("y_ready"), j + 1)
            e.dma_start(A["yT"][:, j], h[:, j, :]).then_inc(S("y_stored"), 16)
        e.wait_ge(S("y_stored"), 16 * KD)

    @block.vector
    def _(e):
        e.nop().then_inc(S("tile_evacuated"), CR_EVAC)
        e.memset(eps6[:], 1e-6).then_inc(S("ones_ready"), 1)
        e.memset(eps5[:], 1e-5).then_inc(S("ones_ready"), 1)
        e.memset(ones[:], 1.0).then_inc(S("ones_ready"), 1)
        stepped = [0]

        def step(ins):
            stepped[0] += 1
            ins.then_inc(S("dve_step"), 1)

        def settle():
            e.wait_ge(S("dve_step"), stepped[0])

        def rest(m, j):
            e.wait_ge(S("xr_ready"), j + (KD * m + 1))
            hj = h[:, bass.ds(j, 1), :].rearrange("p a t -> p (a t)")
            xj = xr[:, bass.ds(j, 1), :].rearrange("p a t -> p (a t)")
            lj = xl[:, bass.ds(j, 1), :].rearrange("p a t -> p (a t)")
            e.scalar_tensor_tensor(lj, hj, prm[:, bass.ds(j + (POFF["gains"] + m * KD), 1)], xj.bitcast(F32),
                                   ALU.mult, ALU.subtract).then_inc(S("x_ready"), 1)

        def add_square(m, j, first):
            e.wait_ge(S("sq_ready"), j + (KD * m + 1))
            if first:
                e.tensor_copy(acc[:], sq[:]).then_inc(S("acc_done"), 1)
            else:
                e.wait_ge(S("acc_done"), j + KD * m)
                e.tensor_tensor(acc[:], acc[:], sq[:], ALU.add).then_inc(S("acc_done"), 1)

        def zero_acc(m):
            if m:
                e.wait_ge(S("ss_ready"), m)
            e.memset(acc[:], 0.0).then_inc(S("acc_zero"), 1)
            e.wait_ge(S("acc_zero"), zeroed[0] + 1)
            zeroed[0] += 1

        zeroed = [0]

        def factor(m):
            e.wait_ge(S("root_ready"), m + 1)
            e.reciprocal(R[:], R[:]).then_inc(S("R_ready"), 1)
            e.wait_ge(S("R_ready"), m + 1)

        def normed(out, u, wait, scale=None):
            e.wait_ge(S("tile_done"), wait)
            if scale is None:
                ins = e.tensor_tensor(two(out), unit(u), two(R[:]), ALU.mult)
            else:
                ins = e.scalar_tensor_tensor(two(out), unit(u), scale, two(R[:]), ALU.mult, ALU.mult)
            ins.then_inc(S("tile_evacuated"), 1)

        def up_phase(n, c):
            p = ph[("up", n, c)]
            u0 = n * TOTAL_U + (CHUNKS[0] if c else 0)
            with e.Fori(0, p.nb // 2) as i:
                for s in range(2):
                    t = p.t0 + 2 * s
                    normed(tg[:], 0, i * 4 + (t + 1 + CR_TILE))
                    normed(tu[:], 1, i * 4 + (t + 2 + CR_TILE))
                    e.wait_ge(S("silu_ready"), i * 2 + (u0 + s + 1))
                    e.wait_ge(S("tile_evacuated"), i * 4 + (t + 2 + CR_EVAC))
                    e.tensor_tensor(hd[:], tu[:], sg[:], ALU.mult).then_inc(S("hidden_made"), 1)
                    e.wait_ge(S("hr_ready"), i * 2 + (u0 + s + 1))
                    r = hr[:, bass.ds(i * 2 + s, 1), :].rearrange("p a t -> p (a t)")
                    q = hl[:, bass.ds(i * 2 + s, 1), :].rearrange("p a t -> p (a t)")
                    e.tensor_tensor(q, hd[:], r.bitcast(F32), ALU.subtract).then_inc(S("hidden_ready"), 1)

        def down_phase(n, c, m_next):
            p = ph[("down", n, c)]
            with e.Fori(0, p.nb // 2) as i:
                for s in range(2):
                    j = i * 2 + s
                    e.wait_ge(S("tile_done"), i * 2 + (p.t0 + s + 1 + CR_TILE))
                    hj = h[:, bass.ds(j, 1), :].rearrange("p o (a t) -> p (o a) t", a=2)
                    e.scalar_tensor_tensor(hj, unit(s), 0.5, hj, ALU.mult, ALU.add
                                           ).then_inc(S("tile_evacuated"), 1)
                    if c == 1:
                        e.wait_ge(S("tile_evacuated"), i * 2 + (p.t0 + s + 1 + CR_EVAC))
                        rest(m_next, j)
                        e.wait_ge(S("sq_ready"), i * 2 + (KD * m_next + s + 1))
                        e.wait_ge(S("acc_done"), i * 2 + (KD * m_next + s))
                        e.tensor_tensor(acc[:], acc[:], sq[:], ALU.add).then_inc(S("acc_done"), 1)

        def ffn(n, m):
            up_phase(n, 0)
            down_phase(n, 0, None)
            up_phase(n, 1)
            zero_acc(m + 1)
            down_phase(n, 1, m + 1)
            factor(m + 1)

        e.wait_ge(S("h_loaded"), 16)
        e.wait_ge(S("prm_loaded"), 16)
        for j in range(KD):
            rest(0, j)
            add_square(0, j, j == 0)
        for hh in range(HEADS):
            e.wait_ge(S("grep_made"), hh + 1)
            if hh:
                e.wait_ge(S("grep_stored"), 16 * hh)
            e.tensor_copy(grep[:].rearrange("p (a y) -> p a y", a=2), ps[:, 6:8, 0:GL // 2]
                          ).then_inc(S("grep_copied"), 1)
        factor(0)
        ffn(0, 0)

        e.wait_ge(S("grep_stored"), 16 * HEADS)
        step(e.memset(up[:, :, 0:HIST], 0.0))
        e.memset(vn[:, :, :, P:P + 1], 1.0).then_inc(S("vn_ones"), 1)
        e.wait_ge(S("wgr_ready"), 1)
        e.tensor_tensor(wgl[:], wgraw[:], wgr[:].bitcast(F32), ALU.subtract).then_inc(S("wg_split"), 2)
        for j in range(TM):
            normed(tg[:], 0, done_at("glu", 2 * j))
            normed(tu[:], 1, done_at("glu", 2 * j + 1))
            e.wait_ge(S("glu_sig"), j + 1)
            e.wait_ge(S("tile_evacuated"), evac_at("glu", 2 * j))
            e.tensor_tensor(up[:, j, HIST:], tg[:, 0:SEQ], sg[:, 0:SEQ], ALU.mult).then_inc(S("u_ready"), 1)
            e.tensor_tensor(us[:, j, :, HIST:], tg[:, SEQ:T].rearrange("p (b t) -> p b t", b=NB),
                            sg[:, SEQ:T].rearrange("p (b t) -> p b t", b=NB), ALU.mult
                            ).then_inc(S("u_ready"), 1)
            e.wait_ge(S("u_ready"), 2 * j + 2)

        e.wait_ge(S("gates_done"), 1)
        step(e.tensor_tensor(two(rowa[:]), ps[0:4, 6:8, 0:HALF], two(R[0:4, :]), ALU.mult))
        step(e.tensor_tensor(two(rowt[:]), ps[32:36, 6:8, 0:HALF], two(R[32:36, :]), ALU.mult))
        settle()
        step(e.tensor_scalar(rowa[:], rowa[:], W("gate_b", 0, rows=4), None, ALU.add))
        e.tensor_scalar(rowt[:], rowt[:], W("gate_b", 1, rows=4), None, ALU.add).then_inc(S("row_z"), 1)
        seg = lambda row: row[:, SEQ:T].rearrange("p (b t) -> p b t", t=TB)
        step(e.memset(rowwi[:], 1.0))
        step(e.memset(rowws[:], 0.0))
        settle()
        step(e.memset(seg(rowwi)[:, :, 0:1], 0.0))
        step(e.memset(seg(rowws)[:, :, 0:1], NEG))
        e.wait_ge(S("row_act"), 3)
        e.wait_ge(S("row_z"), 1)
        step(e.scalar_tensor_tensor(rowt[:], rowt[:], 0.0, rowB[:], ALU.min, ALU.subtract))
        settle()
        step(e.tensor_tensor_scan(rowB[:], rowwi[:], rowt[:], 0.0, ALU.mult, ALU.add))
        settle()
        step(e.tensor_tensor(rowa[:], rowa[:], rowB[:], ALU.subtract))
        settle()
        step(e.tensor_copy(rowt[:], rowa[:]))
        settle()
        m0 = W("m0", 0, NB, rows=4).unsqueeze(2)
        step(e.tensor_tensor(seg(rowt)[:, :, 0:1], seg(rowa)[:, :, 0:1], m0, ALU.max))
        settle()
        step(e.tensor_tensor_scan(rowM[:], rowws[:], rowt[:], 0.0, ALU.add, ALU.max))
        settle()
        e.tensor_tensor(rowt[:], rowB[:], rowM[:], ALU.add).then_inc(S("row_m"), 1)
        e.tensor_tensor(seg(rowwi), m0.broadcast_to([4, NB, TB]), seg(rowM), ALU.subtract).then_inc(S("row_m"), 1)
        e.tensor_scalar(rowws[:, 0:SEQ], rowa[:, 0:SEQ], rowM[:, SEQ - 1:SEQ], None, ALU.subtract
                        ).then_inc(S("row_m"), 1)
        e.tensor_tensor(seg(rowws), seg(rowa), seg(rowM)[:, :, TB - 1:TB].broadcast_to([4, NB, TB]),
                        ALU.subtract).then_inc(S("row_m"), 1)

        e.wait_ge(S("hist_loaded"), 16)
        conv_steps = [0]
        accp, accs = ps[:, 6, 0:SEQ], ps[:, 7, 0:SMP].rearrange("p (b t) -> p b t", b=NB)

        def tap(j, k, outp, outs, sem=None, wait=None):
            w = prm[:, bass.ds(k + (POFF["conv_w"] + j * TAPS), 1)]
            if wait is not None:
                e.wait_ge(S("conv_step"), wait)
            inp = up[:, j, bass.ds(k, SEQ)]
            ins_ = us[:, j, :, bass.ds(k, TB)]
            if wait is None:
                a = e.tensor_scalar(outp, inp, w, W("conv_b", j), ALU.mult, ALU.add)
                b = e.tensor_scalar(outs, ins_, w, W("conv_b", j), ALU.mult, ALU.add)
            else:
                a = e.scalar_tensor_tensor(outp, inp, w, accp, ALU.mult, ALU.add)
                b = e.scalar_tensor_tensor(outs, ins_, w, accs, ALU.mult, ALU.add)
            a.then_inc(S("conv_step"), 1)
            b.then_inc(S(sem or "conv_step"), 1)

        def conv_chunk(slot):
            j, q = slot // 4, slot % 4
            k0, k1 = q * 8, min(q * 8 + 8, TAPS - 1)
            base = conv_steps[0]
            if q == 0:
                if j:
                    e.wait_ge(S("conv_done"), j)
                tap(j, 0, accp, accs)
                base += 2
                k0 = 1
            with e.Fori(0, k1 - k0) as i:
                tap(j, i + k0, accp, accs, wait=i * 2 + base)
            base += 2 * (k1 - k0)
            if q == 3:
                tap(j, TAPS - 1, cv[:, j, 0:SEQ], cv[:, j, SEQ:T].rearrange("p (b t) -> p b t", b=NB),
                    sem="conv_done", wait=base)
                base += 1
            conv_steps[0] = base

        for t in range(8):
            if t < 4:
                normed(kT[:, t, :], t % 2, done_at("kv", t), P ** -0.5)
            else:
                normed(vtmp[t - 4][:], t % 2, done_at("kv", t))
            conv_chunk(t)
        for t in range(8):
            if t < 4:
                normed(qT[:, t, :], t % 2, done_at("qo", t))
            else:
                if t > 4:
                    e.wait_ge(S("o_ready"), t - 4)
                normed(tu[:], t % 2, done_at("qo", t))
            conv_chunk(8 + t)
        e.wait_ge(S("cols_turned"), 1)
        for q in range(2):
            o = q * ST * HEADS
            e.tensor_copy(gcol[:, o:o + 16], ps[:, 4, o:o + 16]).then_inc(S("cols_copied"), 1)
            e.tensor_copy(gcol[0:SMP, o + 16:o + 20], ps[0:SMP, 4, o + 16:o + 20]).then_inc(S("cols_copied"), 1)
        e.wait_ge(S("ln_sum"), 1)
        for j in range(TM):
            e.scalar_tensor_tensor(two(cv[:, j, :]), psn, -1.0 / DA, two(cv[:, j, :]), ALU.mult, ALU.add
                                   ).then_inc(S("ln_centered"), 1)
        e.wait_ge(S("ln_root"), 1)
        step(e.reciprocal(acc[:], acc[:]))
        settle()
        for j in range(TM):
            e.tensor_tensor(cv[:, j, :], cv[:, j, :], acc[:], ALU.mult).then_inc(S("ln_scaled"), 1)
        for j in range(TM):
            e.wait_ge(S("mixr_ready"), j + 1)
            e.tensor_tensor(xl[:, j, :], cv[:, j, :], xr[:, j, :].bitcast(F32), ALU.subtract
                            ).then_inc(S("mix_ready"), 1)

        e.wait_ge(S("mix_ready"), TM)
        e.wait_ge(S("cols_copied"), 4)
        for hh in range(HEADS):
            e.wait_ge(S("bcast_ready"), hh + 1)
            step(e.tensor_copy(smp[:, 0:3 * SMP], ps[:, 6, 0:3 * SMP]))
            e.wait_ge(S("C0_loaded"), 16 * (hh + 1))
            qs = qT[:, hh, SEQ:T].rearrange("p (b t) -> p b t", b=NB)
            e.tensor_tensor(smp[:, 3 * SMP:].rearrange("p (b t) -> p b t", b=NB), qs,
                            C0[:, :, P:P + 1].broadcast_to([P, NB, TB]), ALU.mult).then_inc(S("qn_ready"), 1)
            wcol = lambda i, r=P: gcol[0:r, (ST + i) * HEADS + hh:(ST + i) * HEADS + hh + 1]
            for i in range(TM):
                step(e.tensor_scalar(kw[:, i, :], kn[:, i, hh, :], wcol(i), None, ALU.mult))
            step(e.tensor_scalar(wsm[:], C("blk_col", rows=SMP), wcol(TM, SMP), None, ALU.mult))
            settle()
            e.tensor_tensor(kwm[:], kn[0:SMP, TM, hh, :].unsqueeze(1).broadcast_to([SMP, NB, P]),
                            wsm[:].unsqueeze(2).broadcast_to([SMP, NB, P]), ALU.mult).then_inc(S("kw_ready"), 1)

            def gap(i):
                k = ST * hh + i
                if k >= 2:
                    e.wait_ge(S("decay_ready"), k - 1)
                r, w = (P, SEQ - i * P) if i < TM else (SMP, SMP)
                src = ps[:, 0, i * P:SEQ] if i < TM else smp[0:SMP, 0:SMP]
                a = gcol[0:r, i * HEADS + hh:i * HEADS + hh + 1]
                e.tensor_scalar(Xs[0:r, i % 2, 0:w], src, a, 0.0, ALU.subtract, ALU.max
                                ).then_inc(S("gap_ready"), 1)

            def weigh(i):
                k = ST * hh + i
                r, w = (P, SEQ - i * P) if i < TM else (SMP, SMP)
                e.wait_ge(S("decay_ready"), k + 1)
                e.wait_ge(S("s_ready"), k + 1)
                if k >= 2:
                    e.wait_ge(S("pv_done"), k - 1)
                pm = Pm[i % 2]
                step(e.tensor_tensor(pm[0:r, 0:w], ps[0:r, 4 + i % 2, 0:w], Ds[0:r, i % 2, 0:w], ALU.mult))
                settle()
                m = C("cm") if i < TM else C("blk_ml", rows=SMP)
                n = P if i < TM else SMP
                e.tensor_tensor(pm[0:r, 0:n], pm[0:r, 0:n], m, ALU.mult).then_inc(S("p_ready"), 1)

            gap(0)
            for i in range(ST):
                if i + 1 < ST:
                    gap(i + 1)
                weigh(i)
            e.wait_ge(S("em_copied"), hh + 1)
            e.wait_ge(S("pv_done"), ST * (hh + 1))
            e.wait_ge(S("inter_ready"), hh + 1)
            if hh:
                e.wait_ge(S("mixr_ready"), TM + hh)
            o5, wi = 5 * SMP, smp[:, 2 * SMP:3 * SMP]
            step(e.tensor_scalar(tu[:, 0:SEQ], ps[:, 3, 0:SEQ], -1.0, None, ALU.mult))
            step(e.tensor_tensor(tu[:, SEQ:T], ps[:, 6, o5 + SMP:o5 + 2 * SMP], wi, ALU.mult))
            step(e.tensor_tensor(acc[:, SEQ:T], ps[:, 6, o5:o5 + SMP], wi, ALU.mult))
            settle()
            step(e.tensor_tensor(tu[:, 0:SEQ], tu[:, 0:SEQ], ps[:, 3, 0:SEQ], ALU.max))
            step(e.tensor_tensor(tu[:, SEQ:T], tu[:, SEQ:T], ps[:, 6, 4 * SMP:5 * SMP], ALU.add))
            step(e.tensor_tensor(acc[:, SEQ:T], acc[:, SEQ:T], ps[:, 6, 3 * SMP:4 * SMP], ALU.add))
            settle()
            step(e.scalar_tensor_tensor(tu[:, SEQ:T], tu[:, SEQ:T], -1.0, tu[:, SEQ:T], ALU.mult, ALU.max))
            settle()
            step(e.tensor_tensor(tu[:, 0:SEQ], tu[:, 0:SEQ], hd[:, 0:SEQ], ALU.max))
            step(e.tensor_tensor(tu[:, SEQ:T], tu[:, SEQ:T], smp[:, SMP:2 * SMP], ALU.max))
            settle()
            step(e.reciprocal(tu[:], tu[:]))
            settle()
            e.tensor_tensor(acc[:, 0:SEQ], ps[:, 2, 0:SEQ], tu[:, 0:SEQ], ALU.mult).then_inc(S("h_read"), 1)
            step(e.tensor_tensor(acc[:, SEQ:T], acc[:, SEQ:T], tu[:, SEQ:T], ALU.mult))
            settle()
            e.wait_ge(S("h_read"), hh + 1)
            e.wait_ge(S("o_ready"), HEADS)
            e.tensor_tensor(sq[:], acc[:], oT[:, hh, :], ALU.mult).then_inc(S("b_out"), 1)
            e.wait_ge(S("state_ready"), hh + 1)
            if hh:
                e.wait_ge(S("C_stored"), 32 * hh)
            step(e.tensor_copy(Cp[:], ps[:, 7, 0:P + 1]))
            for b in range(NB):
                o = (b % 3) * (P + 1)
                d = smp[:, 2 * SMP + b * TB + TB - 1:2 * SMP + b * TB + TB]
                ins = e.scalar_tensor_tensor(Cn[:, b, :], C0[:, b, :], d, ps[:, b // 3, o:o + P + 1],
                                             ALU.mult, ALU.add)
                if b < NB - 1:
                    step(ins)
            settle()
            ins.then_inc(S("head_done"), 1)
            e.wait_ge(S("mixr_ready"), TM + hh + 1)
            e.wait_ge(S("b_out"), hh + 1)
            e.tensor_tensor(xl[:, TM + hh, :], sq[:], xr[:, TM + hh, :].bitcast(F32), ALU.subtract
                            ).then_inc(S("mix_ready"), 1)

        def rests(m):
            for j in range(KD):
                rest(m, j)

        def out_and_norm(name, m):
            zero_acc(m)
            for j in range(KD):
                e.wait_ge(S("tile_done"), done_at(name, j))
                e.tensor_tensor(two(h[:, j, :]), unit(j % 2), two(h[:, j, :]), ALU.add
                                ).then_inc(S("tile_evacuated"), 1)
                add_square(m, j, False)
            rests(m)
            factor(m)

        out_and_norm(("out", 0), 2)
        ffn(1, 2)

        def ple(l):
            name, m = ("ple", l), 4 * l + 4
            e.wait_ge(S("pr_ready"), l + 1)
            e.tensor_tensor(pl[:], praw[:], pr[:].bitcast(F32), ALU.subtract).then_inc(S("p_split"), 1)
            zero_acc(m)
            for j in range(KD):
                normed(tg[:], 0, done_at(name, 2 * j))
                e.wait_ge(S("ple_sig"), KD * l + j + 1)
                e.wait_ge(S("tile_done"), done_at(name, 2 * j + 1))
                e.tensor_tensor(two(tu[:]), unit(1), two(sg[:]), ALU.mult).then_inc(S("tile_evacuated"), 1)
                e.wait_ge(S("tile_evacuated"), evac_at(name, 2 * j + 1))
                e.tensor_tensor(h[:, j, :], h[:, j, :], tu[:], ALU.add).then_inc(S("ple_added"), 1)
                add_square(m, j, False)
            if l == 0:
                rests(m)
            factor(m)

        ple(0)
        ffn(2, 4)

        lp = W("lam", 0, 256)
        lpv = lp.rearrange("p (a b d) -> p a b d", a=2, b=2)
        step(e.tensor_tensor(lamt[:].rearrange("p (a d) -> p a d", a=2), lpv[:, :, 0, :], lpv[:, :, 1, :], ALU.mult))
        settle()
        e.tensor_reduce(nlam[:, 2:4], lamt[:].rearrange("p (a d) -> p a d", a=2), AX.X, ALU.add
                        ).then_inc(S("lam_sums"), 1)
        e.wait_ge(S("lam_exp"), 1)
        step(e.tensor_tensor(nlam[:, 4:5], nlam[:, 1:2], nlam[:, 0:1], ALU.subtract))
        settle()
        step(e.tensor_scalar(nlam[:, 4:5], nlam[:, 4:5], -LAM_INIT, None, ALU.add))
        settle()
        step(e.scalar_tensor_tensor(nlam[:, 5:6], C("half1"), nlam[:, 4:5], C("half0"), ALU.mult, ALU.add))
        e.wait_ge(S("strip_loaded"), 16 * HEADS * 5)
        for hh in range(HEADS):
            step(e.tensor_tensor(strip[:, hh, SEQ - P:SEQ], strip[:, hh, SEQ - P:SEQ], C("neg_incl"), ALU.add))
        for pair in range(PAIRS):
            step(e.tensor_tensor(sbias[:, pair * SMP:(pair + 1) * SMP].rearrange("p (b t) -> p b t", b=NB),
                                 C("dneg", pair * SMP, (pair + 1) * SMP).rearrange("p (b t) -> p b t", b=NB),
                                 sstrip[:, PAST:PAST + TB].unsqueeze(1).broadcast_to([P, NB, TB]), ALU.add))
        step(e.memset(qbd[:], 0.0))
        for kind in range(2):
            for t in range(8):
                dst = (oq, ok)[t // 4][kind][:, t % 4, :]
                normed(dst, t % 2, done_at(f"qk{kind}", t), 0.125 if t < 4 else None)
            for t in range(4):
                if kind:
                    e.wait_ge(S("turned"), 12)
                    e.wait_ge(S(f"v_stored{t}"), 16)
                normed(vtmp[t][:], t % 2, done_at(f"v{kind}", t))
        for t in range(4):
            e.wait_ge(S(f"v_stored{t}"), 32)
        e.wait_ge(S("turned"), 16)

        def sample_queries(job):
            kind, pair = job // PAIRS, job % PAIRS
            if job:
                e.wait_ge(S("scores"), score_count(SAMPLE_AT[job - 1] + 1))
            for b in range(2):
                for c in range(2):
                    src = oq[kind][64 * c:64 * c + 64, :, SEQ + (2 * pair + b) * TB:SEQ + (2 * pair + b + 1) * TB]
                    dst = qbd[64 * c:64 * c + 64, b, :].rearrange("p (h x) -> p h x", x=80)[:, :, c * 8:c * 8 + 8]
                    ins = e.tensor_copy(dst, src)
                    if (b, c) != (1, 1):
                        step(ins)
            settle()
            ins.then_inc(S("qbd_ready"), 1)

        def bias_and_max(u, q, buf, w, parts):
            for n, (a, b, bias) in enumerate(parts):
                ins = e.tensor_tensor(buf[:, a:b], ps[:, score_bank(u, q), a:b], bias, ALU.add)
                if n < len(parts) - 1:
                    step(ins)
                    settle()
            ins.then_inc(S("biased"), 1)
            e.wait_ge(S("biased"), softmaxes(u) + q + 1)
            e.tensor_reduce(st(u, q), buf[:, 0:w], AX.X, ALU.max, negate=True).then_inc(S("maxed"), 1)

        def probs(u):
            w = width(u)
            b0, b1 = rows[u % 4], rows2[u % 4]
            e.wait_ge(S("exped"), softmaxes(u + 1))
            if MAPS[u][3] == SAMPLES:
                step(e.reciprocal(st(u, 2), st(u, 2)))
                settle()
                e.tensor_scalar(b0[:, 0:w], b0[:, 0:w], st(u, 2), nlam[:, 5:6], ALU.mult, ALU.mult
                                ).then_inc(S("probs_done"), 1)
                return
            o = 5 * (u % 4) + 2
            step(e.reciprocal(tiny[:, o:o + 2], tiny[:, o:o + 2]))
            settle()
            step(e.tensor_scalar(b0[:, 0:w], b0[:, 0:w], st(u, 2), None, ALU.mult))
            step(e.tensor_scalar(st(u, 3), st(u, 3), nlam[:, 4:5], None, ALU.mult))
            settle()
            e.scalar_tensor_tensor(b0[:, 0:w], b1[:, 0:w], st(u, 3), b0[:, 0:w], ALU.mult, ALU.add
                                   ).then_inc(S("probs_done"), 1)

        def sums(u):
            k, w = u - N, width(u)
            buf, scan, src = rows[u % 4], rows2[u % 4], ps[:, score_bank(u, 0), 0:w]
            if k < 4:
                e.wait_ge(S("probs_done"), u - 3)
                step(e.memset(scan[:, 0:1], 0.0))
            e.wait_ge(S("soft_step"), 3 * k + 3)
            step(e.scalar_tensor_tensor(buf[:, 0:w], src, 0.0, buf[:, 0:w], ALU.max, ALU.add))
            settle()
            step(e.tensor_tensor_scan(scan[:, 1:w + 1], ones[:, 0:1].broadcast_to([P, w]), buf[:, 0:w], 0.0,
                                      ALU.mult, ALU.add))
            if k >= 4:
                e.wait_ge(S("weights_done"), k - 3)
            settle()
            step(e.tensor_scalar(st(u, 4), scan[:, w:w + 1], -1.0, None, ALU.mult))
            e.tensor_tensor(buf[:, 0:w], src, scan[:, 0:w], ALU.add).then_inc(S("summed"), 1)

        def copy_sample_out(u):
            kind, pair = MAPS[u][0:2]
            t0, bank = SEQ + 2 * pair * TB, out_bank(u)
            e.wait_ge(S("sample_turned"), SAMPLE_AT.index(u) + 1)
            if kind == 0:
                ins = e.tensor_copy(oq[0][:, :, t0:t0 + 2 * TB],
                                    ps[:, bank, 0:64].rearrange("p (h x) -> p h x", h=HEADS))
            else:
                for c in range(2):
                    r = slice(64 * c, 64 * c + 64)
                    ins = e.tensor_copy(oq[1][r, :, t0:t0 + 2 * TB].rearrange("p h (b t) -> p h b t", b=2),
                                        ps[r, bank, 0:128].rearrange("p (h b c t) -> p c h b t", b=2, h=HEADS, c=2)[:, c])
                    if c == 0:
                        step(ins)
                settle()
            ins.then_inc(S("sample_copied"), 1)

        sample_queries(0)
        for tick in range(NM + 3):
            if tick < N:
                kind, hh, c, i = MAPS[tick]
                w = width(tick)
                if tick >= 4:
                    e.wait_ge(S("rows_turned"), tick - 3)
                for c in range(1 if i == SAMPLES else 2):
                    e.wait_ge(S("scores"), score_count(tick) + c + 1)
                    bias_and_max(tick, c, (rows, rows2)[c][tick % 4], w,
                                 [(0, w, strip[:, hh, SEQ - w:SEQ])] if i < SAMPLES else
                                 [(0, PAST, sstrip[:, 0:PAST]), (PAST, KEYS, sbias[:, hh * SMP:(hh + 1) * SMP])])
            elif tick < NM:
                sums(tick)
            if 1 <= tick <= N:
                probs(tick - 1)
            if N + 3 <= tick:
                copy_rowsT(e, tick - 3)
            if tick < NM and MAPS[tick][3] == SAMPLES:
                job = SAMPLE_AT.index(tick)
                if job + 1 < 2 * PAIRS:
                    sample_queries(job + 1)
            if tick - 7 in SAMPLE_AT:
                copy_sample_out(tick - 7)

        for hh in range(HEADS):
            buf = (tg, tu)[hh % 2]
            e.wait_ge(S("oc_root"), hh + 1)
            if hh == 0:
                e.wait_ge(S("sample_copied"), 2 * PAIRS)
            step(e.reciprocal(buf[:], buf[:]))
            settle()
            step(e.tensor_tensor(oq[0][:, hh, :], oq[0][:, hh, :], buf[:], ALU.mult))
            settle()
            e.tensor_scalar(oq[0][:, hh, :], oq[0][:, hh, :], W("head_g", hh), 1.0 - LAM_INIT, ALU.mult, ALU.mult
                            ).then_inc(S("oc_scaled"), 1)
        for j in range(KD):
            e.wait_ge(S("mixr_ready"), KD + j + 1)
            e.tensor_tensor(xl[:, j, :], oq[j // TM][:, j % TM, :], xr[:, j, :].bitcast(F32), ALU.subtract
                            ).then_inc(S("mix_ready"), 1)
        out_and_norm(("out", 1), 6)
        ffn(3, 6)
        ple(1)
        for j in range(KD):
            g = W("gains", 8 * KD + j)
            e.scalar_tensor_tensor(h[:, j, :], h[:, j, :], g, R[:], ALU.mult, ALU.mult).then_inc(S("y_ready"), 1)

    return ctx


def constants():
    c = np.zeros((P, CW), np.float32)

    def put(name, a):
        c[:a.shape[0], COFF[name]:COFF[name] + a.shape[1]] = a

    p, j = np.arange(P)[:, None], np.arange(P)[None, :]
    put("ident", np.eye(P, dtype=np.float32))
    put("cm", (j >= p).astype(np.float32))
    put("neg_incl", np.where(j > p, NEG, 0.0).astype(np.float32))
    put("sb_neg", np.where(j >= p, NEG, 0.0).astype(np.float32))
    s, t = np.arange(SMP)[:, None], np.arange(SMP)[None, :]
    put("blk_ml", ((s // TB == t // TB) & (t >= s)).astype(np.float32))
    put("blk_col", (s // TB == np.arange(NB)[None, :]).astype(np.float32))
    row = np.arange(P)
    b2, tq = row // 64, row % TB
    for pair in range(PAIRS):
        own = t // TB == (2 * pair + b2)[:, None]
        incl = own & (t % TB <= tq[:, None])
        strict = own & (t % TB < tq[:, None])
        o = pair * SMP
        c[:, COFF["dneg"] + o:COFF["dneg"] + o + SMP] = np.where(incl, 0.0, NEG)
        c[:, COFF["sneg"] + o:COFF["sneg"] + o + SMP] = np.where(strict, 0.0, NEG)
    head, half = (row % 64) // 16, (row % 16) // 8
    put("fold", ((b2 * 32 + head * 8 + tq)[:, None] == np.arange(64)[None, :]).astype(np.float32))
    put("half0", (half == 0).astype(np.float32)[:, None])
    put("half1", (half == 1).astype(np.float32)[:, None])
    sel = np.zeros((4, 4, P), np.float32)
    for q in range(4):
        sel[q, q] = 1
    put("sel", sel.reshape(4, -1))
    n = np.maximum(SEQ - 1 - np.arange(GL), 0)
    exact = 16
    nf = np.maximum(n, 1).astype(np.float32)
    large = exact + (np.log(nf / exact) / np.float32(np.log(128 / exact)) * (32 - exact)).astype(np.int32)
    bucket = np.where(n < exact, n, np.minimum(large, 31))
    onehot = (bucket[None, :] == np.arange(32)[:, None]).astype(np.float32)
    return c, onehot


def tiles_of(w, nk):
    nj = w.shape[1] // P
    return np.ascontiguousarray(w.reshape(nk, P, nj, P).transpose(2, 1, 0, 3))


def feature_major(a):
    return np.ascontiguousarray(a.reshape(a.shape[0], -1, P).transpose(2, 1, 0))


def by_partition(v):
    return np.ascontiguousarray(v.reshape(-1, P).T)


def kernel(**inputs):
    import concourse.bacc as bacc
    from concourse.bass_utils import run_bass_kernel_spmd

    I = {k: np.asarray(v) for k, v in inputs.items()}
    c, onehot = constants()
    a = {"cst": c, "bone": onehot}
    both = lambda x, y: np.concatenate([x.reshape(SEQ, -1), y.reshape(SMP, -1)], 0)
    a["xT"] = feature_major(both(I["x_prompt"], I["x_sample"]))
    a["pT"] = np.stack([feature_major(both(I["p_prompt"][l], I["p_sample"][l])) for l in range(2)])

    up, d0, d1, ple = [], [], [], []
    for l in range(2):
        for wi, wo in ((I["ffn1_wi"][l], I["ffn1_wo"][l]), (I["ffn2_wi"][l], I["ffn2_wo"][l])):
            t = tiles_of(wi, KD)
            nt = t.shape[0] // 2
            up.append(np.stack([t[:nt], t[nt:]], 2).reshape(nt, P, -1))
            t = tiles_of(wo, DFF // P)
            d0.append(t[:, :, :CHUNKS[0]].reshape(KD, P, -1))
            d1.append(t[:, :, CHUNKS[0]:].reshape(KD, P, -1))
        g, q = tiles_of(I["ple_wg"][l], KD), tiles_of(I["ple_wp"][l], KP)
        ple.append(np.concatenate([g.reshape(KD, P, -1), q.reshape(KD, P, -1)], 2))
    pairs = lambda t: t.reshape(-1, 2, P, KD * P).transpose(0, 2, 1, 3).reshape(-1, P, 2 * KD * P)
    ev = I["ev_w_in"][0]
    t = tiles_of(np.ascontiguousarray(ev[:, :24 * P]), KD)
    val, gate, q, k, v, o = (t[4 * n:4 * n + 4] for n in range(6))
    ev_t = np.concatenate([np.stack([val, gate], 1).reshape(8, *t.shape[1:]), k, v, q, o])
    od_t = tiles_of(I["od_w_in"][0], KD)
    a["up"], a["down0"], a["down1"], a["ple"] = (np.concatenate(x) for x in (up, d0, d1, ple))
    cq, ck, cvv, sq_, sk, sv = (od_t[4 * n:4 * n + 4] for n in range(6))
    a["mixin"] = np.concatenate([pairs(ev_t), pairs(np.concatenate([cq, ck, cvv, sq_, sk, sv]))])
    a["mixout"] = np.concatenate([pairs(tiles_of(I["ev_w_out"][0], KD)), pairs(tiles_of(I["od_w_out"][0], KD))])
    wg = np.zeros((P, KD, 36), np.float32)
    gates = ev[:, 24 * P:].reshape(KD, P, 8).transpose(1, 0, 2)
    wg[:, :, 0:4], wg[:, :, 32:36] = gates[:, :, 0:4], gates[:, :, 4:8]
    a["wg"] = wg

    prm = np.zeros((P, PW), np.float32)

    def put(name, x, at=0):
        prm[:x.shape[0], POFF[name] + at:POFF[name] + at + x.shape[1]] = x

    for l in range(2):
        for n, name in enumerate(("ffn_norm1", "mix_norm", "ffn_norm2", "ple_norm")):
            put("gains", by_partition(I[name][l]), (4 * l + n) * KD)
    put("gains", by_partition(I["final_norm"]), 8 * KD)
    put("conv_w", I["ev_conv_w"][0].reshape(TAPS, TM, P).transpose(2, 1, 0).reshape(P, -1))
    put("conv_b", by_partition(I["ev_conv_b"][0]))
    put("ln_g", by_partition(I["ev_ln_g"][0]))
    put("ln_b", by_partition(I["ev_ln_b"][0]))
    put("gate_b", I["ev_gate_b"][0].reshape(2, 4).T)
    put("head_g", by_partition(I["od_head_g"][0]))
    put("lam", np.broadcast_to(I["od_lambda"][0].reshape(1, 256), (P, 256)))
    put("m0", I["state_mlstm_m"][0].T)
    a["prm"] = prm
    a["hist"] = np.ascontiguousarray(I["state_conv"][0].reshape(NB, HIST, TM, P).transpose(3, 2, 0, 1))
    st = np.concatenate([I["state_mlstm_C"][0], I["state_mlstm_n"][0][..., None]], -1)
    a["C0"] = np.ascontiguousarray(st.transpose(1, 2, 0, 3))
    a["brel"] = np.ascontiguousarray(np.repeat(I["rel_bias"], P, axis=1))
    a["pages"] = I["page_table"].reshape(1, -1)
    for kind, name in enumerate(("diff", "sb")):
        kk = I[f"cache_{name}_k"][0]
        a[f"kc{kind}"] = np.ascontiguousarray(kk.reshape(-1, PAGE, HEADS, P).transpose(0, 3, 2, 1))
        a[f"vc{kind}"] = np.ascontiguousarray(I[f"cache_{name}_v"][0].reshape(-1, PAGE, DA))

    nc = bacc.Bacc("TRN2", target_bir_lowering=False, num_devices=1, dynamic_dma_scratch_size=1024)
    A = {n: nc.dram_tensor(f"in_{n}", x.shape, mybir.dt.from_np(x.dtype), kind="ExternalInput").ap()
         for n, x in a.items()}
    outs = dict(yT=(P, KD, T), conv_p=(P, TM, HIST), conv_s=(P, TM, NB, HIST), Cp=(HEADS, P, P + 1),
                Cs=(HEADS, P, NB, P + 1), mrow=(HEADS, T), dk=(P, TM, T), dv=(P, TM, T), sk=(P, TM, T), sv=(P, TM, T))
    for n, shape in outs.items():
        A[n] = nc.dram_tensor(f"out_{n}", shape, F32, kind="ExternalOutput").ap()
    A["scratch"] = nc.dram_tensor("scratch", (HEADS, P * GL), F32, kind="Internal").ap()
    build(nc, A).close()
    r = run_bass_kernel_spmd(nc, [{f"in_{n}": x for n, x in a.items()}], core_ids=[0]).results[0]
    O = {n: r[f"out_{n}"] for n in outs}

    def token_major(x):
        t = x.transpose(2, 1, 0).reshape(T, -1)
        return t[:SEQ], t[SEQ:]

    yp, ys = token_major(O["yT"])
    res = [yp.reshape(1, SEQ, D), ys.reshape(NB, TB, D)]
    res.append(O["conv_p"].transpose(2, 1, 0).reshape(1, 1, HIST, DA))
    res.append(O["conv_s"].transpose(2, 3, 1, 0).reshape(1, NB, HIST, DA))
    cs = O["Cs"].transpose(2, 0, 1, 3)
    res += [O["Cp"][None, None, :, :, :P], cs[None, ..., :P], O["Cp"][None, None, :, :, P], cs[None, ..., P]]
    res += [O["mrow"][:, SEQ - 1].reshape(1, 1, HEADS), O["mrow"][:, SEQ + TB - 1::TB].T[None]]
    for n, sh in (("dk", (HEADS, P)), ("dv", (HEADS, P)), ("sk", (8, 64)), ("sv", (8, 64))):
        kp, ks = token_major(O[n])
        res += [kp.reshape(1, 1, SEQ, *sh), ks.reshape(1, NB, TB, *sh)]
    return tuple(np.ascontiguousarray(x) for x in res)
```

```python
from contextlib import ExitStack, nullcontext

import numpy as np
import concourse.bass as bass
from concourse import mybir

F32 = mybir.dt.float32
F32R = mybir.dt.float32r
I32 = mybir.dt.int32
ALU = mybir.AluOpType
ACT = mybir.ActivationFunctionType
AX = mybir.AxisListType

P = 128
D = 1024
SEQ = 512
NB, TB = 8, 8
SMP = NB * TB
T = SEQ + SMP
HALF = T // 2
KD = D // P
DFF = 2816
CHUNKS = (12, 10)
assert sum(CHUNKS) * P == DFF
HIST = 30
TAPS = 31
HEADS = 4
DA = 512
TM = DA // P
PAST, PAGE = 256, 128
NPG = PAST // PAGE
PLE = 256
KP = PLE // P
KEYS = PAST + SMP
PAIRS = NB // 2
GL = 640
NEG = -1e30
LAM_INIT = 0.8 - 0.6 * float(np.exp(-0.3))
ST = T // P + 1
BLK = 2048

CONST = dict(ident=128, cm=128, neg_incl=128, sb_neg=128, blk_ml=64, blk_col=8,
             dneg=4 * 64, sneg=4 * 64, fold=64, half0=1, half1=1,
             sel=4 * 128)
COFF = {}
_o = 0
for _n, _w in CONST.items():
    COFF[_n] = _o
    _o += _w
CW = _o
PARAM = dict(gains=9 * KD, conv_w=TM * TAPS, conv_b=TM, ln_g=TM, ln_b=TM, gate_b=2, head_g=TM,
             lam=256, m0=8)
POFF = {}
_o = 0
for _n, _w in PARAM.items():
    POFF[_n] = _o
    _o += _w
PW = _o


class Phase:
    blocks = tiles = 0

    def __init__(self, src, at, nb, ks):
        self.src, self.at, self.nb, self.ks = src, at, nb, ks
        self.width = sum(ks) * P
        self.n0, self.t0, self.T = Phase.blocks, Phase.tiles, len(ks)
        Phase.blocks += nb
        Phase.tiles += nb * len(ks)
        assert nb % 2 == 0 and (nb * len(ks)) % 2 == 0 and self.width <= BLK


def schedule():
    Phase.blocks = Phase.tiles = 0
    ph = {}
    order = []

    def add(name, *a):
        ph[name] = Phase(*a)
        order.append(name)

    def ffn(n):
        at = 0
        for c, k in enumerate(CHUNKS):
            add(("up", n, c), "up", n * sum(CHUNKS) + at, k, (KD, KD))
            at += k
            add(("down", n, c), f"down{c}", n * KD, KD, (k,))

    for l in range(2):
        ffn(2 * l)
        if l == 0:
            add("glu", "mixin", 0, 4, (KD, KD))
            add("kv", "mixin", 4, 4, (KD, KD))
            add("qo", "mixin", 8, 4, (KD, KD))
        else:
            add("qk0", "mixin", 12, 4, (KD, KD))
            add("v0", "mixin", 16, 2, (KD, KD))
            add("qk1", "mixin", 18, 4, (KD, KD))
            add("v1", "mixin", 22, 2, (KD, KD))
        add(("out", l), "mixout", l * 4, 4, (KD, KD))
        ffn(2 * l + 1)
        add(("ple", l), "ple", l * KD, KD, (KD, KP))
    return ph, order


def build(nc, A):
    ph, order = schedule()
    ctx = ExitStack()
    sems = {}

    def S(name):
        if name not in sems:
            sems[name] = ctx.enter_context(nc.semaphore(name))
        return sems[name]

    top = [(nc.sbuf_base + 31) // 32 * 32]
    END = nc.sbuf_base + nc.sbuf_bytes_remaining

    def sb(name, shape, dt=F32, at=None):
        size = (int(np.prod(shape[1:])) * 4 + 31) // 32 * 32
        if at is None:
            a = top[0]
            top[0] += size
        else:
            a = at[0]
            at[0] += size
        assert a + size <= END, (name, a + size - END)
        return nc.alloc_sbuf_tensor_at(name, shape, dt, offset=a)

    h = sb("h", [P, KD, T])
    XR_AT = top[0]
    xr = sb("xr", [P, KD, T], F32R)
    xl = sb("xl", [P, KD, T], F32R)
    raw = [sb(f"raw{s}", [P, BLK]) for s in range(2)]
    wr, wl, W_AT = [], [], []
    for s in range(2):
        W_AT.append(top[0])
        wr.append(sb(f"wr{s}", [P, BLK], F32R))
        wl.append(sb(f"wl{s}", [P, BLK], F32R))
    R = sb("R", [P, T])
    tg, sg, tu, hd, sq, acc = (sb(n, [P, T]) for n in ("tg", "sg", "tu", "hd", "sq", "acc"))
    cst = sb("cst", [P, CW])
    prm = sb("prm", [P, PW])
    ones = sb("ones", [P, P])
    eps6 = sb("eps6", [P, 1])
    eps5 = sb("eps5", [P, 1])
    pages = sb("pages", [1, NB * NPG], I32)
    tiny = sb("tiny", [P, 64])
    ZONE = top[0]
    vtmp = [hd, sq, tg, sg]

    z = [ZONE]
    hr = sb("hr", [P, max(CHUNKS), T], F32R, at=z)
    hl = sb("hl", [P, max(CHUNKS), T], F32R, at=z)
    brel = sb("brel", [32, HEADS * P], at=z)
    bone = sb("bone", [32, GL], at=z)
    grep = sb("grep", [P, GL], at=z)
    z = [ZONE]
    praw = sb("praw", [P, KP, T], at=z)
    pr = sb("pr", [P, KP, T], F32R, at=z)
    pl = sb("pl", [P, KP, T], F32R, at=z)
    z = [ZONE]
    up = sb("up", [P, TM, HIST + SEQ], at=z)
    us = sb("us", [P, TM, NB, HIST + TB], at=z)
    z2 = [ZONE]
    C0 = [sb(f"C0{k}", [P, NB, P + 1], at=z2) for k in range(2)]
    Cn = sb("Cn", [P, NB, P + 1], at=z2)
    Cp = sb("Cp", [P, P + 1], at=z2)
    kw = hd[:, 0:SEQ].rearrange("p (i d) -> p i d", i=TM)
    Mb, emb = (nc.alloc_sbuf_tensor_at(n, [P, HEADS, SEQ], F32, offset=W_AT[1] + q * BLK * 4)
               for q, n in enumerate(("Mb", "emb")))
    assert z2[0] <= z[0]
    cv = sb("cv", [P, TM, T], at=z)
    qT = sb("qT", [P, HEADS, T], at=z)
    kT = sb("kT", [P, HEADS, T], at=z)
    oT = sb("oT", [P, HEADS, T], at=z)
    kn = sb("kn", [P, ST, HEADS, P], at=z)
    vn = sb("vn", [P, ST, HEADS, P + 1], at=z)
    z3 = [z[0]]
    rowt, rowB, rowa, rowws = (sb(n, [HEADS, T], at=z) for n in ("rowt", "rowB", "rowa", "rowws"))
    Xs = sb("Xs", [P, 2, SEQ], at=z3)
    Ds = sb("Ds", [P, 2, SEQ], at=z3)
    assert z3[0] <= z[0]
    rows3 = sb("rows3", [HEADS, 3, T], at=z)
    rowM, rowem, rowwi = (rows3[:, q, :] for q in range(3))
    gcol = sb("gcol", [P, 2 * ST * HEADS], at=z)
    wgraw = sb("wgraw", [P, KD, 36], at=z)
    wgr = sb("wgr", [P, KD, 36], F32R, at=z)
    wgl = sb("wgl", [P, KD, 36], F32R, at=z)
    kwm = sb("kwm", [SMP, NB, P], at=z)
    smp = sb("smp", [P, HEADS, 3, SMP], at=z)
    wsm = sb("wsm", [SMP, NB], at=z)
    qn = tiny
    ENDS = [z[0]]
    Pm = [tg, sg]
    z = [ZONE]
    oq = [sb(f"oq{i}", [P, TM, T], at=z) for i in range(2)]
    ok = [sb(f"ok{i}", [P, TM, T], at=z) for i in range(2)]
    ov = [sb(f"ov{i}", [P, ST, DA], at=z) for i in range(2)]
    strip = sb("strip", [P, HEADS, SEQ], at=z)
    sstrip = sb("sstrip", [P, PAST + TB], at=z)
    sbias = sb("sbias", [P, PAIRS * SMP], at=z)
    kc = [sb("kc0", [P, 2, HEADS, NPG, PAGE], at=z),
          nc.alloc_sbuf_tensor_at("kc1", [P, 2, HEADS, NPG, PAGE], F32, offset=XR_AT)]
    vc = [sb("vc0", [P, 2, NPG, DA], at=z),
          nc.alloc_sbuf_tensor_at("vc1", [P, 2, NPG, DA], F32, offset=XR_AT + KD * T * 4)]
    qbd = sb("qbd", [P, 2, 5 * 64], at=z)
    rows, rowsT = ([nc.alloc_sbuf_tensor_at(f"{n}{k}", [P, SEQ], F32, offset=W_AT[1] + (q * 4 + k) * SEQ * 4)
                    for k in range(4)] for q, n in enumerate(("rows", "rowsT")))
    assert 4 * SEQ <= BLK
    rows2 = [tg, sg, tu, hd]
    srow = sq
    nlam = sb("nlam", [P, 8], at=z)
    lamt = sb("lamt", [P, 128], at=z)
    ENDS.append(z[0])
    assert max(ENDS) <= END, ("zone", [END - x for x in ENDS])

    ps = ctx.enter_context(nc.psum_tensor("ps", [P, 8, 512], F32))

    def unit(u):
        return ps[:, 2 * u:2 * u + 2, 0:HALF]

    def two(ap):
        return ap.rearrange("p (a t) -> p a t", a=2)

    psn = ps[:, 4:6, 0:HALF]

    def C(name, a=0, b=None, rows=P):
        o = COFF[name]
        return cst[0:rows, o + a:o + (CONST[name] if b is None else b)]

    def W(name, a, b=None, rows=P):
        o = POFF[name]
        return prm[0:rows, o + a:o + (a + 1 if b is None else b)]

    scratch = A["scratch"]
    BANKS = ((0, 1, 6), (2, 3, 7))

    CR_TILE = 1
    CR_EVAC = 2

    def done_at(p, t):
        return ph[p].t0 + t + 1 + CR_TILE

    def evac_at(p, t):
        return ph[p].t0 + t + 1 + CR_EVAC

    TOTAL_U = sum(CHUNKS)

    def st(k, q):
        o = 5 * (k % 4) + q
        return tiny[:, o:o + 1]

    SAMPLES = TM
    MAPS = [(0, hh, 0, i) for hh in range(HEADS) for i in (0, SAMPLES, 1, 2, 3)]
    N = len(MAPS)
    MAPS += [(1, hh, c, i) for hh in range(HEADS)
             for i, c in ((0, 0), (0, 1), (SAMPLES, 0), (1, 0), (1, 1), (2, 0), (2, 1), (3, 0), (3, 1))]
    NM = len(MAPS)
    SAMPLE_AT = [u for u, m in enumerate(MAPS) if m[3] == SAMPLES]

    def width(u):
        i = MAPS[u][3]
        return KEYS if i == SAMPLES else (i + 1) * P

    def softmaxes(u):
        return sum(1 if m[3] == SAMPLES else 2 for m in MAPS[:min(u, N)])

    def score_count(u):
        return softmaxes(u) + max(u - N, 0)

    def score_bank(u, c):
        return 2 * (u % 2) + (c if u < N else u // 2 % 2)

    def out_bank(u):
        kind, hh, c, i = MAPS[u]
        return 6 + (hh + (i == SAMPLES)) % 2

    def rows_done(u):
        return (S("probs_done"), u + 1) if u < N else (S("weights_done"), u - N + 1)

    def rowsT_copied(u):
        return (S("probsT_copied"), u + 1) if u < N else (S("weightsT_copied"), u - N + 1)

    def copy_rowsT(e, u):
        e.wait_ge(S("rows_turned"), u + 1)
        if u >= 4:
            e.wait_ge(S("values_done"), u - 3)
        dst, b = rowsT[u % 4], 4 + u % 2
        copy = (lambda o, i: e.activation(o, i, ACT.Copy)) if u < N else e.tensor_copy
        w = width(u)
        if MAPS[u][3] == SAMPLES:
            pitch = P if u >= N else 64
            w = NPG * pitch
            copy(dst[0:SMP, w:w + pitch], ps[0:SMP, b, w:w + pitch]).then_inc(S("rowsT_part"), 1)
            e.wait_ge(S("rowsT_part"), SAMPLE_AT.index(u) + 1)
        copy(dst[:, 0:w], ps[:, b, 0:w]).then_inc(rowsT_copied(u)[0], 1)

    block = ctx.enter_context(nc.Block())

    @block.sync
    def _(e):
        e.dma_start(prm[:], A["prm"]).then_inc(S("prm_loaded"), 16)
        def load_pair(p, i):
            for s in range(2):
                e.wait_ge(S(f"w_split{s}"), i + (p.n0 // 2 + 1))
                e.dma_start(raw[s][:, 0:p.width],
                            A[p.src][bass.ds(i * 2 + (p.at + s), 1)].rearrange("a p w -> p (a w)")
                            ).then_inc(S(f"raw_loaded{s}"), 16)

        def load_cache(job):
            kind, pair = job // PAIRS, job % PAIRS
            for b in range(2):
                for g in range(NPG):
                    n = (2 * pair + b) * NPG + g
                    pg = e.value_load(pages[0:1, n:n + 1], min_val=0, max_val=A["kc0"].shape[0] - 1)
                    e.dma_start(kc[job % 2][:, b, :, g, :],
                                A[f"kc{kind}"][bass.ds(pg, 1)].rearrange("a p h s -> p (a h) s")
                                ).then_inc(S(f"keys_loaded{job % 2}"), 16)
                    e.dma_start(vc[job % 2][:, b, g, :],
                                A[f"vc{kind}"][bass.ds(pg, 1)].rearrange("a s d -> (a s) d")
                                ).then_inc(S(f"values_loaded{job % 2}"), 16)

        for name in order:
            p = ph[name]
            if name != ("out", 1):
                with e.Fori(0, p.nb // 2) as i:
                    load_pair(p, i)
                continue
            load_pair(p, 0)
            e.wait_ge(S("pages_loaded"), 16)
            load_cache(0)
            e.wait_ge(S("tile_done"), done_at("v1", 3))
            load_cache(1)
            for job in range(2, 2 * PAIRS):
                e.wait_ge(S("values_done"), SAMPLE_AT[job - 2] + 1)
                load_cache(job)
            with e.Fori(1, p.nb // 2) as i:
                load_pair(p, i)

    @block.gpsimd
    def _(e):
        for s in range(2):
            e.memset(raw[s][:], 0.0).then_inc(S(f"w_split{s}"), 1)
        for name in order:
            p = ph[name]
            with e.Fori(0, p.nb // 2) as i:
                for s in range(2):
                    e.wait_ge(S("w_rounded"), i * 2 + (p.n0 + s + 1))
                    e.tensor_tensor(wl[s][:, 0:p.width], raw[s][:, 0:p.width],
                                    wr[s][:, 0:p.width].bitcast(F32), ALU.subtract
                                    ).then_inc(S(f"w_split{s}"), 1)

    @block.tensor
    def _(e):
        e.nop().then_inc(S("tile_done"), CR_TILE)

        def mm3(out, wrt, wlt, xrt, xlt, first, last):
            e.matmul(out, wrt, xrt, start=first, stop=False)
            e.matmul(out, wrt, xlt, start=False, stop=False)
            return e.matmul(out, wlt, xrt, start=False, stop=last)

        def gemm(name, rhs, ready, after=None):
            p = ph[name]
            with nullcontext() if after else e.Fori(0, p.nb // 2) as loop:
                for i in range(p.nb // 2) if after else (loop,):
                    for s in range(2):
                        e.wait_ge(S(f"w_split{s}"), i + (p.n0 // 2 + 2))
                        off = 0
                        for tile, kn_ in enumerate(p.ks):
                            t = s * p.T + tile
                            u = t % 2
                            e.wait_ge(S("tile_evacuated"), i * (2 * p.T) + (p.t0 + t - 2 + 1 + CR_EVAC))
                            for k in range(kn_):
                                need = ready(tile, k) if s == 0 else None
                                if need:
                                    e.wait_ge(S(need[0]), need[1])
                                a, b = off + k * P, off + (k + 1) * P
                                r, q = rhs(tile, k)
                                for hf in range(2):
                                    x0, x1 = hf * HALF, (hf + 1) * HALF
                                    mm = mm3(ps[:, 2 * u + hf, 0:HALF], wr[s][:, a:b], wl[s][:, a:b],
                                             r[:, x0:x1], q[:, x0:x1], k == 0, k == kn_ - 1)
                            off += kn_ * P
                            mm.then_inc(S("tile_done"), 1)
                            if after:
                                after(2 * p.T * i + t)

        def xin(tile, k):
            return xr[:, k, :], xl[:, k, :]

        def norm_sum(m):
            e.wait_ge(S("acc_done"), KD * (m + 1))
            if m:
                e.wait_ge(S("root_ready"), m)
            for hf in range(2):
                mm = e.matmul(ps[:, 4 + hf, 0:HALF], ones[:], acc[:, hf * HALF:(hf + 1) * HALF],
                              start=True, stop=True)
            mm.then_inc(S("ss_ready"), 1)

        def x_of(m):
            return lambda tile, k: ("x_ready", KD * m + k + 1) if tile == 0 else None

        no_wait = lambda tile, k: None

        def bias_row(hh):
            if hh == 0:
                e.wait_ge(S("bias_loaded"), 32)
            else:
                e.wait_ge(S("grep_copied"), hh)
            for hf in range(2):
                mm = e.matmul(ps[:, 6 + hf, 0:GL // 2], brel[:, hh * P:(hh + 1) * P],
                              bone[:, hf * (GL // 2):(hf + 1) * (GL // 2)], start=True, stop=True)
            mm.then_inc(S("grep_made"), 1)

        def ffn(n, m):
            hid = n * TOTAL_U
            for c, kc_ in enumerate(CHUNKS):
                gemm(("up", n, c), xin, x_of(m) if c == 0 else no_wait)
                if n == 0:
                    bias_row(2 * c)
                hid += kc_
                gemm(("down", n, c), lambda tile, k: (hr[:, k, :], hl[:, k, :]),
                     lambda tile, k, hid=hid, kc_=kc_: {0: ("hidden_ready", hid - 1),
                                                        kc_ - 1: ("hidden_ready", hid)}.get(k))
                if n == 0:
                    bias_row(2 * c + 1)

        e.wait_ge(S("ones_ready"), 3)
        norm_sum(0)
        ffn(0, 0)
        norm_sum(1)

        e.wait_ge(S("cst_loaded"), 16)
        gemm("glu", xin, x_of(1))
        e.wait_ge(S("wg_split"), 2)
        e.wait_ge(S("root_ready"), 2)
        for hf in range(2):
            for k in range(KD):
                mm = mm3(ps[0:36, 4 + hf, 0:HALF], wgr[:, k, :], wgl[:, k, :],
                         xr[:, k, hf * HALF:(hf + 1) * HALF], xl[:, k, hf * HALF:(hf + 1) * HALF],
                         k == 0, k == KD - 1)
        mm.then_inc(S("gates_done"), 1)

        def turn(src, phase, t, n):
            e.wait_ge(S("tile_evacuated"), evac_at(phase, t))
            if n:
                e.wait_ge(S("turned_copied"), 2 * n)
            else:
                e.wait_ge(S("row_z"), 1)
            for i in range(ST):
                w = P if i < ST - 1 else SMP
                mm = e.transpose(ps[0:w, 4 + i // 4, (i % 4) * P:(i % 4 + 1) * P],
                                 src[:, i * P:i * P + w], C("ident"))
            mm.then_inc(S("turned"), 1)

        def turn_kv(n):
            turn(kT[:, n, :] if n < 4 else vtmp[n - 4][:], "kv", n, n)

        gemm("kv", xin, no_wait, lambda t: turn_kv(t - 2) if t >= 2 else None)
        turn_kv(6)
        turn_kv(7)
        e.wait_ge(S("rows_exp"), 3)
        e.wait_ge(S("turned_copied"), 16)
        for q, row in enumerate((rowa, rowws)):
            for i in range(ST):
                w = P if i < ST - 1 else SMP
                o = (q * ST + i) * HEADS
                mm = e.transpose(ps[0:w, 4, o:o + HEADS], row[:, i * P:i * P + w],
                                 C("ident", 0, 4, rows=4))
        mm.then_inc(S("cols_turned"), 1)
        e.wait_ge(S("cols_copied"), 4)
        sel = lambda hh: C("sel", hh * P, (hh + 1) * P, rows=4)
        for hh in range(HEADS):
            o = hh % 2 * 3 * SMP
            mm = e.matmul(ps[:, 4 + hh // 2, o:o + 3 * SMP], sel(hh), rows3[:, :, SEQ:T], start=True, stop=True)
        mm.then_inc(S("smp_ready"), 1)
        gemm("qo", xin, no_wait)

        def spread(hh):
            if hh >= 2:
                e.wait_ge(S("bcast_copied"), 2 * (hh - 1))
            for q, row in enumerate((rowM, rowem)):
                mm = e.matmul(ps[:, 2 * (hh % 2) + q, :], sel(hh), row[:, 0:SEQ], start=True, stop=True)
            mm.then_inc(S("bcast_ready"), 1)

        e.wait_ge(S("smp_copied"), 2)
        for j in range(TM):
            if j == TM - 1:
                e.wait_ge(S("tile_evacuated"), evac_at("qo", 7))
                spread(0)
                spread(1)
            e.wait_ge(S("conv_done"), j + 1)
            for hf in range(2):
                mm = e.matmul(ps[:, 4 + hf, 0:HALF], ones[:], cv[:, j, hf * HALF:(hf + 1) * HALF],
                              start=j == 0, stop=j == TM - 1)
        mm.then_inc(S("ln_sum"), 1)
        spread(2)
        spread(3)

        def scores(k):
            hh, i = divmod(k, ST)
            w = P if i < ST - 1 else SMP
            n0 = i * P
            n1 = SEQ if i < ST - 1 else T
            if k >= 2:
                e.wait_ge(S("p_ready"), k - 1)
            e.matmul(ps[0:w, 4 + k % 2, 0:n1 - n0], kT[:, hh, n0:n0 + w], qT[:, hh, n0:n1],
                     start=True, stop=True).then_inc(S("s_ready"), 1)

        def values(k):
            hh, i = divmod(k, ST)
            num, den, rws = BANKS[hh % 2]
            n0 = i * P
            if i == 0 and hh >= 2:
                e.wait_ge(S("head_done"), hh - 1)
            e.wait_ge(S("p_ready"), k + 1)
            pm = Pm[k % 2]
            if i < ST - 1:
                e.matmul(ps[:, num, n0:SEQ], vn[:, i, hh, 0:P], pm[:, 0:SEQ - n0],
                         start=i == 0, stop=i == ST - 2)
                e.matmul(ps[:, den, n0:SEQ], ones[:], pm[:, 0:SEQ - n0],
                         start=i == 0, stop=i == ST - 2).then_inc(S("pv_done"), 1)
            else:
                e.matmul(ps[:, rws, 0:SMP], vn[0:SMP, i, hh, 0:P], pm[0:SMP, 0:SMP], start=True, stop=True)
                e.matmul(ps[:, rws, SMP:2 * SMP], ones[0:SMP, :], pm[0:SMP, 0:SMP], start=True, stop=True
                         ).then_inc(S("pv_done"), 1)

        def former(hh):
            rws = BANKS[hh % 2][2]
            e.wait_ge(S("qn_ready"), hh + 1)
            for b in range(NB):
                o = 2 * SMP + b * TB
                e.matmul(ps[:, rws, o:o + TB], C0[hh % 2][:, b, 0:P], qT[:, hh, SEQ + b * TB:SEQ + (b + 1) * TB],
                         start=True, stop=True)
            e.matmul(ps[:, rws, 3 * SMP:4 * SMP], ones[:], qn[:, 0:SMP], start=True, stop=True
                     ).then_inc(S("inter_ready"), 1)

        def states(hh):
            banks = BANKS[hh % 2]
            e.wait_ge(S("kw_ready"), TM * (hh + 1))
            e.wait_ge(S("kwm_ready"), hh + 1)
            e.wait_ge(S("h_read"), hh + 1)
            for i in range(TM):
                e.matmul(ps[:, banks[2], 2 * (P + 1):3 * (P + 1)], kw[:, i, :], vn[:, i, hh, :],
                         start=i == 0, stop=i == TM - 1)
            for b in range(NB):
                o = (b % 3) * (P + 1)
                mm = e.matmul(ps[:, banks[b // 3], o:o + P + 1], kwm[:, b, :], vn[0:SMP, ST - 1, hh, :],
                              start=True, stop=True)
            mm.then_inc(S("state_ready"), 1)

        e.wait_ge(S("ln_centered"), TM)
        scores(0)
        scores(1)
        for j in range(TM):
            e.wait_ge(S("ln_sq"), j + 1)
            for hf in range(2):
                mm = e.matmul(ps[:, 6 + hf, 0:HALF], ones[:], (hd, sq)[j % 2][:, hf * HALF:(hf + 1) * HALF],
                              start=j == 0, stop=j == TM - 1)
            mm.then_inc(S("ln_var"), 1)
        e.wait_ge(S("bcast_copied"), 2 * HEADS)
        e.wait_ge(S("vn_ones"), 1)
        for k in range(ST * HEADS):
            hh, i = divmod(k, ST)
            if k == ST - 1:
                e.wait_ge(S("ln_root"), 1)
            if i == 2 and hh:
                states(hh - 1)
            values(k)
            if i == ST - 1:
                former(hh)
            if k + 2 < ST * HEADS:
                scores(k + 2)
        states(HEADS - 1)

        e.wait_ge(S("head_done"), HEADS - 1)
        gemm(("out", 0), xin, lambda tile, k: ("mix_ready", k + 1) if tile == 0 else
             ("head_done", HEADS) if k == 0 else None)
        norm_sum(2)
        ffn(1, 2)
        norm_sum(3)

        def ple(l):
            gemm(("ple", l), lambda tile, k: (xr[:, k, :], xl[:, k, :]) if tile == 0
                 else (pr[:, k, :], pl[:, k, :]),
                 lambda tile, k: ("x_ready", KD * (4 * l + 3) + k + 1) if tile == 0 else ("p_split", l + 1))

        ple(0)
        norm_sum(4)
        ffn(2, 4)
        norm_sum(5)

        gemm("qk0", xin, x_of(5))
        gemm("v0", xin, no_wait)
        e.wait_ge(S("root_ready"), 6)
        gemm("qk1", xin, no_wait, lambda t: turn(vtmp[t][:], "v0", t, 8 + t) if t < 4 else None)
        gemm("v1", xin, no_wait, lambda t: turn(vtmp[t - 1][:], "v1", t - 1, 11 + t) if t else None)
        turn(vtmp[3][:], "v1", 3, 15)
        e.wait_ge(S("turned_copied"), 32)
        e.wait_ge(S("tile_evacuated"), evac_at("v1", 3))

        def turn_rows(u, src, w, other=None):
            e.wait_ge(*rows_done(u))
            if u >= 2:
                e.wait_ge(*rowsT_copied(u - 2))
            nblk = (w + P - 1) // P
            for b in range(nblk):
                wb = min(P, w - b * P)
                if other is None:
                    mm = e.transpose(ps[0:wb, 4 + u % 2, b * P:(b + 1) * P], src[:, b * P:b * P + wb], C("ident"))
                else:
                    mm = e.matmul(ps[0:wb, 4 + u % 2, b * 64:(b + 1) * 64], src[:, b * P:b * P + wb], other,
                                  start=True, stop=True)
            mm.then_inc(S("rows_turned"), 1)

        for tick in range(NM + 5):
            if tick < NM:
                u = tick
                kind, hh, c, i = MAPS[u]
                w = width(u)
                if i == SAMPLES:
                    job = kind * PAIRS + hh
                    e.wait_ge(S("qbd_ready"), job + 1)
                    e.wait_ge(S(f"keys_loaded{job % 2}"), 16 * 2 * NPG * (job // 2 + 1))
                if u >= N + 4:
                    e.wait_ge(S("summed"), u - 4 - N + 1)
                elif u >= 2:
                    e.wait_ge(S("biased"), softmaxes(min(u - 1, N)))
                if i == SAMPLES:
                    bank = score_bank(u, 0)
                    for b in range(2):
                        r = slice(64 * b, 64 * b + 64)
                        for hh_ in range(HEADS):
                            e.matmul(ps[r, bank, 0:PAST], qbd[:, b, hh_ * 64:(hh_ + 1) * 64],
                                     kc[job % 2][:, b, hh_, :, :].rearrange("p g s -> p (g s)"),
                                     start=hh_ == 0, stop=hh_ == HEADS - 1)
                        if kind:
                            e.matmul(ps[r, bank, PAST:KEYS], C("ident")[:, r], C("sneg", hh * SMP, (hh + 1) * SMP),
                                     start=True, stop=False)
                        for hh_ in range(HEADS):
                            mm = e.matmul(ps[r, bank, PAST:KEYS], qbd[:, b, hh_ * 64:(hh_ + 1) * 64],
                                          ok[kind][:, hh_, SEQ:T], start=hh_ == 0 and kind == 0,
                                          stop=hh_ == HEADS - 1)
                    mm.then_inc(S("scores"), 1)
                else:
                    for c_ in range(2) if kind == 0 else (c,):
                        r, bank = slice(64 * c_, 64 * c_ + 64), score_bank(u, c_)
                        q_ = oq[kind][r, hh, i * P:(i + 1) * P]
                        if kind == 0:
                            mm = e.matmul(ps[:, bank, 0:w], q_, ok[kind][r, hh, 0:w], start=True, stop=True)
                        else:
                            if i:
                                e.matmul(ps[:, bank, 0:w - P], q_, ok[kind][r, hh, 0:w - P], start=True, stop=True)
                            e.matmul(ps[:, bank, w - P:w], C("ident"), C("sb_neg"), start=True, stop=False)
                            mm = e.matmul(ps[:, bank, w - P:w], q_, ok[kind][r, hh, w - P:w], start=False, stop=True)
                        mm.then_inc(S("scores"), 1)
            if 3 <= tick < NM + 3:
                u = tick - 3
                turn_rows(u, rows[u % 4], width(u),
                          C("fold") if u < N and MAPS[u][3] == SAMPLES else None)
            if 4 <= tick < NM + 4:
                u = tick - 4
                kind, hh, c, i = MAPS[u]
                bank, rt = out_bank(u), rowsT[u % 4]
                e.wait_ge(*rowsT_copied(u))
                if i == SAMPLES:
                    job = kind * PAIRS + hh
                    e.wait_ge(S(f"values_loaded{job % 2}"), 16 * 2 * NPG * (job // 2 + 1))
                    if job:
                        e.wait_ge(S("attn_copied"), job)
                    n, pitch = (64, P) if kind else (32, 64)
                    for b in range(2):
                        for g in range(NPG + 1):
                            r = P if g < NPG else SMP
                            o = g * pitch + b * n
                            mm = e.matmul(ps[b * n:(b + 1) * n, bank, :], rt[0:r, o:o + n],
                                          vc[job % 2][:, b, g, :] if g < NPG else ov[kind][0:SMP, ST - 1, :],
                                          start=g == 0, stop=g == NPG)
                else:
                    if i == 0 and c == 0 and kind * HEADS + hh:
                        e.wait_ge(S("sample_copied"), kind * HEADS + hh)
                    f, r = ((slice(hh * P, (hh + 1) * P), slice(0, P)) if kind == 0 else
                               (slice((2 * hh + c) * 64, (2 * hh + c + 1) * 64), slice(64 * c, 64 * c + 64)))
                    for b in range(i + 1):
                        mm = e.matmul(ps[r, bank, i * P:(i + 1) * P], ov[kind][:, b, f],
                                      rt[:, b * P:(b + 1) * P], start=b == 0, stop=b == i)
                mm.then_inc(S("values_done"), 1)
            if tick - 6 in SAMPLE_AT:
                u = tick - 6
                kind, pair = MAPS[u][0:2]
                n = 64 if kind else 32
                e.wait_ge(S("sample_rows"), SAMPLE_AT.index(u) + 1)
                for hh in range(HEADS):
                    pick = C("ident", 0, 2 * n, rows=2 * n).rearrange("p (b h x) -> p h b x", b=2, h=HEADS)[:, hh]
                    mm = e.matmul(ps[:, out_bank(u), hh * n // 2:(hh + 1) * n // 2],
                                  srow[0:2 * n, hh * P:(hh + 1) * P], pick, start=True, stop=True)
                mm.then_inc(S("sample_turned"), 1)

        for hh in range(HEADS):
            e.wait_ge(S("oc_sq"), hh + 1)
            if hh:
                e.wait_ge(S("oc_root"), 2 * hh - 1)
            for hf in range(2):
                mm = e.matmul(ps[:, 4 + hf, 0:HALF], ones[:], (sg, hd)[hh % 2][:, hf * HALF:(hf + 1) * HALF],
                              start=True, stop=True)
            mm.then_inc(S("oc_ss"), 1)
        e.wait_ge(S("oc_root"), 2 * HEADS)
        gemm(("out", 1), xin, lambda tile, k: ("mix_ready", KD + k + 1) if tile == 0 else None)
        norm_sum(6)
        ffn(3, 6)
        norm_sum(7)
        ple(1)
        norm_sum(8)

    @block.scalar
    def _(e):
        def width_after(name):
            at = order.index(name) + 1
            return ph[order[at]].width if at < len(order) else 0

        def round_block(name, i, s, first=False):
            p = ph[name]
            if first:
                k, slot = p.n0 // 2 + 1, 0
                e.wait_ge(S("raw_loaded0"), 16 * k)
                w = p.width
            else:
                slot = 1 - s
                e.wait_ge(S(f"raw_loaded{slot}"), i * 16 + 16 * (p.n0 // 2 + 1 + s))
                e.wait_ge(S("tile_done"), i * (2 * p.T) + (p.t0 + p.T * s + CR_TILE))
                w = max(p.width, width_after(name)) if s == 1 else p.width
            e.activation(wr[slot][:, 0:w], raw[slot][:, 0:w], ACT.Copy).then_inc(S("w_rounded"), 1)

        def blocks(name):
            p = ph[name]
            for n in range(p.nb):
                if not (name == order[-1] and n == p.nb - 1):
                    round_block(name, n // 2, n % 2)
                yield n

        def square(m, j, wait):
            if wait:
                e.wait_ge(*wait)
            if m or not isinstance(j, int) or j:
                e.wait_ge(S("acc_done"), j + KD * m)
            if not isinstance(j, int):
                e.nop(nofuse=True)
            hj = h[:, bass.ds(j, 1), :].rearrange("p a t -> p (a t)")
            e.activation(sq[:], hj, ACT.Square).then_inc(S("sq_ready"), 1)

        def head(m, j, wait=None):
            if wait:
                e.wait_ge(*wait)
                e.nop(nofuse=True)
            hj = h[:, bass.ds(j, 1), :].rearrange("p a t -> p (a t)")
            xj = xr[:, bass.ds(j, 1), :].rearrange("p a t -> p (a t)")
            g0 = POFF["gains"] + m * KD
            e.activation(xj, hj, ACT.Copy, scale=prm[:, bass.ds(j + g0, 1)]).then_inc(S("xr_ready"), 1)

        def root(m):
            e.wait_ge(S("ss_ready"), m + 1)
            e.activation(two(R[:]), psn, ACT.Sqrt, scale=1.0 / D, bias=eps6[:, 0:1]).then_inc(S("root_ready"), 1)

        def up_phase(n, c):
            p = ph[("up", n, c)]
            u0 = n * TOTAL_U + (CHUNKS[0] if c else 0)
            with e.Fori(0, p.nb // 2) as i:
                for s in range(2):
                    round_block(("up", n, c), i, s)
                    e.wait_ge(S("tile_evacuated"), i * 4 + (p.t0 + 2 * s + 1 + CR_EVAC))
                    e.activation(sg[:], tg[:], ACT.Silu).then_inc(S("silu_ready"), 1)
                    e.wait_ge(S("hidden_made"), i * 2 + (u0 + s + 1))
                    e.nop(nofuse=True)
                    e.activation(hr[:, bass.ds(i * 2 + s, 1), :].rearrange("p a t -> p (a t)"), hd[:], ACT.Copy
                                 ).then_inc(S("hr_ready"), 1)

        def down_phase(n, c, m_next):
            p = ph[("down", n, c)]
            with e.Fori(0, p.nb // 2) as i:
                for s in range(2):
                    round_block(("down", n, c), i, s)
                    if c == 1:
                        w = (S("tile_evacuated"), i * 2 + (p.t0 + s + 1 + CR_EVAC))
                        head(m_next, i * 2 + s, w)
                        square(m_next, i * 2 + s, None)

        def store_bias_row(hh):
            e.wait_ge(S("grep_copied"), hh + 1)
            e.dma_start(scratch[hh].rearrange("(p y) -> p y", p=P), grep[:]).then_inc(S("grep_stored"), 16)

        def ffn(n, m):
            for c in range(2):
                up_phase(n, c)
                if n == 0:
                    store_bias_row(2 * c)
                down_phase(n, c, m + 1 if c else None)
                if n == 0:
                    store_bias_row(2 * c + 1)
            root(m + 1)

        for j in range(KD):
            e.dma_start(h[:, j, :], A["xT"][:, j, :]).then_inc(S(f"h_loaded{j}"), 16)
        e.wait_ge(S("prm_loaded"), 16)
        for j in range(KD):
            head(0, j, (S(f"h_loaded{j}"), 16))
            square(0, j, None)
            if j == KD // 2:
                round_block(order[0], 0, 0, first=True)
        e.dma_start(brel[:], A["brel"]).then_inc(S("bias_loaded"), 16)
        e.dma_start(bone[:], A["bone"]).then_inc(S("bias_loaded"), 16)
        e.dma_start(cst[:], A["cst"]).then_inc(S("cst_loaded"), 16)
        e.dma_start(pages[:], A["pages"]).then_inc(S("pages_loaded"), 16)
        e.wait_ge(S("ones_ready"), 3)
        root(0)
        ffn(0, 0)

        e.dma_start(wgraw[:], A["wg"]).then_inc(S("wg_loaded"), 16)
        e.dma_start(us[:, :, :, 0:HIST], A["hist"]).then_inc(S("hist_loaded"), 16)
        e.wait_ge(S("wg_loaded"), 16)
        e.activation(wgr[:], wgraw[:], ACT.Copy).then_inc(S("wgr_ready"), 1)
        for n in blocks("glu"):
            e.wait_ge(S("tile_evacuated"), evac_at("glu", 2 * n + 1))
            e.activation(sg[:], tu[:], ACT.Sigmoid).then_inc(S("glu_sig"), 1)
        e.wait_ge(S("u_ready"), 2 * TM)
        e.dma_start(A["conv_p"], up[:, :, SEQ:SEQ + HIST]).then_inc(S("conv_stored"), 16)
        e.wait_ge(S("hist_loaded"), 16)
        for j in range(TM):
            e.dma_start(A["conv_s"][:, j], us[:, j, :, TB:TB + HIST]).then_inc(S("conv_stored"), 16)
        def copy_turned(n, full, part):
            e.wait_ge(S("turned"), n + 1)
            e.activation(full, ps[:, 4, :].rearrange("p (i d) -> p i d", d=P), ACT.Copy
                         ).then_inc(S("turned_copied"), 1)
            e.activation(part, ps[0:SMP, 5, 0:P], ACT.Copy).then_inc(S("turned_copied"), 1)

        def copy_kv(n):
            dst = kn[:, :, n, :] if n < 4 else vn[:, :, n - 4, 0:P]
            copy_turned(n, dst[:, 0:TM, :], dst[0:SMP, TM, :])

        for n in blocks("kv"):
            if n == 0:
                e.preload_act_table_set("natural_log_exp_and_others")
                e.wait_ge(S("row_z"), 1)
                e.activation(rowB[:], rowt[:], ACT.Abs).then_inc(S("row_act"), 1)
                e.wait_ge(S("row_act"), 1)
                e.activation(rowB[:], rowB[:], ACT.Exp, scale=-1.0).then_inc(S("row_act"), 1)
                e.wait_ge(S("row_act"), 2)
                e.activation(rowB[:], rowB[:], ACT.Ln, bias=1.0).then_inc(S("row_act"), 1)
            if n == 1:
                e.wait_ge(S("row_m"), 1)
                e.dma_start(A["mrow"], rowt[:]).then_inc(S("m_stored"), 16)
                e.activation(rowem[:], rowt[:], ACT.Exp, scale=-1.0).then_inc(S("rows_exp"), 1)
                e.wait_ge(S("row_m"), 2)
                e.activation(rowwi[:, SEQ:T], rowwi[:, SEQ:T], ACT.Exp).then_inc(S("rows_exp"), 1)
                e.wait_ge(S("row_m"), 4)
                e.activation(rowws[:], rowws[:], ACT.Exp).then_inc(S("rows_exp"), 1)
            if n:
                copy_kv(2 * n - 2)
                copy_kv(2 * n - 1)
        copy_kv(6)
        copy_kv(7)
        e.wait_ge(S("cols_turned"), 1)
        for q in range(2):
            o = q * ST * HEADS
            e.activation(gcol[:, o:o + 16], ps[:, 4, o:o + 16], ACT.Copy).then_inc(S("cols_copied"), 1)
            e.activation(gcol[0:SMP, o + 16:o + 20], ps[0:SMP, 4, o + 16:o + 20], ACT.Copy
                         ).then_inc(S("cols_copied"), 1)
        e.wait_ge(S("smp_ready"), 1)
        for q in range(2):
            e.activation(smp[:, 2 * q:2 * q + 2], ps[:, 4 + q, 0:6 * SMP].rearrange("p (h q t) -> p h q t", h=2, q=3),
                         ACT.Copy).then_inc(S("smp_copied"), 1)
        for n in blocks("qo"):
            if n >= 2:
                for o in (2 * (n - 2), 2 * (n - 2) + 1):
                    e.wait_ge(S("tile_evacuated"), evac_at("qo", 4 + o))
                    e.activation(oT[:, o, :], tu[:], ACT.Sigmoid).then_inc(S("o_ready"), 1)
        e.preload_act_table_set("natural_log_exp_and_others")

        def copy_spread(hh):
            e.wait_ge(S("bcast_ready"), hh + 1)
            e.activation(Mb[:, hh, :], ps[:, 2 * (hh % 2), :], ACT.Copy).then_inc(S("bcast_copied"), 1)
            e.activation(emb[:, hh, :], ps[:, 2 * (hh % 2) + 1, :], ACT.Copy).then_inc(S("bcast_copied"), 1)

        def decay(k):
            i = k % ST
            w = SEQ - i * P if i < TM else SMP
            r = P if i < TM else SMP
            e.wait_ge(S("gap_ready"), k + 1)
            e.activation(Ds[0:r, k % 2, 0:w], Xs[0:r, k % 2, 0:w], ACT.Exp, scale=-1.0
                         ).then_inc(S("decay_ready"), 1)

        copy_spread(0)
        copy_spread(1)
        e.wait_ge(S("conv_stored"), 16 * (1 + TM))
        for j in range(TM):
            e.wait_ge(S("ln_centered"), j + 1)
            if j >= 2:
                e.wait_ge(S("ln_var"), j - 1)
            e.activation((hd, sq)[j % 2][:], cv[:, j, :], ACT.Square).then_inc(S("ln_sq"), 1)
            if j % 2:
                decay(j // 2)
        e.wait_ge(S("ln_var"), TM)
        e.activation(two(acc[:]), ps[:, 6:8, 0:HALF], ACT.Ln, scale=1.0 / DA, bias=eps5[:, 0:1]
                     ).then_inc(S("ln_root"), 1)
        e.wait_ge(S("ln_root"), 1)
        e.activation(acc[:], acc[:], ACT.Exp, scale=-0.5).then_inc(S("ln_root"), 1)
        copy_spread(2)
        copy_spread(3)
        for j in range(TM):
            e.wait_ge(S("ln_scaled"), j + 1)
            e.activation(cv[:, j, :], cv[:, j, :], ACT.Silu, scale=W("ln_g", j), bias=W("ln_b", j)
                         ).then_inc(S("conv_out"), 1)
            e.wait_ge(S("conv_out"), j + 1)
            e.activation(xr[:, j, :], cv[:, j, :], ACT.Copy).then_inc(S("mixr_ready"), 1)
        def load_state(hh):
            e.dma_start(C0[hh % 2][:], A["C0"][hh]).then_inc(S(f"C0_loaded{hh % 2}"), 16)

        def store_state(hh):
            e.wait_ge(S("head_done"), hh + 1)
            e.dma_start(A["Cp"][hh], Cp[:]).then_inc(S("C_stored"), 16)
            e.dma_start(A["Cs"][hh], Cn[:]).then_inc(S("C_stored"), 16)
            if hh + 2 < HEADS:
                load_state(hh + 2)

        load_state(0)
        load_state(1)
        for hh in range(HEADS):
            for i in range(2, ST):
                decay(ST * hh + i)
            if hh:
                store_state(hh - 1)
                e.wait_ge(S("state_ready"), hh)
            for i in range(TM):
                o = (ST + i) * HEADS + hh
                e.activation(kw[:, i, :], kn[:, i, hh, :], ACT.Copy, scale=gcol[:, o:o + 1]
                             ).then_inc(S("kw_ready"), 1)
            if hh + 1 < HEADS:
                decay(ST * (hh + 1))
                decay(ST * (hh + 1) + 1)
            e.wait_ge(S("b_out"), hh + 1)
            e.activation(xr[:, TM + hh, :], sq[:], ACT.Copy).then_inc(S("mixr_ready"), 1)
        store_state(HEADS - 1)

        def out_phase(name, m):
            for n in blocks(name):
                for j in (2 * n, 2 * n + 1):
                    square(m, j, (S("tile_evacuated"), evac_at(name, j)))

        def heads_after(m):
            for j in range(KD):
                head(m, j)

        out_phase(("out", 0), 2)
        heads_after(2)
        root(2)
        e.wait_ge(S("C_stored"), 32 * HEADS)
        e.wait_ge(S("m_stored"), 16)
        ffn(1, 2)

        def ple(l):
            m = 4 * l + 4
            e.dma_start(praw[:], A["pT"][l]).then_inc(S("p_loaded"), 16)
            name = ("ple", l)
            for n in blocks(name):
                if n == 0:
                    e.wait_ge(S("p_loaded"), 16 * (l + 1))
                    e.activation(pr[:], praw[:], ACT.Copy).then_inc(S("pr_ready"), 1)
                e.wait_ge(S("tile_evacuated"), evac_at(name, 2 * n))
                e.activation(sg[:], tg[:], ACT.Sigmoid).then_inc(S("ple_sig"), 1)
                square(m, n, (S("ple_added"), KD * l + n + 1))
            if l == 0:
                heads_after(m)
            root(m)

        ple(0)
        ffn(2, 4)

        for hh in range(HEADS):
            e.dma_start(strip[:, hh, :],
                        scratch[hh, P - 1:P - 1 + P * (GL - 1)].rearrange("(p x) -> p x", x=GL - 1)[:, 0:SEQ]
                        ).then_inc(S("strip_loaded"), 16)
            for b in range(2):
                for c in range(2):
                    r = b * 64 + hh * 16 + c * 8
                    o = PAST - 1
                    e.dma_start(sstrip[r:r + TB, :],
                                scratch[hh, o:o + TB * (GL - 1)].rearrange("(t x) -> t x", x=GL - 1)[:, 0:PAST + TB]
                                ).then_inc(S("strip_loaded"), 16)
        e.preload_act_table_set("natural_log_exp_and_others")
        e.wait_ge(S("lam_sums"), 1)
        e.activation(nlam[:, 0:2], nlam[:, 2:4], ACT.Exp).then_inc(S("lam_exp"), 1)
        def copy_v(kind, t):
            dst = ov[kind][:, :, t * P:(t + 1) * P]
            copy_turned(8 + 4 * kind + t, dst[:, 0:TM, :], dst[0:SMP, TM, :])

        for kind in range(2):
            for n in blocks(f"qk{kind}"):
                if kind and n < 2:
                    copy_v(0, 2 * n)
                    copy_v(0, 2 * n + 1)
                if n == 3:
                    e.wait_ge(S("tile_evacuated"), evac_at(f"qk{kind}", 7))
                    e.dma_start(A[("dk", "sk")[kind]], ok[kind][:]).then_inc(S("kv_stored"), 16)
            for n in blocks(f"v{kind}"):
                for t in (2 * n, 2 * n + 1):
                    e.wait_ge(S("tile_evacuated"), evac_at(f"v{kind}", t))
                    e.dma_start(A[("dv", "sv")[kind]][:, t], vtmp[t][:]).then_inc(S(f"v_stored{t}"), 16)
                    if kind and t:
                        copy_v(1, t - 1)
        copy_v(1, 3)
        for t in range(4):
            e.wait_ge(S(f"v_stored{t}"), 32)

        def soft(u):
            w = width(u)
            buf, k = rows[u % 4], u - N
            e.wait_ge(S("rows_turned"), u - 3)
            e.wait_ge(S("scores"), score_count(u + 1))
            e.activation(buf[:, 0:w], ps[:, score_bank(u, 0), 0:w], ACT.Abs).then_inc(S("soft_step"), 1)
            e.wait_ge(S("soft_step"), 3 * k + 1)
            e.activation(buf[:, 0:w], buf[:, 0:w], ACT.Exp, scale=-1.0).then_inc(S("soft_step"), 1)
            e.wait_ge(S("soft_step"), 3 * k + 2)
            e.activation(buf[:, 0:w], buf[:, 0:w], ACT.Ln, bias=1.0).then_inc(S("soft_step"), 1)

        for tick in range(NM + 5):
            if tick < N:
                w = width(tick)
                for c in range(1 if MAPS[tick][3] == SAMPLES else 2):
                    e.wait_ge(S("maxed"), softmaxes(tick) + c + 1)
                    buf = (rows, rows2)[c][tick % 4]
                    e.activation(buf[:, 0:w], buf[:, 0:w], ACT.Exp, bias=st(tick, c),
                                 accum_out=st(tick, 2 + c)).then_inc(S("exped"), 1)
            elif tick < NM:
                soft(tick)
            u = tick - 1
            if N <= u < NM:
                e.wait_ge(S("summed"), u - N + 1)
                buf = rows[u % 4]
                e.activation(buf[:, 0:width(u)], buf[:, 0:width(u)], ACT.Exp, bias=st(u, 4)
                             ).then_inc(S("weights_done"), 1)
            if 3 <= tick < N + 3:
                u = tick - 3
                copy_rowsT(e, u)
            if 5 <= tick:
                u = tick - 5
                kind, hh, c, i = MAPS[u]
                job = kind * PAIRS + hh
                if i == SAMPLES:
                    e.wait_ge(S("values_done"), u + 1)
                    n = 128 if kind else 64
                    if job:
                        e.wait_ge(S("sample_turned"), job)
                    e.activation(srow[0:n, 0:DA], ps[0:n, out_bank(u), :], ACT.Copy).then_inc(S("sample_rows"), 1)
                if i == TM - 1 and c == kind:
                    e.wait_ge(S("values_done"), u + 1)
                    e.activation(oq[kind][:, hh, 0:SEQ], ps[:, out_bank(u), :], ACT.Copy
                                 ).then_inc(S("attn_copied"), 1)

        for hh in range(HEADS):
            if hh == 0:
                e.wait_ge(S("sample_copied"), 2 * PAIRS)
                e.wait_ge(S("attn_copied"), 2 * HEADS)
                e.wait_ge(S("rows_turned"), NM)
            if hh >= 2:
                e.wait_ge(S("oc_ss"), hh - 1)
            e.activation((sg, hd)[hh % 2][:], oq[0][:, hh, :], ACT.Square).then_inc(S("oc_sq"), 1)
            e.wait_ge(S("oc_ss"), hh + 1)
            if hh >= 2:
                e.wait_ge(S("oc_scaled"), hh - 1)
            buf = (tg, tu)[hh % 2]
            e.activation(two(buf[:]), psn, ACT.Ln, scale=1.0 / P, bias=eps6[:, 0:1]).then_inc(S("oc_root"), 1)
            e.wait_ge(S("oc_root"), 2 * hh + 1)
            e.activation(buf[:], buf[:], ACT.Exp, scale=-0.5).then_inc(S("oc_root"), 1)
        for j in range(KD):
            if j < HEADS:
                e.wait_ge(S("oc_scaled"), j + 1)
            e.activation(xr[:, j, :], oq[j // TM][:, j % TM, :], ACT.Copy).then_inc(S("mixr_ready"), 1)

        out_phase(("out", 1), 6)
        heads_after(6)
        root(6)
        e.wait_ge(S("kv_stored"), 32)
        ffn(3, 6)
        ple(1)
        for sem, n in (("conv_stored", 16 * (1 + TM)), ("m_stored", 16), ("C_stored", 32 * HEADS),
                       ("kv_stored", 32), ("grep_stored", 16 * HEADS)):
            e.wait_ge(S(sem), n)
        for j in range(KD):
            e.wait_ge(S("y_ready"), j + 1)
            e.dma_start(A["yT"][:, j], h[:, j, :]).then_inc(S("y_stored"), 16)
        e.wait_ge(S("y_stored"), 16 * KD)

    @block.vector
    def _(e):
        e.nop().then_inc(S("tile_evacuated"), CR_EVAC)
        e.memset(eps6[:], 1e-6).then_inc(S("ones_ready"), 1)
        e.memset(eps5[:], 1e-5).then_inc(S("ones_ready"), 1)
        e.memset(ones[:], 1.0).then_inc(S("ones_ready"), 1)
        stepped = [0]

        def step(ins):
            stepped[0] += 1
            ins.then_inc(S("dve_step"), 1)

        def settle():
            e.wait_ge(S("dve_step"), stepped[0])

        def rest(m, j):
            e.wait_ge(S("xr_ready"), j + (KD * m + 1))
            hj = h[:, bass.ds(j, 1), :].rearrange("p a t -> p (a t)")
            xj = xr[:, bass.ds(j, 1), :].rearrange("p a t -> p (a t)")
            lj = xl[:, bass.ds(j, 1), :].rearrange("p a t -> p (a t)")
            e.scalar_tensor_tensor(lj, hj, prm[:, bass.ds(j + (POFF["gains"] + m * KD), 1)], xj.bitcast(F32),
                                   ALU.mult, ALU.subtract).then_inc(S("x_ready"), 1)

        def add_square(m, j, first):
            e.wait_ge(S("sq_ready"), j + (KD * m + 1))
            if first:
                e.tensor_copy(acc[:], sq[:]).then_inc(S("acc_done"), 1)
            else:
                e.wait_ge(S("acc_done"), j + KD * m)
                e.tensor_tensor(acc[:], acc[:], sq[:], ALU.add).then_inc(S("acc_done"), 1)

        def zero_acc(m):
            if m:
                e.wait_ge(S("ss_ready"), m)
            e.memset(acc[:], 0.0).then_inc(S("acc_zero"), 1)
            e.wait_ge(S("acc_zero"), zeroed[0] + 1)
            zeroed[0] += 1

        zeroed = [0]

        def factor(m):
            e.wait_ge(S("root_ready"), m + 1)
            e.reciprocal(R[:], R[:]).then_inc(S("R_ready"), 1)
            e.wait_ge(S("R_ready"), m + 1)

        def normed(out, u, wait, scale=None):
            e.wait_ge(S("tile_done"), wait)
            if scale is None:
                ins = e.tensor_tensor(two(out), unit(u), two(R[:]), ALU.mult)
            else:
                ins = e.scalar_tensor_tensor(two(out), unit(u), scale, two(R[:]), ALU.mult, ALU.mult)
            ins.then_inc(S("tile_evacuated"), 1)

        def up_phase(n, c):
            p = ph[("up", n, c)]
            u0 = n * TOTAL_U + (CHUNKS[0] if c else 0)
            with e.Fori(0, p.nb // 2) as i:
                for s in range(2):
                    t = p.t0 + 2 * s
                    normed(tg[:], 0, i * 4 + (t + 1 + CR_TILE))
                    normed(tu[:], 1, i * 4 + (t + 2 + CR_TILE))
                    e.wait_ge(S("silu_ready"), i * 2 + (u0 + s + 1))
                    e.wait_ge(S("tile_evacuated"), i * 4 + (t + 2 + CR_EVAC))
                    e.tensor_tensor(hd[:], tu[:], sg[:], ALU.mult).then_inc(S("hidden_made"), 1)
                    e.wait_ge(S("hr_ready"), i * 2 + (u0 + s + 1))
                    r = hr[:, bass.ds(i * 2 + s, 1), :].rearrange("p a t -> p (a t)")
                    q = hl[:, bass.ds(i * 2 + s, 1), :].rearrange("p a t -> p (a t)")
                    e.tensor_tensor(q, hd[:], r.bitcast(F32), ALU.subtract).then_inc(S("hidden_ready"), 1)

        def down_phase(n, c, m_next):
            p = ph[("down", n, c)]
            with e.Fori(0, p.nb // 2) as i:
                for s in range(2):
                    j = i * 2 + s
                    e.wait_ge(S("tile_done"), i * 2 + (p.t0 + s + 1 + CR_TILE))
                    hj = h[:, bass.ds(j, 1), :].rearrange("p o (a t) -> p (o a) t", a=2)
                    e.scalar_tensor_tensor(hj, unit(s), 0.5, hj, ALU.mult, ALU.add
                                           ).then_inc(S("tile_evacuated"), 1)
                    if c == 1:
                        e.wait_ge(S("tile_evacuated"), i * 2 + (p.t0 + s + 1 + CR_EVAC))
                        rest(m_next, j)
                        e.wait_ge(S("sq_ready"), i * 2 + (KD * m_next + s + 1))
                        e.wait_ge(S("acc_done"), i * 2 + (KD * m_next + s))
                        e.tensor_tensor(acc[:], acc[:], sq[:], ALU.add).then_inc(S("acc_done"), 1)

        def copy_bias_row(hh):
            e.wait_ge(S("grep_made"), hh + 1)
            if hh:
                e.wait_ge(S("grep_stored"), 16 * hh)
            e.tensor_copy(grep[:].rearrange("p (a y) -> p a y", a=2), ps[:, 6:8, 0:GL // 2]
                          ).then_inc(S("grep_copied"), 1)

        def ffn(n, m):
            for c in range(2):
                up_phase(n, c)
                if n == 0:
                    copy_bias_row(2 * c)
                if c:
                    zero_acc(m + 1)
                down_phase(n, c, m + 1 if c else None)
                if n == 0:
                    copy_bias_row(2 * c + 1)
            factor(m + 1)

        e.wait_ge(S("prm_loaded"), 16)
        for j in range(KD):
            e.wait_ge(S(f"h_loaded{j}"), 16)
            rest(0, j)
            add_square(0, j, j == 0)
        factor(0)
        ffn(0, 0)

        e.wait_ge(S("grep_stored"), 16 * HEADS)
        e.wait_ge(S("cst_loaded"), 16)
        step(e.memset(up[:, :, 0:HIST], 0.0))
        e.memset(vn[:, :, :, P:P + 1], 1.0).then_inc(S("vn_ones"), 1)
        e.wait_ge(S("wgr_ready"), 1)
        e.tensor_tensor(wgl[:], wgraw[:], wgr[:].bitcast(F32), ALU.subtract).then_inc(S("wg_split"), 2)
        conv_steps = [0]
        accp, accs = ps[:, 6, 0:SEQ], ps[:, 7, 0:SMP].rearrange("p (b t) -> p b t", b=NB)

        def tap(j, k, outp, outs, sem=None, wait=None):
            w = prm[:, bass.ds(k + (POFF["conv_w"] + j * TAPS), 1)]
            if wait is not None:
                e.wait_ge(S("conv_step"), wait - 1)
            inp = up[:, j, bass.ds(k, SEQ)]
            ins_ = us[:, j, :, bass.ds(k, TB)]
            if wait is None:
                a = e.tensor_scalar(outp, inp, w, W("conv_b", j), ALU.mult, ALU.add)
                a.then_inc(S("conv_step"), 1)
                b = e.tensor_scalar(outs, ins_, w, W("conv_b", j), ALU.mult, ALU.add)
            else:
                a = e.scalar_tensor_tensor(outp, inp, w, accp, ALU.mult, ALU.add)
                a.then_inc(S("conv_step"), 1)
                e.wait_ge(S("conv_step"), wait)
                b = e.scalar_tensor_tensor(outs, ins_, w, accs, ALU.mult, ALU.add)
            b.then_inc(S(sem or "conv_step"), 1)

        def conv_chunk(slot):
            j, q = slot // 4, slot % 4
            k0, k1 = q * 8, min(q * 8 + 8, TAPS - 1)
            base = conv_steps[0]
            if q == 0:
                if j:
                    e.wait_ge(S("conv_done"), j)
                tap(j, 0, accp, accs)
                base += 2
                k0 = 1
            n = (k1 - k0) // 2
            with e.Fori(0, n) as i:
                for q_ in range(2):
                    tap(j, i * 2 + (k0 + q_), accp, accs, wait=i * 4 + (base + 2 * q_))
            base += 4 * n
            if (k1 - k0) % 2:
                tap(j, k1 - 1, accp, accs, wait=base)
                base += 2
            if q == 3:
                tap(j, TAPS - 1, cv[:, j, 0:SEQ], cv[:, j, SEQ:T].rearrange("p (b t) -> p b t", b=NB),
                    sem="conv_done", wait=base)
                base += 1
            conv_steps[0] = base

        for j in range(TM):
            normed(tg[:], 0, done_at("glu", 2 * j))
            normed(tu[:], 1, done_at("glu", 2 * j + 1))
            e.wait_ge(S("glu_sig"), j + 1)
            e.wait_ge(S("tile_evacuated"), evac_at("glu", 2 * j))
            e.tensor_tensor(up[:, j, HIST:], tg[:, 0:SEQ], sg[:, 0:SEQ], ALU.mult).then_inc(S("u_ready"), 1)
            e.tensor_tensor(us[:, j, :, HIST:], tg[:, SEQ:T].rearrange("p (b t) -> p b t", b=NB),
                            sg[:, SEQ:T].rearrange("p (b t) -> p b t", b=NB), ALU.mult
                            ).then_inc(S("u_ready"), 1)
            e.wait_ge(S("u_ready"), 2 * j + 2)
            if j == 0:
                e.wait_ge(S("hist_loaded"), 16)
            if j < TM - 1:
                conv_chunk(j)

        e.wait_ge(S("gates_done"), 1)
        step(e.tensor_tensor(two(rowa[:]), ps[0:4, 4:6, 0:HALF], two(R[0:4, :]), ALU.mult))
        step(e.tensor_tensor(two(rowt[:]), ps[32:36, 4:6, 0:HALF], two(R[32:36, :]), ALU.mult))
        settle()
        step(e.tensor_scalar(rowa[:], rowa[:], W("gate_b", 0, rows=4), None, ALU.add))
        e.tensor_scalar(rowt[:], rowt[:], W("gate_b", 1, rows=4), None, ALU.add).then_inc(S("row_z"), 1)
        seg = lambda row: row[:, SEQ:T].rearrange("p (b t) -> p b t", t=TB)
        step(e.memset(rowwi[:], 1.0))
        step(e.memset(rowws[:], 0.0))
        settle()
        step(e.memset(seg(rowwi)[:, :, 0:1], 0.0))
        step(e.memset(seg(rowws)[:, :, 0:1], NEG))
        e.wait_ge(S("row_act"), 3)
        e.wait_ge(S("row_z"), 1)
        step(e.scalar_tensor_tensor(rowt[:], rowt[:], 0.0, rowB[:], ALU.min, ALU.subtract))
        settle()
        step(e.tensor_tensor_scan(rowB[:], rowwi[:], rowt[:], 0.0, ALU.mult, ALU.add))
        settle()
        step(e.tensor_tensor(rowa[:], rowa[:], rowB[:], ALU.subtract))
        settle()
        step(e.tensor_copy(rowt[:], rowa[:]))
        settle()
        m0 = W("m0", 0, NB, rows=4).unsqueeze(2)
        step(e.tensor_tensor(seg(rowt)[:, :, 0:1], seg(rowa)[:, :, 0:1], m0, ALU.max))
        settle()
        step(e.tensor_tensor_scan(rowM[:], rowws[:], rowt[:], 0.0, ALU.add, ALU.max))
        settle()
        e.tensor_tensor(rowt[:], rowB[:], rowM[:], ALU.add).then_inc(S("row_m"), 1)
        e.tensor_tensor(seg(rowwi), m0.broadcast_to([4, NB, TB]), seg(rowM), ALU.subtract).then_inc(S("row_m"), 1)
        e.tensor_scalar(rowws[:, 0:SEQ], rowa[:, 0:SEQ], rowM[:, SEQ - 1:SEQ], None, ALU.subtract
                        ).then_inc(S("row_m"), 1)
        e.tensor_tensor(seg(rowws), seg(rowa), seg(rowM)[:, :, TB - 1:TB].broadcast_to([4, NB, TB]),
                        ALU.subtract).then_inc(S("row_m"), 1)

        for t in range(8):
            if t < 4:
                normed(kT[:, t, :], t % 2, done_at("kv", t), P ** -0.5)
            else:
                normed(vtmp[t - 4][:], t % 2, done_at("kv", t))
            if t >= 2:
                conv_chunk(t + 1)
        for t in range(8):
            if t < 4:
                normed(qT[:, t, :], t % 2, done_at("qo", t))
            else:
                if t > 4:
                    e.wait_ge(S("o_ready"), t - 4)
                normed(tu[:], t % 2, done_at("qo", t))
            if t < 7:
                conv_chunk(9 + t)
        def gap(k):
            hh, i = divmod(k, ST)
            if k >= 2:
                e.wait_ge(S("decay_ready"), k - 1)
            r, w = (P, SEQ - i * P) if i < TM else (SMP, SMP)
            src = Mb[:, hh, i * P:SEQ] if i < TM else smp[0:SMP, hh, 0, :]
            a = gcol[0:r, i * HEADS + hh:i * HEADS + hh + 1]
            e.tensor_scalar(Xs[0:r, k % 2, 0:w], src, a, 0.0, ALU.subtract, ALU.max
                            ).then_inc(S("gap_ready"), 1)

        def weigh(k):
            if k + 1 < ST * HEADS:
                gap(k + 1)
            i = k % ST
            r, w = (P, SEQ - i * P) if i < TM else (SMP, SMP)
            e.wait_ge(S("decay_ready"), k + 1)
            e.wait_ge(S("s_ready"), k + 1)
            if k >= 2:
                e.wait_ge(S("pv_done"), k - 1)
            pm = Pm[k % 2]
            step(e.tensor_tensor(pm[0:r, 0:w], ps[0:r, 4 + k % 2, 0:w], Ds[0:r, k % 2, 0:w], ALU.mult))
            settle()
            m = C("cm") if i < TM else C("blk_ml", rows=SMP)
            n = P if i < TM else SMP
            e.tensor_tensor(pm[0:r, 0:n], pm[0:r, 0:n], m, ALU.mult).then_inc(S("p_ready"), 1)

        e.wait_ge(S("ln_sum"), 1)
        for j in range(TM):
            e.scalar_tensor_tensor(two(cv[:, j, :]), psn, -1.0 / DA, two(cv[:, j, :]), ALU.mult, ALU.add
                                   ).then_inc(S("ln_centered"), 1)
        e.wait_ge(S("bcast_copied"), 2)
        e.wait_ge(S("m_stored"), 16)
        gap(0)
        weigh(0)
        weigh(1)
        e.wait_ge(S("ln_root"), 2)
        for j in range(TM):
            e.tensor_tensor(cv[:, j, :], cv[:, j, :], acc[:], ALU.mult).then_inc(S("ln_scaled"), 1)
        for j in range(TM):
            e.wait_ge(S("mixr_ready"), j + 1)
            e.tensor_tensor(xl[:, j, :], cv[:, j, :], xr[:, j, :].bitcast(F32), ALU.subtract
                            ).then_inc(S("mix_ready"), 1)

        e.wait_ge(S("mix_ready"), TM)
        e.wait_ge(S("cols_copied"), 4)
        e.wait_ge(S("bcast_copied"), 2 * HEADS)

        def prepare(hh):
            if hh:
                e.wait_ge(S("inter_ready"), hh)
                e.wait_ge(S("state_ready"), hh)
            e.wait_ge(S(f"C0_loaded{hh % 2}"), 16 * (hh // 2 + 1))
            e.tensor_tensor(qn[:, 0:SMP].rearrange("p (b t) -> p b t", b=NB),
                            qT[:, hh, SEQ:T].rearrange("p (b t) -> p b t", b=NB),
                            C0[hh % 2][:, :, P:P + 1].broadcast_to([P, NB, TB]), ALU.mult
                            ).then_inc(S("qn_ready"), 1)
            o = (ST + TM) * HEADS + hh
            step(e.tensor_scalar(wsm[:], C("blk_col", rows=SMP), gcol[0:SMP, o:o + 1], None, ALU.mult))
            settle()
            e.tensor_tensor(kwm[:], kn[0:SMP, TM, hh, :].unsqueeze(1).broadcast_to([SMP, NB, P]),
                            wsm[:].unsqueeze(2).broadcast_to([SMP, NB, P]), ALU.mult).then_inc(S("kwm_ready"), 1)

        def output(hh):
            num, den, rws = BANKS[hh % 2]
            e.wait_ge(S("pv_done"), ST * (hh + 1))
            e.wait_ge(S("inter_ready"), hh + 1)
            if hh:
                e.wait_ge(S("mixr_ready"), TM + hh)
            part = lambda n: ps[:, rws, n * SMP:(n + 1) * SMP]
            wi = smp[:, hh, 2, :]
            step(e.tensor_scalar(tu[:, 0:SEQ], ps[:, den, 0:SEQ], -1.0, None, ALU.mult))
            step(e.tensor_tensor(tu[:, SEQ:T], part(3), wi, ALU.mult))
            step(e.tensor_tensor(acc[:, SEQ:T], part(2), wi, ALU.mult))
            settle()
            step(e.tensor_tensor(tu[:, 0:SEQ], tu[:, 0:SEQ], ps[:, den, 0:SEQ], ALU.max))
            step(e.tensor_tensor(tu[:, SEQ:T], tu[:, SEQ:T], part(1), ALU.add))
            step(e.tensor_tensor(acc[:, SEQ:T], acc[:, SEQ:T], part(0), ALU.add))
            settle()
            step(e.scalar_tensor_tensor(tu[:, SEQ:T], tu[:, SEQ:T], -1.0, tu[:, SEQ:T], ALU.mult, ALU.max))
            step(e.tensor_tensor(tu[:, 0:SEQ], tu[:, 0:SEQ], emb[:, hh, :], ALU.max))
            settle()
            step(e.tensor_tensor(tu[:, SEQ:T], tu[:, SEQ:T], smp[:, hh, 1, :], ALU.max))
            settle()
            step(e.reciprocal(tu[:], tu[:]))
            settle()
            e.tensor_tensor(acc[:, 0:SEQ], ps[:, num, 0:SEQ], tu[:, 0:SEQ], ALU.mult).then_inc(S("h_read"), 1)
            step(e.tensor_tensor(acc[:, SEQ:T], acc[:, SEQ:T], tu[:, SEQ:T], ALU.mult))
            settle()
            e.wait_ge(S("h_read"), hh + 1)
            e.wait_ge(S("o_ready"), HEADS)
            e.tensor_tensor(sq[:], acc[:], oT[:, hh, :], ALU.mult).then_inc(S("b_out"), 1)

        def new_states(hh):
            banks = BANKS[hh % 2]
            e.wait_ge(S("mixr_ready"), TM + hh + 1)
            e.wait_ge(S("b_out"), hh + 1)
            e.tensor_tensor(xl[:, TM + hh, :], sq[:], xr[:, TM + hh, :].bitcast(F32), ALU.subtract
                            ).then_inc(S("mix_ready"), 1)
            e.wait_ge(S("state_ready"), hh + 1)
            if hh:
                e.wait_ge(S("C_stored"), 32 * hh)
            step(e.tensor_copy(Cp[:], ps[:, banks[2], 2 * (P + 1):3 * (P + 1)]))
            for b in range(NB):
                o = (b % 3) * (P + 1)
                d = smp[:, hh, 2, b * TB + TB - 1:b * TB + TB]
                ins = e.scalar_tensor_tensor(Cn[:, b, :], C0[hh % 2][:, b, :], d, ps[:, banks[b // 3], o:o + P + 1],
                                             ALU.mult, ALU.add)
                if b < NB - 1:
                    step(ins)
            settle()
            ins.then_inc(S("head_done"), 1)

        for hh in range(HEADS):
            for i in range(2, ST):
                weigh(ST * hh + i)
            if hh:
                new_states(hh - 1)
            prepare(hh)
            if hh + 1 < HEADS:
                weigh(ST * (hh + 1))
                weigh(ST * (hh + 1) + 1)
            output(hh)
        new_states(HEADS - 1)

        def rests(m):
            for j in range(KD):
                rest(m, j)

        def out_and_norm(name, m):
            zero_acc(m)
            for j in range(KD):
                e.wait_ge(S("tile_done"), done_at(name, j))
                e.tensor_tensor(two(h[:, j, :]), unit(j % 2), two(h[:, j, :]), ALU.add
                                ).then_inc(S("tile_evacuated"), 1)
                add_square(m, j, False)
            rests(m)
            factor(m)

        out_and_norm(("out", 0), 2)
        ffn(1, 2)

        def ple(l):
            name, m = ("ple", l), 4 * l + 4
            e.wait_ge(S("pr_ready"), l + 1)
            e.tensor_tensor(pl[:], praw[:], pr[:].bitcast(F32), ALU.subtract).then_inc(S("p_split"), 1)
            zero_acc(m)
            for j in range(KD):
                normed(tg[:], 0, done_at(name, 2 * j))
                e.wait_ge(S("ple_sig"), KD * l + j + 1)
                e.wait_ge(S("tile_done"), done_at(name, 2 * j + 1))
                e.tensor_tensor(two(tu[:]), unit(1), two(sg[:]), ALU.mult).then_inc(S("tile_evacuated"), 1)
                e.wait_ge(S("tile_evacuated"), evac_at(name, 2 * j + 1))
                e.tensor_tensor(h[:, j, :], h[:, j, :], tu[:], ALU.add).then_inc(S("ple_added"), 1)
                add_square(m, j, False)
            if l == 0:
                rests(m)
            factor(m)

        ple(0)
        ffn(2, 4)

        lp = W("lam", 0, 256)
        lpv = lp.rearrange("p (a b d) -> p a b d", a=2, b=2)
        step(e.tensor_tensor(lamt[:].rearrange("p (a d) -> p a d", a=2), lpv[:, :, 0, :], lpv[:, :, 1, :], ALU.mult))
        settle()
        e.tensor_reduce(nlam[:, 2:4], lamt[:].rearrange("p (a d) -> p a d", a=2), AX.X, ALU.add
                        ).then_inc(S("lam_sums"), 1)
        e.wait_ge(S("lam_exp"), 1)
        step(e.tensor_tensor(nlam[:, 4:5], nlam[:, 1:2], nlam[:, 0:1], ALU.subtract))
        settle()
        step(e.tensor_scalar(nlam[:, 4:5], nlam[:, 4:5], -LAM_INIT, None, ALU.add))
        settle()
        step(e.scalar_tensor_tensor(nlam[:, 5:6], C("half1"), nlam[:, 4:5], C("half0"), ALU.mult, ALU.add))
        e.wait_ge(S("strip_loaded"), 16 * HEADS * 5)
        for hh in range(HEADS):
            step(e.tensor_tensor(strip[:, hh, SEQ - P:SEQ], strip[:, hh, SEQ - P:SEQ], C("neg_incl"), ALU.add))
        for pair in range(PAIRS):
            step(e.tensor_tensor(sbias[:, pair * SMP:(pair + 1) * SMP].rearrange("p (b t) -> p b t", b=NB),
                                 C("dneg", pair * SMP, (pair + 1) * SMP).rearrange("p (b t) -> p b t", b=NB),
                                 sstrip[:, PAST:PAST + TB].unsqueeze(1).broadcast_to([P, NB, TB]), ALU.add))
        step(e.memset(qbd[:], 0.0))
        for kind in range(2):
            for t in range(8):
                dst = (oq, ok)[t // 4][kind][:, t % 4, :]
                normed(dst, t % 2, done_at(f"qk{kind}", t), 0.125 if t < 4 else None)
            for t in range(4):
                if kind:
                    e.wait_ge(S("turned"), 12)
                    e.wait_ge(S(f"v_stored{t}"), 16)
                normed(vtmp[t][:], t % 2, done_at(f"v{kind}", t))
        for t in range(4):
            e.wait_ge(S(f"v_stored{t}"), 32)
        e.wait_ge(S("turned"), 16)

        def sample_queries(job):
            kind, pair = job // PAIRS, job % PAIRS
            if job:
                e.wait_ge(S("scores"), score_count(SAMPLE_AT[job - 1] + 1))
            for b in range(2):
                for c in range(2):
                    src = oq[kind][64 * c:64 * c + 64, :, SEQ + (2 * pair + b) * TB:SEQ + (2 * pair + b + 1) * TB]
                    dst = qbd[64 * c:64 * c + 64, b, :].rearrange("p (h x) -> p h x", x=80)[:, :, c * 8:c * 8 + 8]
                    ins = e.tensor_copy(dst, src)
                    if (b, c) != (1, 1):
                        step(ins)
            settle()
            ins.then_inc(S("qbd_ready"), 1)

        def bias_and_max(u, q, buf, w, parts):
            for n, (a, b, bias) in enumerate(parts):
                ins = e.tensor_tensor(buf[:, a:b], ps[:, score_bank(u, q), a:b], bias, ALU.add)
                if n < len(parts) - 1:
                    step(ins)
                    settle()
            ins.then_inc(S("biased"), 1)
            e.wait_ge(S("biased"), softmaxes(u) + q + 1)
            e.tensor_reduce(st(u, q), buf[:, 0:w], AX.X, ALU.max, negate=True).then_inc(S("maxed"), 1)

        def probs(u):
            w = width(u)
            b0, b1 = rows[u % 4], rows2[u % 4]
            e.wait_ge(S("exped"), softmaxes(u + 1))
            if MAPS[u][3] == SAMPLES:
                step(e.reciprocal(st(u, 2), st(u, 2)))
                settle()
                e.tensor_scalar(b0[:, 0:w], b0[:, 0:w], st(u, 2), nlam[:, 5:6], ALU.mult, ALU.mult
                                ).then_inc(S("probs_done"), 1)
                return
            o = 5 * (u % 4) + 2
            step(e.reciprocal(tiny[:, o:o + 2], tiny[:, o:o + 2]))
            settle()
            step(e.tensor_scalar(b0[:, 0:w], b0[:, 0:w], st(u, 2), None, ALU.mult))
            step(e.tensor_scalar(st(u, 3), st(u, 3), nlam[:, 4:5], None, ALU.mult))
            settle()
            e.scalar_tensor_tensor(b0[:, 0:w], b1[:, 0:w], st(u, 3), b0[:, 0:w], ALU.mult, ALU.add
                                   ).then_inc(S("probs_done"), 1)

        def sums(u):
            k, w = u - N, width(u)
            buf, scan, src = rows[u % 4], rows2[u % 4], ps[:, score_bank(u, 0), 0:w]
            if k < 4:
                e.wait_ge(S("probs_done"), u - 3)
                step(e.memset(scan[:, 0:1], 0.0))
            e.wait_ge(S("soft_step"), 3 * k + 3)
            step(e.scalar_tensor_tensor(buf[:, 0:w], src, 0.0, buf[:, 0:w], ALU.max, ALU.add))
            settle()
            step(e.tensor_tensor_scan(scan[:, 1:w + 1], ones[:, 0:1].broadcast_to([P, w]), buf[:, 0:w], 0.0,
                                      ALU.mult, ALU.add))
            if k >= 4:
                e.wait_ge(S("weights_done"), k - 3)
            settle()
            step(e.tensor_scalar(st(u, 4), scan[:, w:w + 1], -1.0, None, ALU.mult))
            e.tensor_tensor(buf[:, 0:w], src, scan[:, 0:w], ALU.add).then_inc(S("summed"), 1)

        def copy_sample_out(u):
            kind, pair = MAPS[u][0:2]
            t0, bank = SEQ + 2 * pair * TB, out_bank(u)
            e.wait_ge(S("sample_turned"), SAMPLE_AT.index(u) + 1)
            if kind == 0:
                ins = e.tensor_copy(oq[0][:, :, t0:t0 + 2 * TB],
                                    ps[:, bank, 0:64].rearrange("p (h x) -> p h x", h=HEADS))
            else:
                for c in range(2):
                    r = slice(64 * c, 64 * c + 64)
                    ins = e.tensor_copy(oq[1][r, :, t0:t0 + 2 * TB].rearrange("p h (b t) -> p h b t", b=2),
                                        ps[r, bank, 0:128].rearrange("p (h b c t) -> p c h b t", b=2, h=HEADS, c=2)[:, c])
                    if c == 0:
                        step(ins)
                settle()
            ins.then_inc(S("sample_copied"), 1)

        hg = tiny[:, 32:32 + HEADS]
        step(e.tensor_scalar(hg, W("head_g", 0, HEADS), 1.0 - LAM_INIT, None, ALU.mult))
        sample_queries(0)
        for tick in range(NM + 3):
            if tick < N:
                kind, hh, c, i = MAPS[tick]
                w = width(tick)
                if tick >= 4:
                    e.wait_ge(S("rows_turned"), tick - 3)
                for c in range(1 if i == SAMPLES else 2):
                    e.wait_ge(S("scores"), score_count(tick) + c + 1)
                    bias_and_max(tick, c, (rows, rows2)[c][tick % 4], w,
                                 [(0, w, strip[:, hh, SEQ - w:SEQ])] if i < SAMPLES else
                                 [(0, PAST, sstrip[:, 0:PAST]), (PAST, KEYS, sbias[:, hh * SMP:(hh + 1) * SMP])])
            elif tick < NM:
                sums(tick)
            if 1 <= tick <= N:
                probs(tick - 1)
            if N + 3 <= tick:
                copy_rowsT(e, tick - 3)
            if tick < NM and MAPS[tick][3] == SAMPLES:
                job = SAMPLE_AT.index(tick)
                if job + 1 < 2 * PAIRS:
                    sample_queries(job + 1)
            if tick - 7 in SAMPLE_AT:
                copy_sample_out(tick - 7)

        for hh in range(HEADS):
            buf = (tg, tu)[hh % 2]
            e.wait_ge(S("oc_root"), 2 * hh + 2)
            if hh == 0:
                e.wait_ge(S("sample_copied"), 2 * PAIRS)
            e.scalar_tensor_tensor(oq[0][:, hh, :], oq[0][:, hh, :], hg[:, hh:hh + 1], buf[:], ALU.mult, ALU.mult
                                   ).then_inc(S("oc_scaled"), 1)
        for j in range(KD):
            e.wait_ge(S("mixr_ready"), KD + j + 1)
            e.tensor_tensor(xl[:, j, :], oq[j // TM][:, j % TM, :], xr[:, j, :].bitcast(F32), ALU.subtract
                            ).then_inc(S("mix_ready"), 1)
        out_and_norm(("out", 1), 6)
        ffn(3, 6)
        ple(1)
        for j in range(KD):
            g = W("gains", 8 * KD + j)
            e.scalar_tensor_tensor(h[:, j, :], h[:, j, :], g, R[:], ALU.mult, ALU.mult).then_inc(S("y_ready"), 1)

    return ctx


def constants():
    c = np.zeros((P, CW), np.float32)

    def put(name, a):
        c[:a.shape[0], COFF[name]:COFF[name] + a.shape[1]] = a

    p, j = np.arange(P)[:, None], np.arange(P)[None, :]
    put("ident", np.eye(P, dtype=np.float32))
    put("cm", (j >= p).astype(np.float32))
    put("neg_incl", np.where(j > p, NEG, 0.0).astype(np.float32))
    put("sb_neg", np.where(j >= p, NEG, 0.0).astype(np.float32))
    s, t = np.arange(SMP)[:, None], np.arange(SMP)[None, :]
    put("blk_ml", ((s // TB == t // TB) & (t >= s)).astype(np.float32))
    put("blk_col", (s // TB == np.arange(NB)[None, :]).astype(np.float32))
    row = np.arange(P)
    b2, tq = row // 64, row % TB
    for pair in range(PAIRS):
        own = t // TB == (2 * pair + b2)[:, None]
        incl = own & (t % TB <= tq[:, None])
        strict = own & (t % TB < tq[:, None])
        o = pair * SMP
        c[:, COFF["dneg"] + o:COFF["dneg"] + o + SMP] = np.where(incl, 0.0, NEG)
        c[:, COFF["sneg"] + o:COFF["sneg"] + o + SMP] = np.where(strict, 0.0, NEG)
    head, half = (row % 64) // 16, (row % 16) // 8
    put("fold", ((b2 * 32 + head * 8 + tq)[:, None] == np.arange(64)[None, :]).astype(np.float32))
    put("half0", (half == 0).astype(np.float32)[:, None])
    put("half1", (half == 1).astype(np.float32)[:, None])
    sel = np.zeros((4, 4, P), np.float32)
    for q in range(4):
        sel[q, q] = 1
    put("sel", sel.reshape(4, -1))
    n = np.maximum(SEQ - 1 - np.arange(GL), 0)
    exact = 16
    nf = np.maximum(n, 1).astype(np.float32)
    large = exact + (np.log(nf / exact) / np.float32(np.log(128 / exact)) * (32 - exact)).astype(np.int32)
    bucket = np.where(n < exact, n, np.minimum(large, 31))
    onehot = (bucket[None, :] == np.arange(32)[:, None]).astype(np.float32)
    return c, onehot


def tiles_of(w, nk):
    nj = w.shape[1] // P
    return np.ascontiguousarray(w.reshape(nk, P, nj, P).transpose(2, 1, 0, 3))


def feature_major(a):
    return np.ascontiguousarray(a.reshape(a.shape[0], -1, P).transpose(2, 1, 0))


def by_partition(v):
    return np.ascontiguousarray(v.reshape(-1, P).T)


def kernel(**inputs):
    import concourse.bacc as bacc
    from concourse.bass_utils import run_bass_kernel_spmd

    I = {k: np.asarray(v) for k, v in inputs.items()}
    c, onehot = constants()
    a = {"cst": c, "bone": onehot}
    both = lambda x, y: np.concatenate([x.reshape(SEQ, -1), y.reshape(SMP, -1)], 0)
    a["xT"] = feature_major(both(I["x_prompt"], I["x_sample"]))
    a["pT"] = np.stack([feature_major(both(I["p_prompt"][l], I["p_sample"][l])) for l in range(2)])

    up, d0, d1, ple = [], [], [], []
    for l in range(2):
        for wi, wo in ((I["ffn1_wi"][l], I["ffn1_wo"][l]), (I["ffn2_wi"][l], I["ffn2_wo"][l])):
            t = tiles_of(wi, KD)
            nt = t.shape[0] // 2
            up.append(np.stack([t[:nt], t[nt:]], 2).reshape(nt, P, -1))
            t = tiles_of(wo, DFF // P)
            d0.append(t[:, :, :CHUNKS[0]].reshape(KD, P, -1))
            d1.append(t[:, :, CHUNKS[0]:].reshape(KD, P, -1))
        g, q = tiles_of(I["ple_wg"][l], KD), tiles_of(I["ple_wp"][l], KP)
        ple.append(np.concatenate([g.reshape(KD, P, -1), q.reshape(KD, P, -1)], 2))
    pairs = lambda t: t.reshape(-1, 2, P, KD * P).transpose(0, 2, 1, 3).reshape(-1, P, 2 * KD * P)
    ev = I["ev_w_in"][0]
    t = tiles_of(np.ascontiguousarray(ev[:, :24 * P]), KD)
    val, gate, q, k, v, o = (t[4 * n:4 * n + 4] for n in range(6))
    ev_t = np.concatenate([np.stack([val, gate], 1).reshape(8, *t.shape[1:]), k, v, q, o])
    od_t = tiles_of(I["od_w_in"][0], KD)
    a["up"], a["down0"], a["down1"], a["ple"] = (np.concatenate(x) for x in (up, d0, d1, ple))
    cq, ck, cvv, sq_, sk, sv = (od_t[4 * n:4 * n + 4] for n in range(6))
    a["mixin"] = np.concatenate([pairs(ev_t), pairs(np.concatenate([cq, ck, cvv, sq_, sk, sv]))])
    a["mixout"] = np.concatenate([pairs(tiles_of(I["ev_w_out"][0], KD)), pairs(tiles_of(I["od_w_out"][0], KD))])
    wg = np.zeros((P, KD, 36), np.float32)
    gates = ev[:, 24 * P:].reshape(KD, P, 8).transpose(1, 0, 2)
    wg[:, :, 0:4], wg[:, :, 32:36] = gates[:, :, 0:4], gates[:, :, 4:8]
    a["wg"] = wg

    prm = np.zeros((P, PW), np.float32)

    def put(name, x, at=0):
        prm[:x.shape[0], POFF[name] + at:POFF[name] + at + x.shape[1]] = x

    for l in range(2):
        for n, name in enumerate(("ffn_norm1", "mix_norm", "ffn_norm2", "ple_norm")):
            put("gains", by_partition(I[name][l]), (4 * l + n) * KD)
    put("gains", by_partition(I["final_norm"]), 8 * KD)
    put("conv_w", I["ev_conv_w"][0].reshape(TAPS, TM, P).transpose(2, 1, 0).reshape(P, -1))
    put("conv_b", by_partition(I["ev_conv_b"][0]))
    put("ln_g", by_partition(I["ev_ln_g"][0]))
    put("ln_b", by_partition(I["ev_ln_b"][0]))
    put("gate_b", I["ev_gate_b"][0].reshape(2, 4).T)
    put("head_g", by_partition(I["od_head_g"][0]))
    put("lam", np.broadcast_to(I["od_lambda"][0].reshape(1, 256), (P, 256)))
    put("m0", I["state_mlstm_m"][0].T)
    a["prm"] = prm
    a["hist"] = np.ascontiguousarray(I["state_conv"][0].reshape(NB, HIST, TM, P).transpose(3, 2, 0, 1))
    st = np.concatenate([I["state_mlstm_C"][0], I["state_mlstm_n"][0][..., None]], -1)
    a["C0"] = np.ascontiguousarray(st.transpose(1, 2, 0, 3))
    a["brel"] = np.ascontiguousarray(np.repeat(I["rel_bias"], P, axis=1))
    a["pages"] = I["page_table"].reshape(1, -1)
    for kind, name in enumerate(("diff", "sb")):
        kk = I[f"cache_{name}_k"][0]
        a[f"kc{kind}"] = np.ascontiguousarray(kk.reshape(-1, PAGE, HEADS, P).transpose(0, 3, 2, 1))
        a[f"vc{kind}"] = np.ascontiguousarray(I[f"cache_{name}_v"][0].reshape(-1, PAGE, DA))

    nc = bacc.Bacc("TRN2", target_bir_lowering=False, num_devices=1, dynamic_dma_scratch_size=1024)
    A = {n: nc.dram_tensor(f"in_{n}", x.shape, mybir.dt.from_np(x.dtype), kind="ExternalInput").ap()
         for n, x in a.items()}
    outs = dict(yT=(P, KD, T), conv_p=(P, TM, HIST), conv_s=(P, TM, NB, HIST), Cp=(HEADS, P, P + 1),
                Cs=(HEADS, P, NB, P + 1), mrow=(HEADS, T), dk=(P, TM, T), dv=(P, TM, T), sk=(P, TM, T), sv=(P, TM, T))
    for n, shape in outs.items():
        A[n] = nc.dram_tensor(f"out_{n}", shape, F32, kind="ExternalOutput").ap()
    A["scratch"] = nc.dram_tensor("scratch", (HEADS, P * GL), F32, kind="Internal").ap()
    build(nc, A).close()
    r = run_bass_kernel_spmd(nc, [{f"in_{n}": x for n, x in a.items()}], core_ids=[0]).results[0]
    O = {n: r[f"out_{n}"] for n in outs}

    def token_major(x):
        t = x.transpose(2, 1, 0).reshape(T, -1)
        return t[:SEQ], t[SEQ:]

    yp, ys = token_major(O["yT"])
    res = [yp.reshape(1, SEQ, D), ys.reshape(NB, TB, D)]
    res.append(O["conv_p"].transpose(2, 1, 0).reshape(1, 1, HIST, DA))
    res.append(O["conv_s"].transpose(2, 3, 1, 0).reshape(1, NB, HIST, DA))
    cs = O["Cs"].transpose(2, 0, 1, 3)
    res += [O["Cp"][None, None, :, :, :P], cs[None, ..., :P], O["Cp"][None, None, :, :, P], cs[None, ..., P]]
    res += [O["mrow"][:, SEQ - 1].reshape(1, 1, HEADS), O["mrow"][:, SEQ + TB - 1::TB].T[None]]
    for n, sh in (("dk", (HEADS, P)), ("dv", (HEADS, P)), ("sk", (8, 64)), ("sv", (8, 64))):
        kp, ks = token_major(O[n])
        res += [kp.reshape(1, 1, SEQ, *sh), ks.reshape(1, NB, TB, *sh)]
    return tuple(np.ascontiguousarray(x) for x in res)
```
